# Optimizing a Trainium2 kernel written in Bass

```python
import math
import jax
import jax.numpy as jnp
from jax import lax
import numpy as np

D_MODEL = 1024
BATCH = 1
SEQ = 256
DEPTH = 2

D_MIX = D_MODEL
ATT_HEADS = 8
ATT_HEAD_DIM = 64
ATT_WIDTH = ATT_HEADS * ATT_HEAD_DIM
MOBA_BLOCK = 256
MOBA_TOPK = 3
Q_CHUNK = 128
ROPE_THETA = 500000.0
ROPE_DIM = ATT_HEAD_DIM // 4
ML_HEADS = 4
ML_WIDTH = D_MIX - ATT_WIDTH
ML_V_DIM = ML_WIDTH // ML_HEADS
ML_QK_DIM = ML_V_DIM // 2
ML_QK_WIDTH = ML_HEADS * ML_QK_DIM
ML_CHUNK = 128
CONV_WIDTH = 4
N_IN = 3 * ATT_WIDTH + 2 * ML_QK_WIDTH + 2 * ML_WIDTH + 2 * ML_HEADS
D_FF = 2816
N_EXPERTS = 8
TOP_K = 2
D_EXPERT = 3584
N_DENSE = (DEPTH + 1) // 2
N_MOE = DEPTH // 2
LN_EPS = 1e-5
RMS_EPS = 1e-6

kernel_name = "hymba_moba_mlstm_deepnorm_moe"

def layer_norm(x, g, b):
    xf = x.astype(jnp.float32)
    mu = xf.mean(-1, keepdims=True)
    var = jnp.square(xf - mu).mean(-1, keepdims=True)
    return ((xf - mu) * lax.rsqrt(var + LN_EPS) * g.astype(jnp.float32) + b.astype(jnp.float32)).astype(x.dtype)

def head_rmsnorm(h, g, out_dtype):
    B, S, H, Dh = h.shape
    hf = h.astype(jnp.float32)
    hf = hf * lax.rsqrt(jnp.mean(jnp.square(hf), -1, keepdims=True) + RMS_EPS)
    return (hf.reshape(B, S, H * Dh) * g.astype(jnp.float32)).astype(out_dtype)

def partial_rope(x, positions):
    half = ROPE_DIM // 2
    inv_freq = ROPE_THETA ** (-jnp.arange(half, dtype=jnp.float32) / half)
    ang = positions.astype(jnp.float32)[:, None, :, None] * inv_freq
    cos, sin = jnp.cos(ang), jnp.sin(ang)
    xf = x.astype(jnp.float32)
    x1, x2, rest = xf[..., :half], xf[..., half:ROPE_DIM], xf[..., ROPE_DIM:]
    out = jnp.concatenate([x1 * cos - x2 * sin, x2 * cos + x1 * sin, rest], -1)
    return out.astype(x.dtype)

def moba_attention(q, k, v):
    B, H, S, Dh = q.shape
    nb = -(-S // MOBA_BLOCK)
    pad = nb * MOBA_BLOCK - S
    kp = jnp.pad(k, ((0, 0), (0, 0), (0, pad), (0, 0)))
    vp = jnp.pad(v, ((0, 0), (0, 0), (0, pad), (0, 0)))
    kb = kp.reshape(B, H, nb, MOBA_BLOCK, Dh)
    vb = vp.reshape(B, H, nb, MOBA_BLOCK, Dh)
    k_mean = kb.astype(jnp.float32).mean(3)
    topk = min(MOBA_TOPK, nb)
    scale = Dh ** -0.5
    bi = jnp.arange(B)[:, None, None, None]
    hi = jnp.arange(H)[None, :, None, None]
    block_ids = jnp.arange(nb)

    def one_chunk(c):
        q0 = c * Q_CHUNK
        blk = q0 // MOBA_BLOCK
        qf = lax.dynamic_slice_in_dim(q, q0, Q_CHUNK, axis=2).astype(jnp.float32)
        gate = jnp.einsum('bhqd,bhnd->bhqn', qf, k_mean)
        gate = jnp.where(block_ids < blk, gate, -jnp.inf)
        _, sel = lax.top_k(gate, topk)
        sel_ok = sel < blk
        k_sel = kb[bi, hi, sel].astype(jnp.float32)
        v_sel = vb[bi, hi, sel].astype(jnp.float32)
        s_sel = jnp.einsum('bhqd,bhqknd->bhqkn', qf, k_sel) * scale
        s_sel = jnp.where(sel_ok[..., None], s_sel, -jnp.inf)
        k_own = lax.dynamic_index_in_dim(kb, blk, axis=2, keepdims=False).astype(jnp.float32)
        v_own = lax.dynamic_index_in_dim(vb, blk, axis=2, keepdims=False).astype(jnp.float32)
        s_own = jnp.einsum('bhqd,bhnd->bhqn', qf, k_own) * scale
        q_pos = q0 + jnp.arange(Q_CHUNK)
        k_pos = blk * MOBA_BLOCK + jnp.arange(MOBA_BLOCK)
        s_own = jnp.where(k_pos[None, :] <= q_pos[:, None], s_own, -jnp.inf)
        n_sel = topk * MOBA_BLOCK
        p = jax.nn.softmax(jnp.concatenate([s_sel.reshape(B, H, Q_CHUNK, n_sel), s_own], -1), axis=-1)
        p_sel = p[..., :n_sel].reshape(B, H, Q_CHUNK, topk, MOBA_BLOCK)
        p_own = p[..., n_sel:]
        out = (jnp.einsum('bhqkn,bhqknd->bhqd', p_sel, v_sel)
               + jnp.einsum('bhqn,bhnd->bhqd', p_own, v_own))
        return out.astype(q.dtype)

    outs = lax.map(one_chunk, jnp.arange(S // Q_CHUNK))
    return jnp.moveaxis(outs, 0, 2).reshape(B, H, S, Dh)

def causal_depthwise_conv(x, w, b):
    S = x.shape[1]
    xp = jnp.pad(x, ((0, 0), (CONV_WIDTH - 1, 0), (0, 0)))
    y = b + w[0] * xp[:, 0:S]
    for j in range(1, CONV_WIDTH):
        y = y + w[j] * xp[:, j:j + S]
    return y

def mlstm_chunkwise(q, k, v, i_pre, f_pre):
    B, H, S, Dk = q.shape
    Dv = v.shape[-1]
    L = ML_CHUNK
    nc = S // L
    qf = q.astype(jnp.float32) * (Dk ** -0.5)
    kf = k.astype(jnp.float32)
    vf = v.astype(jnp.float32)
    ig = i_pre.astype(jnp.float32)
    logf = jax.nn.log_sigmoid(f_pre.astype(jnp.float32))

    def chunks(t):
        return jnp.moveaxis(t.reshape(B, H, nc, L, *t.shape[3:]), 2, 0)

    causal = jnp.tril(jnp.ones((L, L), dtype=bool))

    def step(carry, xs):
        C, n, m = carry
        qc, kc, vc, ic, fc = xs
        b = jnp.cumsum(fc, axis=-1)
        d_log = jnp.where(causal, b[..., :, None] - b[..., None, :] + ic[..., None, :], -jnp.inf)
        inter = b + m[..., None]
        m_t = jnp.maximum(inter, d_log.max(-1))
        w_intra = jnp.exp(d_log - m_t[..., None])
        w_inter = jnp.exp(inter - m_t)
        s = jnp.einsum('bhtd,bhsd->bhts', qc, kc) * w_intra
        num = (jnp.einsum('bhts,bhsv->bhtv', s, vc)
               + w_inter[..., None] * jnp.einsum('bhvd,bhtd->bhtv', C, qc))
        den = s.sum(-1) + w_inter * jnp.einsum('bhd,bhtd->bht', n, qc)
        h = num / jnp.maximum(jnp.abs(den), jnp.exp(-m_t))[..., None]
        b_last = b[..., -1]
        decay = b_last[..., None] - b + ic
        m_new = jnp.maximum(b_last + m, decay.max(-1))
        w_state = jnp.exp(decay - m_new[..., None])
        carry_scale = jnp.exp(b_last + m - m_new)
        C_new = carry_scale[..., None, None] * C + jnp.einsum('bhs,bhsv,bhsd->bhvd', w_state, vc, kc)
        n_new = carry_scale[..., None] * n + jnp.einsum('bhs,bhsd->bhd', w_state, kc)
        return (C_new, n_new, m_new), h

    init = (jnp.zeros((B, H, Dv, Dk), jnp.float32), jnp.zeros((B, H, Dk), jnp.float32),
            jnp.zeros((B, H), jnp.float32))
    _, hs = lax.scan(step, init, (chunks(qf), chunks(kf), chunks(vf), chunks(ig), chunks(logf)))
    return jnp.moveaxis(hs, 0, 2).reshape(B, H, S, Dv)

def hybrid_mixer(x, positions, w_in, gate_bias, conv_w, conv_b, norm_attn, norm_mlstm, w_out):
    B, S, _ = x.shape
    proj = x @ w_in
    cuts = [int(c) for c in np.cumsum([ATT_WIDTH, ATT_WIDTH, ATT_WIDTH, 2 * ML_QK_WIDTH, ML_WIDTH, ML_WIDTH])]
    aq, ak, av, mqk, mv, mo, mg = jnp.split(proj, cuts, axis=-1)

    def att_heads(t):
        return t.reshape(B, S, ATT_HEADS, ATT_HEAD_DIM).transpose(0, 2, 1, 3)
    qa = partial_rope(att_heads(aq), positions)
    ka = partial_rope(att_heads(ak), positions)
    att = moba_attention(qa, ka, att_heads(av))
    att_out = head_rmsnorm(att.transpose(0, 2, 1, 3), norm_attn, x.dtype)

    mqk = jax.nn.silu(causal_depthwise_conv(mqk, conv_w, conv_b))
    mq, mk = mqk[..., :ML_QK_WIDTH], mqk[..., ML_QK_WIDTH:]
    def ml_heads(t, d):
        return t.reshape(B, S, ML_HEADS, d).transpose(0, 2, 1, 3)
    gates = (mg + gate_bias).transpose(0, 2, 1)
    h_ml = mlstm_chunkwise(ml_heads(mq, ML_QK_DIM), ml_heads(mk, ML_QK_DIM), ml_heads(mv, ML_V_DIM),
                           gates[:, :ML_HEADS], gates[:, ML_HEADS:])
    ml_out = head_rmsnorm(h_ml.transpose(0, 2, 1, 3), norm_mlstm, x.dtype) * jax.nn.sigmoid(mo)

    return jnp.concatenate([att_out, ml_out], axis=-1) @ w_out

def swiglu(x, w_gate, w_up, w_down):
    return (jax.nn.silu(x @ w_gate) * (x @ w_up)) @ w_down

def moe_swiglu(x, router_w, router_b, w_gate, w_up, w_down):
    logits = (x @ router_w).astype(jnp.float32) + router_b.astype(jnp.float32)
    top_val, top_idx = lax.top_k(logits, TOP_K)
    top_w = jax.nn.softmax(top_val, axis=-1)
    combine = jnp.sum(jax.nn.one_hot(top_idx, N_EXPERTS, dtype=jnp.float32) * top_w[..., None], axis=-2)
    combine = combine.astype(x.dtype)
    y = jnp.zeros_like(x)
    for e in range(N_EXPERTS):
        y = y + combine[..., e:e + 1] * swiglu(x, w_gate[e], w_up[e], w_down[e])
    return y

def setup_inputs(seed: int = 0) -> dict:
    key = jax.random.key(seed)
    ks = jax.random.split(key, 24)
    f32 = jnp.float32
    beta = (8.0 * DEPTH) ** -0.25

    def nrm(k, shape, scale):
        return scale * jax.random.normal(k, shape, f32)

    x = nrm(ks[0], (BATCH, SEQ, D_MODEL), 1.0)
    positions = jnp.broadcast_to(jnp.arange(SEQ, dtype=jnp.int32), (BATCH, SEQ))
    w_in = nrm(ks[1], (DEPTH, D_MODEL, N_IN), D_MODEL ** -0.5)
    i_bias = nrm(ks[2], (DEPTH, ML_HEADS), 0.1)
    f_bias = jnp.linspace(3.0, 6.0, ML_HEADS, dtype=f32) + nrm(ks[3], (DEPTH, ML_HEADS), 0.1)
    gate_bias = jnp.concatenate([i_bias, f_bias], axis=-1)
    conv_w = nrm(ks[4], (DEPTH, CONV_WIDTH, 2 * ML_QK_WIDTH), CONV_WIDTH ** -0.5)
    conv_b = nrm(ks[5], (DEPTH, 2 * ML_QK_WIDTH), 0.02)
    norm_attn = 1.0 + nrm(ks[6], (DEPTH, ATT_WIDTH), 0.02)
    norm_mlstm = 1.0 + nrm(ks[7], (DEPTH, ML_WIDTH), 0.02)
    w_out = nrm(ks[8], (DEPTH, D_MIX, D_MODEL), beta * D_MIX ** -0.5)
    ln1_g = 1.0 + nrm(ks[9], (DEPTH, D_MODEL), 0.02)
    ln1_b = nrm(ks[10], (DEPTH, D_MODEL), 0.02)
    dense_w_gate = nrm(ks[11], (N_DENSE, D_MODEL, D_FF), D_MODEL ** -0.5)
    dense_w_up = nrm(ks[12], (N_DENSE, D_MODEL, D_FF), D_MODEL ** -0.5)
    dense_w_down = nrm(ks[13], (N_DENSE, D_FF, D_MODEL), beta * D_FF ** -0.5)
    router_w = nrm(ks[14], (N_MOE, D_MODEL, N_EXPERTS), D_MODEL ** -0.5)
    router_b = nrm(ks[15], (N_MOE, N_EXPERTS), 0.01)
    moe_w_gate = nrm(ks[16], (N_MOE, N_EXPERTS, D_MODEL, D_EXPERT), D_MODEL ** -0.5)
    moe_w_up = nrm(ks[17], (N_MOE, N_EXPERTS, D_MODEL, D_EXPERT), D_MODEL ** -0.5)
    moe_w_down = nrm(ks[18], (N_MOE, N_EXPERTS, D_EXPERT, D_MODEL), beta * D_EXPERT ** -0.5)
    ln2_g = 1.0 + nrm(ks[19], (DEPTH, D_MODEL), 0.02)
    ln2_b = nrm(ks[20], (DEPTH, D_MODEL), 0.02)
    return {"x": x, "positions": positions, "w_in": w_in, "gate_bias": gate_bias,
            "conv_w": conv_w, "conv_b": conv_b, "norm_attn": norm_attn, "norm_mlstm": norm_mlstm,
            "w_out": w_out, "ln1_g": ln1_g, "ln1_b": ln1_b,
            "dense_w_gate": dense_w_gate, "dense_w_up": dense_w_up, "dense_w_down": dense_w_down,
            "router_w": router_w, "router_b": router_b,
            "moe_w_gate": moe_w_gate, "moe_w_up": moe_w_up, "moe_w_down": moe_w_down,
            "ln2_g": ln2_g, "ln2_b": ln2_b}

def reference(x, positions, w_in, gate_bias, conv_w, conv_b, norm_attn, norm_mlstm, w_out,
              ln1_g, ln1_b, dense_w_gate, dense_w_up, dense_w_down, router_w, router_b,
              moe_w_gate, moe_w_up, moe_w_down, ln2_g, ln2_b):
    alpha = (2.0 * DEPTH) ** 0.25
    for l in range(DEPTH):
        mix = hybrid_mixer(x, positions, w_in[l], gate_bias[l], conv_w[l], conv_b[l],
                           norm_attn[l], norm_mlstm[l], w_out[l])
        x = layer_norm(alpha * x + mix, ln1_g[l], ln1_b[l])
        j = l // 2
        if l % 2 == 0:
            ffn = swiglu(x, dense_w_gate[j], dense_w_up[j], dense_w_down[j])
        else:
            ffn = moe_swiglu(x, router_w[j], router_b[j], moe_w_gate[j], moe_w_up[j], moe_w_down[j])
        x = layer_norm(alpha * x + ffn, ln2_g[l], ln2_b[l])
    return x


_drawn_inputs = setup_inputs


def setup_inputs(seed=0):
    import zlib

    import numpy as np

    out = dict(_drawn_inputs(seed))
    spreads = {}
    factors = {'conv_b': 5.547, 'norm_attn': 13.844, 'norm_mlstm': 20.247, 'router_b': 22.578}
    for name, (base, spread) in spreads.items():
        noise = np.random.default_rng([zlib.crc32(name.encode()), seed]).standard_normal(out[name].shape)
        drawn = base * np.exp(spread * noise) if base else spread * noise
        out[name] = jnp.asarray(drawn.astype(out[name].dtype))
    for name, factor in factors.items():
        out[name] = (out[name] * factor).astype(out[name].dtype)
    return out
```

```python
from contextlib import ExitStack

import concourse.bass as bass
from concourse import mybir

F32 = mybir.dt.float32
F32R = mybir.dt.float32r
BF16 = mybir.dt.bfloat16
I32 = mybir.dt.int32
ALU = mybir.AluOpType
ACT = mybir.ActivationFunctionType
AX_X = mybir.AxisListType.X

P = 128
TWO_PI = 6.283185307179586
PI_SAFE = 3.1415925
NEG = -1.0e30
LN_EPS = 1e-5
RMS_EPS = 1e-6
ROPE_THETA = 500000.0

RAW_UNITS = 3
PIECES = 4
SPLIT_SLOTS = 6
ROUND = RAW_UNITS * PIECES
WIDE = 512


def hybrid_moe_program(nc, x, positions, w_in, gate_bias, conv_w, conv_b, norm_attn, norm_mlstm, w_out,
                       ln1_g, ln1_b, dense_w_gate, dense_w_up, dense_w_down, router_w, router_b,
                       moe_w_gate, moe_w_up, moe_w_down, ln2_g, ln2_b, out):
    _, SEQ, D = x.shape
    DEPTH = w_in.shape[0]
    N_IN = w_in.shape[2]
    D_FF = dense_w_gate.shape[2]
    E, D_EXPERT = moe_w_gate.shape[1], moe_w_gate.shape[3]
    NT = SEQ // P
    KD = D // P
    AH, AD = 8, 64
    AW = AH * AD
    MH, MV, MK = 4, 128, 64
    ALPHA = (2.0 * DEPTH) ** 0.25
    HALF_ROPE = AD // 4 // 2
    MAX_PASSES = E + 3
    assert NT == 2 and DEPTH == 2 and N_IN == 3 * AW + 3 * WIDE + 2 * MH and KD == 8

    MIX_ROUNDS = 3
    DENSE_FULL = D_FF // WIDE
    DENSE_ROUNDS = DENSE_FULL + 1
    MOE_CHUNKS = D_EXPERT // WIDE
    LAYER_ROUNDS = MIX_ROUNDS + DENSE_ROUNDS
    MOE_BASE = LAYER_ROUNDS + MIX_ROUNDS
    assert D_FF - DENSE_FULL * WIDE == WIDE // 2

    xd = x.rearrange("a (t p) d -> p (a t) d", p=P)
    outd = out.rearrange("a (t p) d -> p (a t) d", p=P)

    with ExitStack() as ctx:
        def sb(name, shape, dt=F32, where=ctx):
            return where.enter_context(nc.sbuf_tensor(name, shape, dt))

        def sem(name):
            return ctx.enter_context(nc.semaphore(name))

        raw = sb("raw", [P, RAW_UNITS, 8 * WIDE])
        wh = sb("wh", [P, SPLIT_SLOTS, 2 * WIDE], F32R)
        wl = sb("wl", [P, SPLIT_SLOTS, 2 * WIDE], F32R)
        xs = sb("xs", [P, NT, D])
        xth = sb("xth", [P, KD, SEQ], F32R)
        xtl = sb("xtl", [P, KD, SEQ], F32R)
        lng = sb("lng", [P, D])
        lnb = sb("lnb", [P, D])
        ident = sb("ident", [P, P])
        ones = sb("ones", [P, P])
        tri = sb("tri", [P, P])
        trs = sb("trs", [P, P])
        mask3 = sb("mask3", [P, 3 * P])
        maskt = sb("maskt", [P, P])
        slot_no = sb("slot_no", [P, P])
        zrow = sb("zrow", [P, WIDE], BF16)
        eps = sb("eps", [P, 2])
        rw = sb("rw", [P, KD, E])
        rwh = sb("rwh", [P, KD, E], F32R)
        rwl = sb("rwl", [P, KD, E], F32R)
        rb = sb("rb", [P, E])
        stats = sb("stats", [P, NT, 2, 6])
        moments = sb("moments", [P, NT, 2])
        lnc = sb("lnc", [P, NT, 3])

        mix_mem = ctx.enter_context(ExitStack())
        qk = sb("qk", [P, NT, 2 * AW], F32, mix_mem)
        mix = qk
        qkt = sb("qkt", [P, 8, SEQ], F32, mix_mem)
        posi = sb("posi", [P, NT], I32, mix_mem)
        posf = sb("posf", [P, NT], F32, mix_mem)
        invf = sb("invf", [P, HALF_ROPE], F32, mix_mem)
        ang = sb("ang", [P, 2, NT, HALF_ROPE], F32, mix_mem)
        turn = sb("turn", [P, 2, NT, HALF_ROPE], F32, mix_mem)
        turni = sb("turni", [P, 2, NT, HALF_ROPE], I32, mix_mem)
        sc8 = sb("sc8", [P, 2, NT, HALF_ROPE], F32, mix_mem)
        sincos = sb("sincos", [P, 2, NT, 2 * AH, HALF_ROPE], F32, mix_mem)
        gbias = sb("gbias", [P, 2 * MH], F32, mix_mem)
        cw = sb("cw", [P, 4, 4], F32, mix_mem)
        cb = sb("cb", [P, 4], F32, mix_mem)
        gna = sb("gna", [P, AW], F32, mix_mem)
        gnm = sb("gnm", [P, MH * MV], F32, mix_mem)
        vv = sb("vv", [P, NT, AW], F32, mix_mem)
        mpre = sb("mpre", [P, 4, 3 + SEQ], F32, mix_mem)
        cacc = sb("cacc", [P, 4, SEQ], F32, mix_mem)
        mqkt = sb("mqkt", [P, 4, SEQ], F32, mix_mem)
        ktok = sb("ktok", [P, MH * MK], F32, mix_mem)
        mv = sb("mv", [P, NT, MH, MV + 2], F32, mix_mem)
        mo = sb("mo", [P, NT, MH * MV], F32, mix_mem)
        sm = sb("sm", [P, 2, 3 * P], F32, mix_mem)
        pm = sb("pm", [P, 2, 3 * P], F32, mix_mem)
        ptm = sb("ptm", [P, 2, 3 * P], F32, mix_mem)
        smax = sb("smax", [P, AH, NT], F32, mix_mem)
        snb = sb("snb", [P, AH, NT], F32, mix_mem)
        norms = sb("norms", [P, 5, 24], F32, mix_mem)
        rsum = sb("rsum", [P, NT, AH], F32, mix_mem)
        araw = cacc[:, :, :].rearrange("p c n -> p (c n)").rearrange("p (t h d) -> p t h d", t=NT, h=AH)
        gates = sb("gates", [P, NT, 2 * MH], F32, mix_mem)
        gtmp = sb("gtmp", [P, 4, NT, MH], F32, mix_mem)
        bl = sb("bl", [P, NT, 2 * MH], F32, mix_mem)
        aa = sb("aa", [P, NT, MH], F32, mix_mem)
        diag = sb("diag", [P, NT, MH, P], F32, mix_mem)
        wtmp = sb("wtmp", [P, NT, MH, P], F32, mix_mem)
        st = diag
        wflat = wtmp[:, :, :, :].rearrange("p c h n -> p (c h n)")
        rt = wflat.rearrange("p (i t h j) -> p i t h j", i=4, t=NT, h=2 * AH)
        itmp = wflat[:, 0:MH * (MV + 2)].rearrange("p (h v) -> p h v", h=MH)
        mxs = sb("mxs", [P, 6, MH], F32, mix_mem)
        ein = sb("ein", [P, 4, MH], F32, mix_mem)
        eout = sb("eout", [P, 4, MH], F32, mix_mem)
        vw = sb("vw", [P, MH, MV + 2], F32, mix_mem)
        csb = sb("csb", [P, 2, MV + 2], F32, mix_mem)
        tot = sb("tot", [P, NT, MH, MV + 2], F32, mix_mem)
        mix_mem.close()
        hbuf = sb("hbuf", [P, NT, WIDE])
        hth = sb("hth", [P, 4, SEQ], F32R)
        htl = sb("htl", [P, 4, SEQ], F32R)
        xh = sb("xh", [P, NT, D], F32R)
        xl = sb("xl", [P, NT, D], F32R)
        yh = sb("yh", [P, D], F32R)
        yl = sb("yl", [P, D], F32R)
        pick = sb("pick", [P, NT, P], F32R)
        pickt = sb("pickt", [P, SEQ], F32R)
        lg = sb("lg", [P, NT, E])
        cmp4 = sb("cmp4", [P, 3, NT, E, E])
        rank = sb("rank", [P, NT, E])
        isel = sb("isel", [P, 3, NT, E])
        topv = sb("topv", [P, 6, NT])
        comb = sb("comb", [P, NT, E])
        posc = sb("posc", [P, 3, E])
        blk = sb("blk", [P, 5, E])
        pt11 = sb("pt11", [P, 5, MAX_PASSES, E])
        slotpos = sb("slotpos", [P, NT, MAX_PASSES])
        cbp = sb("cbp", [P, NT, MAX_PASSES])
        tabf = sb("tabf", [P, MAX_PASSES + 1])
        tabi = sb("tabi", [P, MAX_PASSES + 1], I32)
        low8 = sb("low8", [P, E, E])
        pass_no = sb("pass_no", [P, MAX_PASSES])
        expert_no = sb("expert_no", [P, E])

        B = [ctx.enter_context(nc.psum_tensor(f"B{i}", [P, WIDE], F32)) for i in range(8)]

        raw_full = [sem(f"raw_full{i}") for i in range(RAW_UNITS)]
        rounded = sem("rounded")
        split = sem("split")
        piece_used = sem("piece_used")
        x_loaded, const_ready, rope_in = sem("x_loaded"), sem("const_ready"), sem("rope_in")
        const_step = sem("const_step")
        mixp_loaded, ln_loaded, router_loaded = sem("mixp_loaded"), sem("ln_loaded"), sem("router_loaded")
        dve_init = sem("dve_init")
        rope_step, sin_in, sin_done, rope_table = sem("rope_step"), sem("sin_in"), sem("sin_done"), sem("rope_table")
        xt_psum, xt_high, xt_low = sem("xt_psum"), sem("xt_high"), sem("xt_low")
        q_copied, k_copied, v_copied = sem("q_copied"), sem("k_copied"), sem("v_copied")
        mqk_copied, roped, rot_step = sem("mqk_copied"), sem("roped"), sem("rot_step")
        conv_step, conv_done, conv_silu = sem("conv_step"), sem("conv_done"), sem("conv_silu")
        gates_in, absf, exp_f, ln_f, logf_done = sem("gates_in"), sem("absf"), sem("exp_f"), sem("ln_f"), sem("logf_done")
        cum_psum, cum_copied, a_done, ktok_psum, ktok_copied = (
            sem("cum_psum"), sem("cum_copied"), sem("a_done"), sem("ktok_psum"), sem("ktok_copied"))
        qkt_psum, qt_copied, kt_copied = sem("qkt_psum"), sem("qt_copied"), sem("kt_copied")
        score_psum, masked, row_max, score_ready = sem("score_psum"), sem("masked"), sem("row_max"), sem("score_ready")
        probs_done, probs_t_psum, probs_t, att_psum, att_copied = (
            sem("probs_done"), sem("probs_t_psum"), sem("probs_t"), sem("att_psum"), sem("att_copied"))
        diag_a, arow_psum, amask_step, m_step, diag_m, mrow_psum = (
            sem("diag_a"), sem("arow_psum"), sem("amask_step"), sem("m_step"), sem("diag_m"), sem("mrow_psum"))
        exp_small, wlog, wexp, kq_psum, st_done = (
            sem("exp_small"), sem("wlog"), sem("wexp"), sem("kq_psum"), sem("st_done"))
        mv_copied, mo_exp, vw_done, c_psum, c_copied = (
            sem("mv_copied"), sem("mo_exp"), sem("vw_done"), sem("c_psum"), sem("c_copied"))
        num_psum, num0_copied, inter_psum, inter_scaled, tot_done = (
            sem("num_psum"), sem("num0_copied"), sem("inter_psum"), sem("inter_scaled"), sem("tot_done"))
        mo_gate, squares, norm_step, mean_sq, std_done, mix_done = (
            sem("mo_gate"), sem("squares"), sem("norm_step"), sem("mean_sq"), sem("std_done"), sem("mix_done"))
        residual = sem("residual")
        ln_step, ln_var, ln_std, ln_coef, ln_scaled, ln_out = (
            sem("ln_step"), sem("ln_var"), sem("ln_std"), sem("ln_coef"), sem("ln_scaled"), sem("ln_out"))
        silu_done, h_done, ht_psum, ht_high, ht_low, ffn_added = (
            sem("silu_done"), sem("h_done"), sem("ht_psum"), sem("ht_high"), sem("ht_low"), sem("ffn_added"))
        rw_high, rw_low, logits_psum, route_step, picks_ready, pos_psum, table_ready = (
            sem("rw_high"), sem("rw_low"), sem("logits_psum"), sem("route_step"), sem("picks_ready"),
            sem("pos_psum"), sem("table_ready"))
        x_high, x_low = sem("x_high"), sem("x_low")
        pick_done, pick_psum, pick_copied, gathered, gath_high, gath_low = (
            sem("pick_done"), sem("pick_psum"), sem("pick_copied"), sem("gathered"), sem("gath_high"), sem("gath_low"))
        y_high, y_low, scattered, accumulated = (
            sem("y_high"), sem("y_low"), sem("scattered"), sem("accumulated"))
        stored = sem("stored")

        block = ctx.enter_context(nc.Block())

        class Rounds:

            def __init__(self, eng, r):
                fixed = isinstance(r, int)
                self.r = r if fixed else eng.snap(r)
                self.pieces = r * ROUND if fixed else eng.snap(self.r * ROUND)
                self.loads = r * 16 if fixed else eng.snap(self.r * 16)

        def piece_slot(g):
            return g % SPLIT_SLOTS

        def unit_of(g):
            return g // PIECES

        def ffn_stretch(eng, first, chunk, tail, r0, chunks, half):
            first(Rounds(eng, r0))
            with eng.Fori(0, chunks - 1) as c:
                chunk(Rounds(eng, c + r0), WIDE, WIDE)
            if half:
                chunk(Rounds(eng, r0 + chunks - 1), WIDE // 2, WIDE)
                tail(Rounds(eng, r0 + chunks), WIDE // 2)
            else:
                tail(Rounds(eng, r0 + chunks - 1), WIDE)

        @block.sync
        def _(sp):
            def load(R, j, dst, src):
                sp.wait_ge(split, R.pieces + PIECES * j + PIECES)
                sp.dma_start(dst, src).then_inc(raw_full[j % RAW_UNITS], 16)

            def slices(j, width, n=8):
                return raw[:, j % RAW_UNITS, 0:n * width].rearrange("p (k n) -> p k n", k=n)

            def columns(w2d, c0, width):
                return w2d.rearrange("(k p) n -> p k n", p=P)[:, :, c0:c0 + width]

            def load_columns(R, j, w2d, c0, width):
                load(R, j, slices(j, width), columns(w2d, c0, width))

            def load_rows(R, j, w2d, r0, n):
                load(R, j, raw[:, j % RAW_UNITS, 0:n * D].rearrange("p (k n) -> p k n", k=n), w2d(r0, n))

            with sp.Fori(0, DEPTH) as l:
                R = Rounds(sp, l * LAYER_ROUNDS)
                wi = w_in[bass.ds(l, 1), :, :].rearrange("a (k p) n -> p (a k) n", p=P)
                wo = w_out[bass.ds(l, 1), :, :].rearrange("a (k p) n -> p (a k) n", p=P)
                order = [(0, WIDE), (AW, WIDE), (3 * AW, WIDE), (3 * AW + 3 * WIDE, 2 * MH),
                         (2 * AW, WIDE), (3 * AW + WIDE, WIDE), (3 * AW + 2 * WIDE, WIDE)]
                for j, (c0, width) in enumerate(order):
                    load(R, j, slices(j, width), wi[:, :, c0:c0 + width])
                for n in range(2):
                    load(R, 7 + n, slices(7 + n, WIDE), wo[:, :, n * WIDE:(n + 1) * WIDE])
                with sp.If(l < 1):
                    def down_rows(r0, n):
                        return dense_w_down[0, r0:r0 + n * P, :].rearrange("(k p) n -> p k n", p=P)

                    R = Rounds(sp, MIX_ROUNDS)
                    load_columns(R, 0, dense_w_gate[0], 0, WIDE)
                    load_columns(R, 1, dense_w_up[0], 0, WIDE)
                    with sp.Fori(0, DENSE_FULL - 1) as c:
                        R = Rounds(sp, c + MIX_ROUNDS)
                        cols = bass.ds(c * WIDE + WIDE, WIDE)
                        load(R, 2, slices(2, WIDE), dense_w_gate[0, :, cols].rearrange("(k p) n -> p k n", p=P))
                        load(R, 3, slices(3, WIDE), dense_w_up[0, :, cols].rearrange("(k p) n -> p k n", p=P))
                        load(R, 4, raw[:, 4 % RAW_UNITS, 0:4 * D].rearrange("p (k n) -> p k n", k=4),
                             dense_w_down[0, bass.ds(c * WIDE, WIDE), :].rearrange("(k p) n -> p k n", p=P))
                    R = Rounds(sp, MIX_ROUNDS + DENSE_FULL - 1)
                    load_columns(R, 2, dense_w_gate[0], DENSE_FULL * WIDE, WIDE // 2)
                    load_columns(R, 3, dense_w_up[0], DENSE_FULL * WIDE, WIDE // 2)
                    load_rows(R, 4, down_rows, (DENSE_FULL - 1) * WIDE, 4)
                    load_rows(Rounds(sp, MIX_ROUNDS + DENSE_FULL), 2, down_rows, DENSE_FULL * WIDE, 2)

            sp.wait_ge(table_ready, 1)
            passes = sp.value_load(tabi[0:1, MAX_PASSES:MAX_PASSES + 1], min_val=1, max_val=MAX_PASSES)
            with sp.Fori(0, passes) as p:
                e = sp.value_load(tabi[0:1, bass.ds(p, 1)], min_val=0, max_val=E - 1)

                def expert_columns(w, cols):
                    return w[0, bass.ds(e, 1), :, cols].rearrange("a (k p) n -> p (a k) n", p=P)

                def expert_rows(rows):
                    return moe_w_down[0, bass.ds(e, 1), rows, :].rearrange("a (k p) n -> p (a k) n", p=P)

                r0 = sp.snap(p * MOE_CHUNKS + MOE_BASE)
                R = Rounds(sp, r0)
                load(R, 0, slices(0, WIDE), expert_columns(moe_w_gate, slice(0, WIDE)))
                load(R, 1, slices(1, WIDE), expert_columns(moe_w_up, slice(0, WIDE)))
                with sp.Fori(0, MOE_CHUNKS - 1) as c:
                    R = Rounds(sp, c + r0)
                    cols = bass.ds(c * WIDE + WIDE, WIDE)
                    load(R, 2, slices(2, WIDE), expert_columns(moe_w_gate, cols))
                    load(R, 3, slices(3, WIDE), expert_columns(moe_w_up, cols))
                    load(R, 4, raw[:, 4 % RAW_UNITS, 0:4 * D].rearrange("p (k n) -> p k n", k=4),
                         expert_rows(bass.ds(c * WIDE, WIDE)))
                R = Rounds(sp, r0 + (MOE_CHUNKS - 1))
                load(R, 2, raw[:, 2, 0:4 * D].rearrange("p (k n) -> p k n", k=4),
                     expert_rows(slice((MOE_CHUNKS - 1) * WIDE, MOE_CHUNKS * WIDE)))

            for t in range(NT):
                sp.wait_ge(ln_out, 2 * NT * (DEPTH - 1) + NT + t + 1)
                sp.dma_start(outd[:, t, :], xs[:, t, :]).then_inc(stored, 16)
            sp.wait_ge(stored, 16 * NT)

        @block.gpsimd
        def _(pool):
            pool.dma_start(xs[:, :, :], xd).then_inc(x_loaded, 16)
            with nc.allow_non_contiguous_dma(reason="one position per partition"):
                pool.dma_start(posi[:, :], positions.rearrange("a (t p) -> p (a t)", p=P)).then_inc(rope_in, 16)

            pool.memset(zrow[:, :], 0.0)
            pool.memset(eps[:, 0:1], LN_EPS)
            pool.memset(eps[:, 1:2], RMS_EPS)
            pool.memset(ident[:, :], 0.0)
            pool.memset(tri[:, :], 1.0)
            pool.memset(trs[:, :], 1.0)
            pool.memset(mask3[:, :], 0.0)
            pool.memset(maskt[:, :], 0.0)
            pool.memset(ones[:, :], 1.0).then_inc(const_step, 1)
            pool.iota(slot_no[:, :], pattern=[[1, P]], base=0, channel_multiplier=0,
                      allow_small_or_imprecise_dtypes=True)
            pool.wait_ge(const_step, 1)
            pool.affine_select(out=ident[:, :], in_=ident[:, :], compare_op=ALU.not_equal, fill=1.0,
                               base=0, pattern=[[-1, P]], channel_multiplier=1)
            pool.affine_select(out=tri[:, :], in_=tri[:, :], compare_op=ALU.is_ge, fill=0.0,
                               base=0, pattern=[[1, P]], channel_multiplier=-1)
            pool.affine_select(out=trs[:, :], in_=trs[:, :], compare_op=ALU.is_ge, fill=0.0,
                               base=-1, pattern=[[1, P]], channel_multiplier=-1)
            pool.affine_select(out=maskt[:, :], in_=maskt[:, :], compare_op=ALU.is_ge, fill=NEG,
                               base=0, pattern=[[1, P]], channel_multiplier=-1)
            pool.affine_select(out=mask3[:, 0:P], in_=mask3[:, 0:P], compare_op=ALU.is_ge, fill=NEG,
                               base=0, pattern=[[-1, P]], channel_multiplier=1)
            pool.affine_select(out=mask3[:, 2 * P:3 * P], in_=mask3[:, 2 * P:3 * P], compare_op=ALU.is_ge,
                               fill=NEG, base=0, pattern=[[-1, P]], channel_multiplier=1).then_inc(const_ready, 1)
            with nc.allow_non_contiguous_dma(reason="small parameters"):
                pool.dma_start(rw[:, :, :], router_w[0].rearrange("(k p) e -> p k e", p=P)).then_inc(router_loaded, 16)
                pool.dma_start(rb[:, :], router_b.broadcast_to((P, E))).then_inc(router_loaded, 16)

            def load_ln(g, b, done):
                if done is not None:
                    pool.wait_ge(ln_out, done)
                pool.dma_start(lng[:, :], g.broadcast_to((P, D))).then_inc(ln_loaded, 16)
                pool.dma_start(lnb[:, :], b.broadcast_to((P, D))).then_inc(ln_loaded, 16)

            load_ln(ln1_g[0:1, :], ln1_b[0:1, :], None)
            with pool.Fori(0, DEPTH) as l:
                row = bass.ds(l, 1)
                pool.wait_ge(dve_init, 2 + l)
                with nc.allow_non_contiguous_dma(reason="small parameters"):
                    for j in range(4):
                        pool.dma_start(cw[:, :, j], conv_w[row, j, :].rearrange("a (c p) -> p (a c)", p=P))\
                            .then_inc(mixp_loaded, 16)
                    pool.dma_start(cb[:, :], conv_b[row, :].rearrange("a (c p) -> p (a c)", p=P)).then_inc(mixp_loaded, 16)
                    pool.dma_start(gbias[:, :], gate_bias[row, :].broadcast_to((P, 2 * MH))).then_inc(mixp_loaded, 16)
                    pool.dma_start(gna[:, :], norm_attn[row, :].broadcast_to((P, AW))).then_inc(mixp_loaded, 16)
                    pool.dma_start(gnm[:, :], norm_mlstm[row, :].broadcast_to((P, MH * MV))).then_inc(mixp_loaded, 16)

                pool.wait_ge(a_done, l + 1)
                for c in range(NT):
                    pool.tensor_tensor(diag[:, c], ident[:, :].unsqueeze(1).broadcast_to((P, MH, P)),
                                       aa[:, c, :].unsqueeze(2).broadcast_to((P, MH, P)), ALU.mult).then_inc(diag_a, 1)
                pool.wait_ge(m_step, l * 6 + 6)
                pool.wait_ge(arow_psum, l * 2 + 2)
                for c in range(NT):
                    pool.tensor_tensor(diag[:, c], ident[:, :].unsqueeze(1).broadcast_to((P, MH, P)),
                                       mxs[:, 4 + c, :].unsqueeze(2).broadcast_to((P, MH, P)), ALU.mult)\
                        .then_inc(diag_m, 1)
                pool.wait_ge(mixp_loaded, l * 128 + 128)
                pool.wait_ge(ln_loaded, l * 64 + 32)
                pool.wait_ge(exp_small, l + 1)
                pool.wait_ge(mv_copied, l * 2 + 1)
                pool.tensor_tensor(vw[:, :, 0:MV + 1], mv[:, 0, :, 0:MV + 1],
                                   eout[:, 0, :].unsqueeze(2).broadcast_to((P, MH, MV + 1)), ALU.mult)\
                    .then_inc(vw_done, 1)
                with pool.If(l < 1):
                    load_ln(ln2_g[0:1, :], ln2_b[0:1, :], NT)
                    pool.wait_ge(ln_loaded, 64)
                    load_ln(ln1_g[1:2, :], ln1_b[1:2, :], 2 * NT)
            load_ln(ln2_g[1:2, :], ln2_b[1:2, :], 3 * NT)
            pool.memset(low8[:, :, :], 1.0).then_inc(const_step, 1)
            pool.iota(pass_no[:, :], pattern=[[1, MAX_PASSES]], base=0, channel_multiplier=0,
                      allow_small_or_imprecise_dtypes=True)
            pool.iota(expert_no[:, :], pattern=[[1, E]], base=0, channel_multiplier=0,
                      allow_small_or_imprecise_dtypes=True)
            pool.wait_ge(const_step, 2)
            pool.affine_select(out=low8[:, :, :], in_=low8[:, :, :], compare_op=ALU.is_gt, fill=0.0,
                               base=0, pattern=[[1, E], [-1, E]], channel_multiplier=0).then_inc(const_ready, 1)
            pool.wait_ge(mixp_loaded, 16 * 8 * DEPTH)
            pool.wait_ge(ln_loaded, 16 * 2 * 2 * DEPTH)
            pool.wait_ge(router_loaded, 32)
            pool.wait_ge(x_loaded, 16)
            pool.wait_ge(rope_in, 16)

        @block.scalar
        def _(act):
            def round_piece(R, g, n):
                if g % PIECES == 0:
                    act.wait_ge(raw_full[unit_of(g) % RAW_UNITS], R.loads + 16 * (unit_of(g) // RAW_UNITS) + 16)
                act.wait_ge(piece_used, R.pieces + g + 1)
                src = raw[:, unit_of(g) % RAW_UNITS, (g % PIECES) * n:(g % PIECES + 1) * n]
                act.activation(wh[:, piece_slot(g), 0:n], src, ACT.Copy).then_inc(rounded, 1)

            def pe_done(R, g):
                act.wait_ge(piece_used, R.pieces + SPLIT_SLOTS + g + 1)

            def transposed_high(base, t):
                act.wait_ge(xt_psum, base + t + 1)
                for b in range(2):
                    last = act.activation(xth[:, 4 * b:4 * b + 4, t * P:(t + 1) * P],
                                          B[2 * t + b][:, :].rearrange("p (k n) -> p k n", k=4), ACT.Copy)
                last.then_inc(xt_high, 1)

            def layer_norm_act(base):
                for t in range(NT):
                    act.wait_ge(ln_var, base + t + 1)
                    act.activation(lnc[:, t, 0:1], moments[:, t, 1:2], ACT.Sqrt, bias=eps[:, 0:1]).then_inc(ln_std, 1)
                for t in range(NT):
                    act.wait_ge(ln_coef, base + t + 1)
                    act.activation(xs[:, t, :], xs[:, t, :], ACT.Identity, bias=lnc[:, t, 2:3],
                                   scale=lnc[:, t, 1:2]).then_inc(ln_scaled, 1)

            def ffn_act(r0, chunks, half, tiles, tbank, chunk_off):
                def n_chunk(R):
                    return R.r - chunk_off

                def ht_high_parts(R, k, w):
                    act.wait_ge(ht_psum, k)
                    for t in range(tiles):
                        last = act.activation(hth[:, 0:w // P, t * P:(t + 1) * P],
                                              B[tbank[t]][:, 0:w].rearrange("p (f n) -> p f n", n=P), ACT.Copy)
                    last.then_inc(ht_high, 1)

                def silu(R, g, w):
                    pe_done(R, g)
                    for t in range(tiles):
                        last = act.activation(hbuf[:, t, 0:w], B[t][:, 0:w], ACT.Silu)
                    last.then_inc(silu_done, 1)

                def first(R):
                    for g in range(8):
                        round_piece(R, g, 2 * WIDE)
                        if g == 7:
                            silu(R, 3, WIDE)

                def chunk(R, w, wprev):
                    for g in range(8, 20):
                        round_piece(R, g, (2 * w if g < 16 else 2 * WIDE))
                        if g == 11:
                            ht_high_parts(R, n_chunk(R) + 1, wprev)
                        if g == 17:
                            silu(R, 11, w)

                def tail(R, w):
                    for g in range(8, 12):
                        round_piece(R, g, 2 * w)
                        if g == 9:
                            ht_high_parts(R, n_chunk(R) + 1, w)

                ffn_stretch(act, first, chunk, tail, r0, chunks, half)

            act.wait_ge(sin_in, 1)
            act.activation(sc8[:, :, :, :], ang[:, :, :, :], ACT.Sin).then_inc(sin_done, 1)
            for t in range(NT):
                transposed_high(0, t)

            with act.Fori(0, DEPTH) as l:
                R = Rounds(act, l * LAYER_ROUNDS)
                one, two, eight = act.snap(l * 1), act.snap(l * 2), act.snap(l * 8)
                FULL = 2 * WIDE
                for g in range(8):
                    round_piece(R, g, FULL)
                pe_done(R, 3)
                for t in range(NT):
                    act.activation(qk[:, t, 0:AW], B[t][:, :], ACT.Copy).then_inc(q_copied, 1)
                for g in range(8, 12):
                    round_piece(R, g, FULL)
                pe_done(R, 7)
                for t in range(NT):
                    act.activation(qk[:, t, AW:2 * AW], B[2 + t][:, :], ACT.Copy).then_inc(k_copied, 1)
                for g in range(12, 16):
                    round_piece(R, g, 2 * 2 * MH)
                round_piece(R, 16, FULL)
                round_piece(R, 17, FULL)
                pe_done(R, 11)
                act.wait_ge(dve_init, 1)
                for ct in range(4):
                    act.activation(mpre[:, ct, 3:3 + SEQ], B[4 + ct][:, 0:SEQ], ACT.Copy).then_inc(mqk_copied, 1)
                round_piece(R, 18, FULL)
                round_piece(R, 19, FULL)
                act.wait_ge(conv_done, one + 1)
                act.activation(mqkt[:, :, :], cacc[:, :, :], ACT.Silu).then_inc(conv_silu, 1)
                act.wait_ge(absf, one + 1)
                act.activation(gtmp[:, 1], gtmp[:, 0], ACT.Exp).then_inc(exp_f, 1)
                act.wait_ge(exp_f, one + 1)
                act.activation(gtmp[:, 2], gtmp[:, 1], ACT.Ln, bias=ones[:, 0:1]).then_inc(ln_f, 1)
                round_piece(R, 20, FULL)
                round_piece(R, 21, FULL)
                pe_done(R, 19)
                for t in range(NT):
                    act.activation(vv[:, t, :], B[2 + t][:, :], ACT.Copy).then_inc(v_copied, 1)
                act.wait_ge(ktok_psum, one + 1)
                act.activation(ktok[:, :], B[1][:, 0:MH * MK], ACT.Copy).then_inc(ktok_copied, 1)
                act.wait_ge(qkt_psum, one + 1)
                for b in range(2):
                    act.activation(qkt[:, 2 * b:2 * b + 2, :], B[4 + b][:, :].rearrange("p (j n) -> p j n", j=2),
                                   ACT.Copy).then_inc(qt_copied, 1)

                def probs(h):
                    act.wait_ge(score_ready, eight + h + 1)
                    if h >= 2:
                        act.wait_ge(probs_t_psum, eight + h - 1)
                    else:
                        act.wait_ge(dve_init, 1)
                    act.activation(pm[:, h % 2, 0:P], sm[:, h % 2, 0:P], ACT.Exp, bias=snb[:, h, 0:1],
                                   scale=AD ** -0.5, accum_out=rsum[:, 0, h:h + 1])
                    act.activation(pm[:, h % 2, P:3 * P], sm[:, h % 2, P:3 * P], ACT.Exp, bias=snb[:, h, 1:2],
                                   scale=AD ** -0.5, accum_out=rsum[:, 1, h:h + 1]).then_inc(probs_done, 1)

                def probs_transposed(h):
                    act.wait_ge(probs_t_psum, eight + h + 1)
                    if h >= 2:
                        act.wait_ge(att_psum, eight + h - 1)
                    act.activation(ptm[:, h % 2, :], B[6][:, 0:3 * P], ACT.Copy).then_inc(probs_t, 1)

                def copy_attention(half):
                    act.wait_ge(att_psum, eight + 4 * half + 4)
                    act.activation(araw[:, :, 4 * half:4 * half + 4, :],
                                   B[7][:, :].rearrange("p (t h d) -> p t h d", t=NT, h=4), ACT.Copy)\
                        .then_inc(att_copied, 1)

                def state_weights(c):
                    act.wait_ge(wlog, two + c + 1)
                    for h in range(MH):
                        last = act.activation(wtmp[:, c, h, :], wtmp[:, c, h, :], ACT.Exp, bias=aa[:, c, h:h + 1])
                    last.then_inc(wexp, 1)

                for s in range(8):
                    round_piece(R, 22 + s, FULL)
                    if s == 4:
                        pe_done(R, 23)
                        act.wait_ge(dve_init, 1)
                        for t in range(NT):
                            act.activation(mv[:, t, :, 0:MV], B[t][:, :].rearrange("p (h v) -> p h v", h=MH),
                                           ACT.Copy).then_inc(mv_copied, 1)
                    probs(s)
                    if s >= 1:
                        probs_transposed(s - 1)
                    if s == 3:
                        act.wait_ge(m_step, l * 6 + 6)
                        act.activation(eout[:, :, :], ein[:, :, :], ACT.Exp).then_inc(exp_small, 1)
                    if s == 4:
                        state_weights(0)
                    if s == 5:
                        state_weights(1)
                        copy_attention(0)
                    if s == 7:
                        act.wait_ge(c_psum, one + 1)
                        act.activation(csb[:, :, 0:MV + 1],
                                       B[5][:, 0:2 * (MV + 2)].rearrange("p (j v) -> p j v", j=2)[:, :, 0:MV + 1],
                                       ACT.Copy).then_inc(c_copied, 1)
                round_piece(R, 30, FULL)
                pe_done(R, 27)
                for t in range(NT):
                    act.activation(mo[:, t, :], B[t][:, :], ACT.Exp, scale=-1.0).then_inc(mo_exp, 1)
                probs_transposed(7)
                act.wait_ge(num_psum, two + 1)
                for b in range(2):
                    last = act.activation(tot[:, 0, 2 * b:2 * b + 2, 0:MV + 1],
                                          B[2 + b][:, 0:2 * (MV + 2)].rearrange("p (j v) -> p j v", j=2)[:, :, 0:MV + 1],
                                          ACT.Copy)
                last.then_inc(num0_copied, 1)
                round_piece(R, 31, FULL)
                copy_attention(1)
                act.wait_ge(inter_psum, one + 1)
                act.wait_ge(norm_step, l * 9 + 1)
                for h in range(MH):
                    last = act.activation(itmp[:, h, 0:MV + 1],
                                          B[4 + h % 2][:, (h // 2) * (MV + 2):(h // 2) * (MV + 2) + MV + 1],
                                          ACT.Copy, scale=ein[:, 1, h:h + 1])
                last.then_inc(inter_scaled, 1)
                act.wait_ge(att_copied, two + 2)
                act.activation(mix[:, :, 0:AW], araw[:, :, :, :].rearrange("p t h d -> p t (h d)"),
                               ACT.Square).then_inc(squares, 1)
                act.wait_ge(tot_done, one + 1)
                act.wait_ge(num0_copied, one + 1)
                for c in range(NT):
                    last = act.activation(mix[:, c, AW:D].rearrange("p (h v) -> p h v", h=MH), tot[:, c, :, 0:MV],
                                          ACT.Square)
                last.then_inc(squares, 1)
                round_piece(R, 32, FULL)
                round_piece(R, 33, FULL)
                act.wait_ge(mean_sq, one + 1)
                act.activation(norms[:, 3, :], norms[:, 2, :], ACT.Sqrt, bias=eps[:, 1:2]).then_inc(std_done, 1)
                xt0 = act.snap(l * 6)
                for t in range(NT):
                    transposed_high(xt0 + 2, t)
                round_piece(R, 34, FULL)
                round_piece(R, 35, FULL)
                layer_norm_act(act.snap(l * 4))
                for t in range(NT):
                    transposed_high(xt0 + 4, t)
                with act.If(l < 1):
                    ffn_act(MIX_ROUNDS, DENSE_FULL, True, NT, (2, 3), 3)
                    layer_norm_act(2)
                    for t in range(NT):
                        transposed_high(6, t)

            act.wait_ge(router_loaded, 32)
            act.activation(rwh[:, :, :], rw[:, :, :], ACT.Copy).then_inc(rw_high, 1)
            act.wait_ge(ln_out, 3 * NT)
            for t in range(NT):
                act.activation(xh[:, t, :], xs[:, t, :], ACT.Copy).then_inc(x_high, 1)
            act.wait_ge(route_step, 8)
            act.activation(topv[:, 3, :], topv[:, 2, :], ACT.Exp).then_inc(exp_f, 1)
            act.wait_ge(table_ready, 1)
            passes = act.value_load(tabi[0:1, MAX_PASSES:MAX_PASSES + 1], min_val=1, max_val=MAX_PASSES)
            with act.Fori(0, passes) as p:
                act.wait_ge(pick_psum, p + 1)
                act.activation(pickt[:, :], B[6][:, 0:SEQ], ACT.Copy).then_inc(pick_copied, 1)
                act.wait_ge(gathered, p + 1)
                for b in range(2):
                    last = act.activation(xth[:, 4 * b:4 * b + 4, 0:P], B[b][:, :].rearrange("p (k n) -> p k n", k=4),
                                          ACT.Copy)
                last.then_inc(gath_high, 1)
                ffn_act(act.snap(p * MOE_CHUNKS + MOE_BASE), MOE_CHUNKS, False, 1, (7,),
                        MOE_BASE - DENSE_FULL - 1)
                pe_done(Rounds(act, p * MOE_CHUNKS + (MOE_BASE + MOE_CHUNKS)), -1)
                for n in range(2):
                    act.activation(yh[:, n * WIDE:(n + 1) * WIDE], B[4 + n][:, :], ACT.Copy).then_inc(y_high, 1)
            layer_norm_act(3 * NT)

        @block.vector
        def _(dve):
            dve.sem_inc(split, ROUND)

            def low_piece(R, g, n):
                dve.wait_ge(rounded, R.pieces + g + 1)
                src = raw[:, unit_of(g) % RAW_UNITS, (g % PIECES) * n:(g % PIECES + 1) * n]
                dve.tensor_tensor(wl[:, piece_slot(g), 0:n], src, wh[:, piece_slot(g), 0:n].bitcast(F32),
                                  ALU.subtract).then_inc(split, 1)

            def pe_done(R, g):
                dve.wait_ge(piece_used, R.pieces + SPLIT_SLOTS + g + 1)

            def transposed_low(base, t):
                dve.wait_ge(xt_high, base + t + 1)
                for b in range(2):
                    last = dve.tensor_tensor(xtl[:, 4 * b:4 * b + 4, t * P:(t + 1) * P],
                                             B[2 * t + b][:, :].rearrange("p (k n) -> p k n", k=4),
                                             xth[:, 4 * b:4 * b + 4, t * P:(t + 1) * P].bitcast(F32), ALU.subtract)
                last.then_inc(xt_low, 1)

            def layer_norm_dve(base, params, steps):
                for t in range(NT):
                    for n in range(2):
                        last = dve.bn_stats(stats[:, t, n, :], xs[:, t, n * WIDE:(n + 1) * WIDE])
                    last.then_inc(ln_step, 1)
                dve.wait_ge(ln_step, steps + NT)
                dve.memset(lnc[:, :, 0:1], 1.0)
                for t in range(NT):
                    dve.bn_aggr(moments[:, t, :], stats[:, t, :, :]).then_inc(ln_var, 1)
                for t in range(NT):
                    dve.wait_ge(ln_std, base + t + 1)
                    dve.reciprocal(lnc[:, t, 1:2], lnc[:, t, 0:1]).then_inc(ln_step, 1)
                    dve.wait_ge(ln_step, steps + 2 + 2 * t + 1)
                    dve.scalar_tensor_tensor(out=lnc[:, t, 2:3], in0=moments[:, t, 0:1], scalar=-1.0,
                                             in1=lnc[:, t, 1:2], op0=ALU.mult, op1=ALU.mult).then_inc(ln_coef, 1)
                    if t == 0:
                        dve.wait_ge(ln_loaded, params)
                    dve.wait_ge(ln_scaled, base + t + 1)
                    dve.tensor_tensor(xs[:, t, :], xs[:, t, :], lng[:, :], ALU.mult).then_inc(ln_step, 1)
                    dve.wait_ge(ln_step, steps + 2 + 2 * t + 2)
                    dve.tensor_tensor(xs[:, t, :], xs[:, t, :], lnb[:, :], ALU.add).then_inc(ln_out, 1)

            def ffn_dve(r0, chunks, half, tiles, tbank, chunk_off):
                def ht_low_parts(R, k, w):
                    dve.wait_ge(ht_high, k)
                    for t in range(tiles):
                        last = dve.tensor_tensor(htl[:, 0:w // P, t * P:(t + 1) * P],
                                                 B[tbank[t]][:, 0:w].rearrange("p (f n) -> p f n", n=P),
                                                 hth[:, 0:w // P, t * P:(t + 1) * P].bitcast(F32), ALU.subtract)
                    last.then_inc(ht_low, 1)

                def hidden(R, g, k, w):
                    dve.wait_ge(silu_done, k)
                    pe_done(R, g)
                    for t in range(tiles):
                        last = dve.tensor_tensor(hbuf[:, t, 0:w], hbuf[:, t, 0:w], B[2 + t][:, 0:w], ALU.mult)
                    last.then_inc(h_done, 1)

                def first(R):
                    for g in range(8):
                        low_piece(R, g, 2 * WIDE)
                    hidden(R, 7, R.r - chunk_off + 1, WIDE)

                def chunk(R, w, wprev):
                    for g in range(8, 20):
                        low_piece(R, g, (2 * w if g < 16 else 2 * WIDE))
                        if g == 11:
                            ht_low_parts(R, R.r - chunk_off + 1, wprev)
                    hidden(R, 15, R.r - chunk_off + 2, w)

                def tail(R, w):
                    for g in range(8, 12):
                        low_piece(R, g, 2 * w)
                        if g == 9:
                            ht_low_parts(R, R.r - chunk_off + 1, w)

                ffn_stretch(dve, first, chunk, tail, r0, chunks, half)

            dve.memset(mpre[:, :, 0:3], 0.0)
            dve.memset(mv[:, :, :, :], 1.0)
            dve.memset(smax[:, :, :], 0.0).then_inc(dve_init, 1)
            for j in range(HALF_ROPE):
                last = dve.memset(invf[:, j:j + 1], float(ROPE_THETA ** (-j / HALF_ROPE)))
            last.then_inc(rope_step, 1)
            dve.wait_ge(rope_in, 16)
            dve.tensor_copy(posf[:, :], posi[:, :]).then_inc(rope_step, 1)
            dve.wait_ge(rope_step, 2)
            for t in range(NT):
                last = dve.tensor_scalar(ang[:, 0, t, :], invf[:, :], posf[:, t:t + 1], None, ALU.mult)
            last.then_inc(rope_step, 1)
            dve.wait_ge(rope_step, 3)
            dve.tensor_scalar(turn[:, 0], ang[:, 0], 1.0 / TWO_PI, None, ALU.mult)
            dve.tensor_scalar(turn[:, 1], ang[:, 0], 1.0 / TWO_PI, 0.25, ALU.mult, ALU.add).then_inc(rope_step, 1)
            dve.tensor_copy(ang[:, 1], ang[:, 0])
            dve.wait_ge(rope_step, 4)
            dve.tensor_copy(turni[:, :, :, :], turn[:, :, :, :]).then_inc(rope_step, 1)
            dve.wait_ge(rope_step, 5)
            dve.tensor_copy(turn[:, :, :, :], turni[:, :, :, :]).then_inc(rope_step, 1)
            for i, part in enumerate((6.28125, 0.0019350051879882812, TWO_PI - 6.28125 - 0.0019350051879882812)):
                dve.wait_ge(rope_step, 6 + i)
                dve.scalar_tensor_tensor(out=ang[:, :, :, :], in0=turn[:, :, :, :], scalar=-part,
                                         in1=ang[:, :, :, :], op0=ALU.mult, op1=ALU.add).then_inc(rope_step, 1)
            dve.wait_ge(rope_step, 9)
            dve.tensor_scalar(ang[:, 1], ang[:, 1], TWO_PI / 4, None, ALU.add).then_inc(rope_step, 1)
            dve.wait_ge(rope_step, 10)
            dve.tensor_scalar(ang[:, :, :, :], ang[:, :, :, :], PI_SAFE, -PI_SAFE, ALU.min, ALU.max).then_inc(sin_in, 1)
            dve.wait_ge(sin_done, 1)
            for i in range(2):
                last = dve.tensor_copy(sincos[:, i],
                                       sc8[:, i].unsqueeze(2).broadcast_to((P, NT, 2 * AH, HALF_ROPE)))
            last.then_inc(rope_table, 1)
            dve.sem_inc(dve_init, 1)
            for t in range(NT):
                transposed_low(0, t)

            with dve.Fori(0, DEPTH) as l:
                R = Rounds(dve, l * LAYER_ROUNDS)
                one, two, four, eight = (dve.snap(l * k) for k in (1, 2, 4, 8))
                FULL = 2 * WIDE
                for g in range(12):
                    low_piece(R, g, FULL)
                heads = qk[:, :, :].rearrange("p t (h d) -> p t h d", d=AD)
                x1, x2 = heads[:, :, :, 0:HALF_ROPE], heads[:, :, :, HALF_ROPE:2 * HALF_ROPE]
                sin, cos = sincos[:, 0], sincos[:, 1]
                dve.wait_ge(q_copied, two + 2)
                dve.wait_ge(k_copied, two + 2)
                dve.wait_ge(rope_table, 1)
                dve.tensor_tensor(rt[:, 0], x1, cos, ALU.mult)
                dve.tensor_tensor(rt[:, 1], x2, sin, ALU.mult)
                dve.tensor_tensor(rt[:, 2], x2, cos, ALU.mult)
                dve.tensor_tensor(rt[:, 3], x1, sin, ALU.mult).then_inc(rot_step, 1)
                dve.wait_ge(rot_step, one + 1)
                dve.tensor_tensor(x1, rt[:, 0], rt[:, 1], ALU.subtract)
                dve.tensor_tensor(x2, rt[:, 2], rt[:, 3], ALU.add).then_inc(roped, 1)
                for g in range(12, 16):
                    low_piece(R, g, 2 * 2 * MH)
                low_piece(R, 16, FULL)
                low_piece(R, 17, FULL)
                dve.wait_ge(mixp_loaded, l * 128 + 128)
                dve.wait_ge(mqk_copied, four + 4)
                for ct in range(4):
                    last = dve.tensor_scalar(cacc[:, ct, :], mpre[:, ct, 0:SEQ], cw[:, ct, 0:1], cb[:, ct:ct + 1],
                                             ALU.mult, ALU.add)
                last.then_inc(conv_step, 1)
                for j in range(1, 4):
                    dve.wait_ge(conv_step, l * 3 + j)
                    for ct in range(4):
                        last = dve.scalar_tensor_tensor(out=cacc[:, ct, :], in0=mpre[:, ct, j:j + SEQ],
                                                        scalar=cw[:, ct, j:j + 1], in1=cacc[:, ct, :],
                                                        op0=ALU.mult, op1=ALU.add)
                    last.then_inc(conv_step if j < 3 else conv_done, 1)
                low_piece(R, 18, FULL)
                low_piece(R, 19, FULL)
                pe_done(R, 15)
                for t in range(NT):
                    last = dve.tensor_tensor(gates[:, t, :], B[t][:, 0:2 * MH], gbias[:, :], ALU.add)
                last.then_inc(gates_in, 1)
                dve.wait_ge(gates_in, one + 1)
                dve.scalar_tensor_tensor(out=gtmp[:, 0], in0=gates[:, :, MH:2 * MH], scalar=-1.0,
                                         in1=gates[:, :, MH:2 * MH], op0=ALU.mult, op1=ALU.min).then_inc(absf, 1)
                low_piece(R, 20, FULL)
                dve.wait_ge(ln_f, one + 1)
                dve.scalar_tensor_tensor(out=gtmp[:, 3], in0=gates[:, :, MH:2 * MH], scalar=0.0, in1=gtmp[:, 2],
                                         op0=ALU.min, op1=ALU.subtract).then_inc(logf_done, 1)
                low_piece(R, 21, FULL)
                dve.wait_ge(qkt_psum, one + 1)
                for b in range(2):
                    dve.tensor_copy(qkt[:, 4 + 2 * b:6 + 2 * b, :], B[6 + b][:, :].rearrange("p (j n) -> p j n", j=2))\
                        .then_inc(kt_copied, 1)
                dve.wait_ge(cum_psum, one + 1)
                dve.tensor_copy(bl[:, :, :], B[0][:, 0:4 * MH].rearrange("p (c n) -> p c n", c=NT)).then_inc(cum_copied, 1)
                dve.wait_ge(cum_copied, one + 1)
                dve.tensor_tensor(aa[:, :, :], gates[:, :, 0:MH], bl[:, :, 0:MH], ALU.subtract).then_inc(a_done, 1)

                def scores(h):
                    dve.wait_ge(score_psum, eight + h + 1)
                    if h >= 2:
                        dve.wait_ge(probs_done, eight + h - 1)
                    dve.tensor_tensor(sm[:, h % 2, :], B[4][:, 0:3 * P], mask3[:, :], ALU.add).then_inc(masked, 1)
                    dve.wait_ge(masked, eight + h + 1)
                    dve.reduce_max(smax[:, h, 0:1], sm[:, h % 2, 0:P], AX_X)
                    dve.reduce_max(smax[:, h, 1:2], sm[:, h % 2, P:3 * P], AX_X).then_inc(row_max, 1)
                    dve.wait_ge(row_max, eight + h + 1)
                    dve.tensor_scalar(snb[:, h, :], smax[:, h, :], -(AD ** -0.5), None, ALU.mult)\
                        .then_inc(score_ready, 1)

                def row_maxima():
                    causal = mask3[:, 0:P].unsqueeze(1).broadcast_to((P, MH, P))
                    for c in range(NT):
                        dve.wait_ge(arow_psum, two + c + 1)
                        dve.tensor_tensor(wtmp[:, c], B[2 + c][:, :].rearrange("p (h n) -> p h n", h=MH), causal,
                                          ALU.add).then_inc(amask_step, 1)
                    dve.reduce_max(mxs[:, 2, :], B[2][:, :].rearrange("p (h n) -> p h n", h=MH), AX_X)
                    for c in range(NT):
                        dve.wait_ge(amask_step, two + c + 1)
                        dve.reduce_max(mxs[:, c, :], wtmp[:, c], AX_X).then_inc(m_step, 1)
                    six = dve.snap(l * 6)
                    dve.wait_ge(m_step, six + 2)
                    dve.tensor_scalar(mxs[:, 2, :], mxs[:, 2, :], 0.0, None, ALU.max)
                    dve.tensor_scalar(mxs[:, 4, :], mxs[:, 0, :], 0.0, None, ALU.max).then_inc(m_step, 1)
                    dve.wait_ge(m_step, six + 3)
                    dve.tensor_tensor(mxs[:, 3, :], bl[:, 0, MH:2 * MH], mxs[:, 2, :], ALU.add).then_inc(m_step, 1)
                    dve.tensor_tensor(ein[:, 0, :], aa[:, 0, :], mxs[:, 2, :], ALU.subtract)
                    dve.wait_ge(m_step, six + 4)
                    dve.tensor_tensor(mxs[:, 5, :], mxs[:, 1, :], mxs[:, 3, :], ALU.max).then_inc(m_step, 1)
                    dve.wait_ge(m_step, six + 5)
                    dve.tensor_tensor(ein[:, 1, :], mxs[:, 3, :], mxs[:, 5, :], ALU.subtract)
                    dve.scalar_tensor_tensor(out=ein[:, 2:4, :], in0=bl[:, :, 0:MH], scalar=-1.0, in1=mxs[:, 4:6, :],
                                             op0=ALU.mult, op1=ALU.subtract).then_inc(m_step, 1)

                def weight_logs():
                    for c in range(NT):
                        dve.wait_ge(mrow_psum, two + c + 1)
                        dve.tensor_tensor(wtmp[:, c], maskt[:, :].unsqueeze(1).broadcast_to((P, MH, P)),
                                          B[2 + c][:, :].rearrange("p (h n) -> p h n", h=MH), ALU.subtract)\
                            .then_inc(wlog, 1)

                def weighted_scores(c):
                    dve.wait_ge(wexp, two + c + 1)
                    dve.wait_ge(kq_psum, one + 1)
                    for j in range(2):
                        last = dve.scalar_tensor_tensor(
                            out=st[:, c].rearrange("p (i j) n -> p i j n", j=2)[:, :, j, :],
                            in0=B[2 + j][:, 2 * c * P:(2 * c + 2) * P].rearrange("p (i n) -> p i n", i=2),
                            scalar=MK ** -0.5, in1=wtmp[:, c].rearrange("p (i j) n -> p i j n", j=2)[:, :, j, :],
                            op0=ALU.mult, op1=ALU.mult)
                    last.then_inc(st_done, 1)

                for s in range(8):
                    low_piece(R, 22 + s, FULL)
                    scores(s)
                    if s == 2:
                        row_maxima()
                    if s == 4:
                        weight_logs()
                    if s == 5:
                        weighted_scores(0)
                    if s == 6:
                        weighted_scores(1)
                low_piece(R, 30, FULL)
                nine = dve.snap(l * 9)
                dve.wait_ge(exp_small, one + 1)
                dve.tensor_scalar(ein[:, 1, :], eout[:, 1, :], MK ** -0.5, None, ALU.mult).then_inc(norm_step, 1)
                dve.wait_ge(mo_exp, two + 2)
                dve.tensor_scalar(mo[:, :, :], mo[:, :, :], 1.0, None, ALU.add).then_inc(norm_step, 1)
                dve.wait_ge(norm_step, nine + 2)
                dve.reciprocal(mo[:, :, :], mo[:, :, :]).then_inc(norm_step, 1)
                dve.wait_ge(norm_step, nine + 3)
                dve.tensor_tensor(mo[:, :, :], mo[:, :, :], gnm[:, :].unsqueeze(1).broadcast_to((P, NT, MH * MV)),
                                  ALU.mult).then_inc(mo_gate, 1)
                low_piece(R, 31, FULL)
                dve.wait_ge(num_psum, two + 2)
                dve.wait_ge(inter_scaled, one + 1)
                for b in range(2):
                    last = dve.tensor_tensor(tot[:, 1, 2 * b:2 * b + 2, 0:MV + 1],
                                             B[b][:, 0:2 * (MV + 2)].rearrange("p (j v) -> p j v", j=2)[:, :, 0:MV + 1],
                                             itmp[:, 2 * b:2 * b + 2, 0:MV + 1], ALU.add)
                last.then_inc(tot_done, 1)
                dve.wait_ge(probs_done, eight + 8)
                dve.wait_ge(num0_copied, one + 1)
                dve.wait_ge(tot_done, one + 1)
                dve.reciprocal(norms[:, 0, 0:16], rsum[:, :, :].rearrange("p t h -> p (t h)"))
                dve.scalar_tensor_tensor(out=norms[:, 3, 16:24].rearrange("p (c h) -> p c h", c=NT),
                                         in0=tot[:, :, :, MV], scalar=-1.0, in1=tot[:, :, :, MV],
                                         op0=ALU.mult, op1=ALU.max).then_inc(norm_step, 1)
                dve.wait_ge(norm_step, nine + 4)
                dve.tensor_tensor(norms[:, 3, 16:24], norms[:, 3, 16:24],
                                  eout[:, 2:4, :].rearrange("p c h -> p (c h)"), ALU.max).then_inc(norm_step, 1)
                dve.wait_ge(norm_step, nine + 5)
                dve.reciprocal(norms[:, 0, 16:24], norms[:, 3, 16:24]).then_inc(norm_step, 1)
                dve.wait_ge(squares, two + 2)
                for t in range(NT):
                    dve.reduce_sum(norms[:, 1, 8 * t:8 * t + 8],
                                   mix[:, t, 0:AW].rearrange("p (h d) -> p h d", h=AH), AX_X)
                for c in range(NT):
                    last = dve.reduce_sum(norms[:, 1, 16 + 4 * c:20 + 4 * c],
                                          mix[:, c, AW:D].rearrange("p (h v) -> p h v", h=MH), AX_X)
                last.then_inc(norm_step, 1)
                dve.wait_ge(norm_step, nine + 7)
                dve.scalar_tensor_tensor(out=norms[:, 2, 0:16], in0=norms[:, 1, 0:16], scalar=1.0 / AD,
                                         in1=norms[:, 0, 0:16], op0=ALU.mult, op1=ALU.mult)
                dve.scalar_tensor_tensor(out=norms[:, 2, 16:24], in0=norms[:, 1, 16:24], scalar=1.0 / MV,
                                         in1=norms[:, 0, 16:24], op0=ALU.mult, op1=ALU.mult).then_inc(norm_step, 1)
                dve.wait_ge(norm_step, nine + 8)
                dve.tensor_tensor(norms[:, 2, :], norms[:, 2, :], norms[:, 0, :], ALU.mult).then_inc(mean_sq, 1)
                low_piece(R, 32, FULL)
                low_piece(R, 33, FULL)
                dve.wait_ge(std_done, one + 1)
                dve.reciprocal(norms[:, 4, :], norms[:, 3, :]).then_inc(norm_step, 1)
                dve.wait_ge(norm_step, nine + 9)
                dve.tensor_tensor(norms[:, 4, :], norms[:, 4, :], norms[:, 0, :], ALU.mult).then_inc(mix_done, 1)
                dve.wait_ge(mo_gate, one + 1)
                five = dve.snap(l * 5)
                dve.wait_ge(mix_done, five + 1)
                for t in range(NT):
                    dve.tensor_tensor(mix[:, t, 0:AW].rearrange("p (h d) -> p h d", h=AH), araw[:, t],
                                      norms[:, 4, 8 * t:8 * t + 8].unsqueeze(2).broadcast_to((P, AH, AD)), ALU.mult)
                    dve.tensor_tensor(mix[:, t, AW:D].rearrange("p (h v) -> p h v", h=MH), tot[:, t, :, 0:MV],
                                      norms[:, 4, 16 + 4 * t:20 + 4 * t].unsqueeze(2).broadcast_to((P, MH, MV)),
                                      ALU.mult).then_inc(mix_done, 1)
                    dve.wait_ge(mix_done, five + 2 + 2 * t)
                    dve.tensor_tensor(mix[:, t, 0:AW], mix[:, t, 0:AW], gna[:, :], ALU.mult)
                    dve.tensor_tensor(mix[:, t, AW:D], mix[:, t, AW:D], mo[:, t, :], ALU.mult).then_inc(mix_done, 1)
                xt0 = dve.snap(l * 6)
                for t in range(NT):
                    transposed_low(xt0 + 2, t)
                low_piece(R, 34, FULL)
                low_piece(R, 35, FULL)
                for n in range(2):
                    pe_done(R, 31 + 4 * n)
                    for t in range(NT):
                        cols = xs[:, t, n * WIDE:(n + 1) * WIDE]
                        last = dve.scalar_tensor_tensor(out=cols, in0=cols, scalar=ALPHA, in1=B[4 + 2 * t + n][:, :],
                                                        op0=ALU.mult, op1=ALU.add)
                last.then_inc(residual, 1)
                dve.wait_ge(residual, two + 1)
                layer_norm_dve(dve.snap(l * 4), l * 64 + 32, dve.snap(l * 12))
                dve.wait_ge(ln_out, four + 2)
                dve.sem_inc(dve_init, 1)
                for t in range(NT):
                    transposed_low(xt0 + 4, t)
                with dve.If(l < 1):
                    ffn_dve(MIX_ROUNDS, DENSE_FULL, True, NT, (2, 3), 3)
                    pe_done(Rounds(dve, LAYER_ROUNDS), -1)
                    for n in range(2):
                        for t in range(NT):
                            cols = xs[:, t, n * WIDE:(n + 1) * WIDE]
                            last = dve.scalar_tensor_tensor(out=cols, in0=cols, scalar=ALPHA,
                                                            in1=B[4 + 2 * t + n][:, :], op0=ALU.mult, op1=ALU.add)
                    last.then_inc(residual, 1)
                    dve.wait_ge(residual, 2)
                    layer_norm_dve(2, 64, 6)
                    for t in range(NT):
                        transposed_low(6, t)

            dve.wait_ge(rw_high, 1)
            dve.tensor_tensor(rwl[:, :, :], rw[:, :, :], rwh[:, :, :].bitcast(F32), ALU.subtract).then_inc(rw_low, 1)
            for t in range(NT):
                dve.wait_ge(x_high, t + 1)
                dve.tensor_tensor(xl[:, t, :], xs[:, t, :], xh[:, t, :].bitcast(F32), ALU.subtract).then_inc(x_low, 1)
            for t in range(NT):
                dve.wait_ge(x_low, t + 1)
                dve.tensor_scalar(xs[:, t, :], xs[:, t, :], ALPHA, None, ALU.mult).then_inc(accumulated, 1)
            steps = [0]

            def then(ins):
                steps[0] += 1
                ins.then_inc(route_step, 1)
                dve.wait_ge(route_step, steps[0])

            dve.wait_ge(logits_psum, 1)
            dve.wait_ge(const_ready, 2)
            for t in range(NT):
                last = dve.tensor_tensor(lg[:, t, :], B[t][:, 0:E], rb[:, :], ALU.add)
            then(last)
            for t in range(NT):
                other = lg[:, t, :].unsqueeze(1).broadcast_to((P, E, E))
                own = lg[:, t, :].unsqueeze(2).broadcast_to((P, E, E))
                dve.tensor_tensor(cmp4[:, 0, t], other, own, ALU.is_gt)
                last = dve.tensor_tensor(cmp4[:, 1, t], other, own, ALU.is_equal)
            then(last)
            for t in range(NT):
                last = dve.tensor_tensor(cmp4[:, 1, t], cmp4[:, 1, t], low8[:, :, :], ALU.mult)
            then(last)
            for t in range(NT):
                last = dve.tensor_tensor(cmp4[:, 2, t], cmp4[:, 0, t], cmp4[:, 1, t], ALU.add)
            then(last)
            for t in range(NT):
                last = dve.reduce_sum(rank[:, t, :], cmp4[:, 2, t], AX_X)
            then(last)
            dve.tensor_scalar(isel[:, 0], rank[:, :, :], 0.0, None, ALU.is_equal)
            dve.tensor_scalar(isel[:, 1], rank[:, :, :], 1.0, None, ALU.is_equal)
            dve.tensor_scalar(isel[:, 2], rank[:, :, :], 1.0, None, ALU.is_le).then_inc(picks_ready, 1)
            dve.wait_ge(picks_ready, 1)
            for i in range(2):
                last = dve.tensor_tensor(cmp4[:, 0, :, i, :], isel[:, i], lg[:, :, :], ALU.mult)
            then(last)
            for i in range(2):
                last = dve.reduce_sum(topv[:, i, :], cmp4[:, 0, :, i, :], AX_X)
            then(last)
            then(dve.tensor_tensor(topv[:, 2, :], topv[:, 1, :], topv[:, 0, :], ALU.subtract))
            dve.wait_ge(exp_f, DEPTH + 1)
            then(dve.tensor_scalar(topv[:, 4, :], topv[:, 3, :], 1.0, None, ALU.add))
            then(dve.reciprocal(topv[:, 4, :], topv[:, 4, :]))
            then(dve.tensor_tensor(topv[:, 5, :], topv[:, 4, :], topv[:, 3, :], ALU.mult))
            for t in range(NT):
                last = dve.tensor_scalar(comb[:, t, :], isel[:, 0, t, :], topv[:, 4, t:t + 1], None, ALU.mult)
            then(last)
            for t in range(NT):
                last = dve.scalar_tensor_tensor(out=comb[:, t, :], in0=isel[:, 1, t, :], scalar=topv[:, 5, t:t + 1],
                                                in1=comb[:, t, :], op0=ALU.mult, op1=ALU.add)
            then(last)
            dve.wait_ge(pos_psum, 1)
            then(dve.tensor_copy(posc[:, :, :], B[2][:, 0:3 * E].rearrange("p (a e) -> p a e", a=3)))
            dve.tensor_scalar(blk[:, 0, :], posc[:, 2, :], 0.0, None, ALU.is_gt)
            then(dve.tensor_scalar(blk[:, 1, :], posc[:, 2, :], float(P), None, ALU.is_gt))
            then(dve.tensor_tensor(blk[:, 2, :], blk[:, 0, :], blk[:, 1, :], ALU.add))
            dve.tensor_copy(blk[:, 3, 0:1], blk[:, 2, 0:1])
            then(dve.memset(blk[:, 4, 0:1], 0.0))
            for i in range(1, E):
                then(dve.tensor_tensor(blk[:, 3, i:i + 1], blk[:, 3, i - 1:i], blk[:, 2, i:i + 1], ALU.add))
            then(dve.tensor_copy(blk[:, 4, 1:E], blk[:, 3, 0:E - 1]))
            shape = (P, MAX_PASSES, E)
            passn = pass_no[:, :].unsqueeze(2).broadcast_to(shape)
            dve.tensor_tensor(pt11[:, 0], passn, blk[:, 4, :].unsqueeze(1).broadcast_to(shape), ALU.is_ge)
            dve.tensor_tensor(pt11[:, 1], passn, blk[:, 3, :].unsqueeze(1).broadcast_to(shape), ALU.is_lt)
            then(dve.tensor_tensor(pt11[:, 2], passn, blk[:, 4, :].unsqueeze(1).broadcast_to(shape), ALU.subtract))
            then(dve.tensor_tensor(pt11[:, 0], pt11[:, 0], pt11[:, 1], ALU.mult))
            then(dve.scalar_tensor_tensor(out=pt11[:, 2], in0=pt11[:, 2], scalar=float(P), in1=pt11[:, 0],
                                          op0=ALU.mult, op1=ALU.mult))
            then(dve.tensor_tensor(pt11[:, 3], pt11[:, 0], expert_no[:, :].unsqueeze(1).broadcast_to(shape), ALU.mult))
            dve.reduce_sum(tabf[:, 0:MAX_PASSES], pt11[:, 3], AX_X)
            then(dve.tensor_copy(tabf[:, MAX_PASSES:MAX_PASSES + 1], blk[:, 3, E - 1:E]))
            dve.tensor_copy(tabi[:, :], tabf[:, :]).then_inc(table_ready, 1)
            for t in range(NT):
                then(dve.tensor_scalar(posc[:, t, :], posc[:, t, :], 4096.0, None, ALU.add))
                then(dve.tensor_tensor(posc[:, t, :], posc[:, t, :], isel[:, 2, t, :], ALU.mult))
                then(dve.tensor_scalar(posc[:, t, :], posc[:, t, :], -4096.0, None, ALU.add))
                then(dve.tensor_tensor(pt11[:, 3], pt11[:, 0], posc[:, t, :].unsqueeze(1).broadcast_to(shape), ALU.mult))
                dve.tensor_tensor(pt11[:, 4], pt11[:, 0], comb[:, t, :].unsqueeze(1).broadcast_to(shape), ALU.mult)
                then(dve.tensor_tensor(pt11[:, 3], pt11[:, 3], pt11[:, 2], ALU.subtract))
                dve.reduce_sum(slotpos[:, t, :], pt11[:, 3], AX_X)
                then(dve.reduce_sum(cbp[:, t, :], pt11[:, 4], AX_X))

            dve.wait_ge(table_ready, 1)
            passes = dve.value_load(tabi[0:1, MAX_PASSES:MAX_PASSES + 1], min_val=1, max_val=MAX_PASSES)
            with dve.Fori(0, passes) as p:
                for t in range(NT):
                    last = dve.tensor_scalar(pick[:, t, :], slot_no[:, :], slotpos[:, t, bass.ds(p, 1)], None,
                                             ALU.is_equal)
                last.then_inc(pick_done, 1)
                dve.wait_ge(gathered, p + 1)
                for b in range(2):
                    last = dve.tensor_copy(xtl[:, 4 * b:4 * b + 4, 0:P], B[2 + b][:, :].rearrange("p (k n) -> p k n", k=4))
                last.then_inc(gath_low, 1)
                ffn_dve(dve.snap(p * MOE_CHUNKS + MOE_BASE), MOE_CHUNKS, False, 1, (7,), MOE_BASE - DENSE_FULL - 1)
                for n in range(2):
                    dve.wait_ge(y_high, p * 2 + n + 1)
                    dve.tensor_tensor(yl[:, n * WIDE:(n + 1) * WIDE], B[4 + n][:, :],
                                      yh[:, n * WIDE:(n + 1) * WIDE].bitcast(F32), ALU.subtract).then_inc(y_low, 1)
                dve.wait_ge(scattered, p + 1)
                dve.wait_ge(accumulated, p + NT)
                for t in range(NT):
                    for n in range(2):
                        cols = xs[:, t, n * WIDE:(n + 1) * WIDE]
                        last = dve.scalar_tensor_tensor(out=cols, in0=B[2 * t + n][:, :],
                                                        scalar=cbp[:, t, bass.ds(p, 1)], in1=cols,
                                                        op0=ALU.mult, op1=ALU.add)
                last.then_inc(accumulated, 1)
            dve.wait_ge(accumulated, dve.snap(passes + NT))
            layer_norm_dve(3 * NT, 128, 18)

        @block.tensor
        def _(pe):
            pe.sem_inc(piece_used, SPLIT_SLOTS)
            pe.wait_ge(const_ready, 1)

            def mm3(out_ap, high, low, w_high, w_low, start, stop):
                pe.matmul(out_ap, high, w_high, start=start, stop=False, skip_group_check=True)
                pe.matmul(out_ap, high, w_low, start=False, stop=False, skip_group_check=True)
                return pe.matmul(out_ap, low, w_high, start=False, stop=stop, skip_group_check=True)

            def use_piece(R, g, per_piece, width, body):
                pe.wait_ge(split, R.pieces + ROUND + g + 1)
                for i in range(per_piece):
                    s = (g % PIECES) * per_piece + i
                    cols = slice(i * width, (i + 1) * width)
                    last = body(s, wh[:, piece_slot(g), cols], wl[:, piece_slot(g), cols])
                last.then_inc(piece_used, 1)

            def project(banks, width=WIDE, tiles=NT):
                def body(s, w_high, w_low):
                    for t in range(tiles):
                        last = mm3(B[banks[t]][:, 0:width], xth[:, s, t * P:(t + 1) * P], xtl[:, s, t * P:(t + 1) * P],
                                   w_high, w_low, s == 0, s == KD - 1)
                    return last
                return body

            def project_transposed(s, w_high, w_low):
                for ct in range(4):
                    out_ap, cols = B[4 + ct][:, 0:SEQ], slice(ct * P, (ct + 1) * P)
                    pe.matmul(out_ap, w_high[:, cols], xth[:, s, :], start=s == 0, stop=False)
                    pe.matmul(out_ap, w_high[:, cols], xtl[:, s, :], start=False, stop=False)
                    last = pe.matmul(out_ap, w_low[:, cols], xth[:, s, :], start=False, stop=s == KD - 1)
                return last

            def transpose_tile(src, t):
                for k in range(KD):
                    last = pe.transpose(B[2 * t + k // 4][:, (k % 4) * P:(k % 4 + 1) * P],
                                        src[:, t, k * P:(k + 1) * P], ident[:, :])
                last.then_inc(xt_psum, 1)

            def down_body(tiles, stop_at):
                def body(s, w_high, w_low):
                    f, n = s // 2, s % 2
                    for t in range(tiles):
                        last = mm3(B[4 + 2 * t + n][:, :], hth[:, f, t * P:(t + 1) * P], htl[:, f, t * P:(t + 1) * P],
                                   w_high, w_low, False, f == stop_at)
                    return last
                return body

            def ffn_pe(r0, chunks, half, tiles, tbank, chunk_off):
                def transpose_h(k, w):
                    pe.wait_ge(h_done, k)
                    for t in range(tiles):
                        for f in range(w // P):
                            last = pe.transpose(B[tbank[t]][:, f * P:(f + 1) * P], hbuf[:, t, f * P:(f + 1) * P],
                                                ident[:, :])
                    last.then_inc(ht_psum, 1)

                def gate_up(R, g0, w, k):
                    for g in range(g0, g0 + 4):
                        use_piece(R, g, 2, w, project((0, 1), w, tiles))
                    if k is not None and tiles > 1:
                        pe.wait_ge(ht_low, k)
                    for g in range(g0 + 4, g0 + 8):
                        use_piece(R, g, 2, w, project((2, 3), w, tiles))

                for i in range(2 * tiles):
                    pe.matmul(B[4 + i][:, :], zrow[:, 0:P], zrow[:, :], start=True, stop=False,
                              skip_group_check=True)

                def first(R):
                    gate_up(R, 0, WIDE, None)
                    transpose_h(R.r - chunk_off + 1, WIDE)

                def chunk(R, w, wprev):
                    gate_up(R, 8, w, R.r - chunk_off + 1)
                    pe.wait_ge(ht_low, R.r - chunk_off + 1)
                    for g in range(16, 20):
                        use_piece(R, g, 2, WIDE, down_body(tiles, None))
                    transpose_h(R.r - chunk_off + 2, w)

                def tail(R, w):
                    pe.wait_ge(ht_low, R.r - chunk_off + 1)
                    for g in range(8, 12):
                        use_piece(R, g, w // 256, WIDE, down_body(tiles, w // P - 1))

                ffn_stretch(pe, first, chunk, tail, r0, chunks, half)

            pe.wait_ge(x_loaded, 16)
            for t in range(NT):
                transpose_tile(xs, t)

            with pe.Fori(0, DEPTH) as l:
                R = Rounds(pe, l * LAYER_ROUNDS)
                one, two, four, eight = (pe.snap(l * k) for k in (1, 2, 4, 8))
                pe.wait_ge(xt_low, l * 6 + 2)
                for g in range(0, 4):
                    use_piece(R, g, 2, WIDE, project((0, 1)))
                for g in range(4, 8):
                    use_piece(R, g, 2, WIDE, project((2, 3)))
                for g in range(8, 12):
                    use_piece(R, g, 2, WIDE, project_transposed)
                pe.wait_ge(q_copied, two + 2)
                for g in range(12, 16):
                    use_piece(R, g, 2, 2 * MH, project((0, 1), 2 * MH))
                pe.wait_ge(k_copied, two + 2)
                for g in range(16, 20):
                    use_piece(R, g, 2, WIDE, project((2, 3)))
                pe.wait_ge(roped, one + 1)
                pe.wait_ge(mqk_copied, four + 4)
                for j in range(8):
                    for t in range(NT):
                        last = pe.transpose(B[4 + j // 2][:, (j % 2) * SEQ + t * P:(j % 2) * SEQ + (t + 1) * P],
                                            qk[:, t, j * P:(j + 1) * P], ident[:, :])
                last.then_inc(qkt_psum, 1)
                pe.wait_ge(conv_silu, one + 1)
                pe.wait_ge(gates_in, one + 1)
                for j in range(2):
                    last = pe.transpose(B[1][:, j * P:(j + 1) * P], mqkt[:, 2 + j, 0:P], ident[:, :])
                last.then_inc(ktok_psum, 1)
                pe.wait_ge(logf_done, one + 1)
                for c in range(NT):
                    pe.matmul(B[0][:, 8 * c:8 * c + MH], tri[:, :], gtmp[:, 3, c, :], start=True, stop=True)
                    last = pe.matmul(B[0][:, 8 * c + MH:8 * c + 2 * MH], ones[:, :], gtmp[:, 3, c, :],
                                     start=True, stop=True)
                last.then_inc(cum_psum, 1)
                pe.wait_ge(cum_copied, one + 1)
                pe.wait_ge(ktok_copied, one + 1)

                def scores(h):
                    r = slice(AD * (h % 2), AD * (h % 2) + AD)
                    if h == 0:
                        pe.wait_ge(qt_copied, two + 2)
                        pe.wait_ge(kt_copied, two + 2)
                    else:
                        pe.wait_ge(masked, eight + h)
                    q, k = qkt[r, h // 2, :], qkt[r, 4 + h // 2, :]
                    pe.matmul(B[4][:, 0:P], q[:, 0:P], k[:, 0:P], start=True, stop=True)
                    pe.matmul(B[4][:, P:3 * P], q[:, P:2 * P], k, start=True, stop=True).then_inc(score_psum, 1)

                def transpose_probs(h):
                    pe.wait_ge(probs_done, eight + h + 1)
                    if h >= 1:
                        pe.wait_ge(probs_t, eight + h)
                    else:
                        pe.wait_ge(kt_copied, two + 2)
                    for j in range(3):
                        last = pe.transpose(B[6][:, j * P:(j + 1) * P], pm[:, h % 2, j * P:(j + 1) * P], ident[:, :])
                    last.then_inc(probs_t_psum, 1)

                def attend(h):
                    pe.wait_ge(probs_t, eight + h + 1)
                    if h == 0:
                        pe.wait_ge(v_copied, two + 2)
                    if h == 4:
                        pe.wait_ge(att_copied, two + 1)
                    o, cols = (h % 4) * AD, slice(h * AD, (h + 1) * AD)
                    pt = ptm[:, h % 2, :]
                    pe.matmul(B[7][:, o:o + AD], pt[:, 0:P], vv[:, 0, cols], start=True, stop=True)
                    pe.matmul(B[7][:, 4 * AD + o:5 * AD + o], pt[:, P:2 * P], vv[:, 0, cols], start=True, stop=False)
                    pe.matmul(B[7][:, 4 * AD + o:5 * AD + o], pt[:, 2 * P:3 * P], vv[:, 1, cols],
                              start=False, stop=True).then_inc(att_psum, 1)

                def diag_rows(c, ready, done):
                    pe.wait_ge(ready, two + c + 1)
                    pe.matmul(B[2 + c][:, :], ones[:, :], diag[:, c].rearrange("p h n -> p (h n)"),
                              start=True, stop=True).then_inc(done, 1)

                def kq():
                    pe.wait_ge(wlog, two + 2)
                    for c in range(NT):
                        for h in range(MH):
                            r, o = slice(MK * (h % 2), MK * (h % 2) + MK), (2 * c + h // 2) * P
                            last = pe.matmul(B[2 + h % 2][:, o:o + P], mqkt[r, 2 + h // 2, c * P:(c + 1) * P],
                                             mqkt[r, h // 2, c * P:(c + 1) * P], start=True, stop=True)
                    last.then_inc(kq_psum, 1)

                def carried_state():
                    pe.wait_ge(vw_done, one + 1)
                    for h in range(MH):
                        o = (h // 2) * (MV + 2)
                        last = pe.matmul(B[5][MK * (h % 2):MK * (h % 2) + MK, o:o + MV + 1],
                                         ktok[:, h * MK:(h + 1) * MK], vw[:, h, 0:MV + 1], start=True, stop=True)
                    last.then_inc(c_psum, 1)

                def numerators(c, bank):
                    pe.wait_ge(st_done, two + 2)
                    pe.wait_ge(mv_copied, two + 2)
                    for h in range(MH):
                        o = (h % 2) * (MV + 2)
                        last = pe.matmul(B[bank + h // 2][:, o:o + MV + 1], st[:, c, h, :], mv[:, c, h, 0:MV + 1],
                                         start=True, stop=True)
                    last.then_inc(num_psum, 1)

                for s in range(8):
                    if s == 4:
                        pe.wait_ge(mv_copied, two + 2)
                    use_piece(R, 20 + s, 2, WIDE, project((0, 1)))
                    scores(s)
                    if s >= 1:
                        transpose_probs(s - 1)
                    if s >= 2:
                        attend(s - 2)
                    if s == 1:
                        pe.wait_ge(v_copied, two + 2)
                        diag_rows(0, diag_a, arow_psum)
                        diag_rows(1, diag_a, arow_psum)
                    if s == 3:
                        pe.wait_ge(m_step, l * 6 + 6)
                        diag_rows(0, diag_m, mrow_psum)
                        diag_rows(1, diag_m, mrow_psum)
                    if s == 4:
                        kq()
                    if s == 6:
                        carried_state()
                    if s == 7:
                        numerators(0, 2)
                transpose_probs(7)
                attend(6)
                attend(7)
                pe.wait_ge(mo_exp, two + 2)
                numerators(1, 0)
                pe.wait_ge(c_copied, one + 1)
                pe.wait_ge(masked, eight + 8)
                for h in range(MH):
                    r, o = slice(MK * (h % 2), MK * (h % 2) + MK), (h // 2) * (MV + 2)
                    last = pe.matmul(B[4 + h % 2][:, o:o + MV + 1], mqkt[r, h // 2, P:2 * P], csb[r, h // 2, 0:MV + 1],
                                     start=True, stop=True)
                last.then_inc(inter_psum, 1)
                pe.wait_ge(tot_done, one + 1)
                pe.wait_ge(num0_copied, one + 1)
                for t in range(NT):
                    pe.wait_ge(mix_done, l * 5 + 3 + 2 * t)
                    transpose_tile(mix, t)
                pe.wait_ge(xt_low, l * 6 + 4)
                pe.wait_ge(att_copied, two + 2)
                for g in range(28, 32):
                    use_piece(R, g, 2, WIDE, project((4, 6)))
                for g in range(32, 36):
                    use_piece(R, g, 2, WIDE, project((5, 7)))
                for t in range(NT):
                    pe.wait_ge(ln_out, four + t + 1)
                    transpose_tile(xs, t)
                with pe.If(l < 1):
                    pe.wait_ge(xt_low, 6)
                    ffn_pe(MIX_ROUNDS, DENSE_FULL, True, NT, (2, 3), 3)
                    for t in range(NT):
                        pe.wait_ge(ln_out, NT + t + 1)
                        transpose_tile(xs, t)

            pe.wait_ge(xt_low, 12)
            pe.wait_ge(rw_low, 1)
            for t in range(NT):
                for k in range(KD):
                    last = mm3(B[t][:, 0:E], xth[:, k, t * P:(t + 1) * P], xtl[:, k, t * P:(t + 1) * P],
                               rwh[:, k, :], rwl[:, k, :], k == 0, k == KD - 1)
            last.then_inc(logits_psum, 1)
            pe.wait_ge(picks_ready, 1)
            pe.matmul(B[2][:, 0:E], trs[:, :], isel[:, 2, 0, :], start=True, stop=True)
            pe.matmul(B[2][:, E:2 * E], trs[:, :], isel[:, 2, 1, :], start=True, stop=False)
            pe.matmul(B[2][:, E:2 * E], ones[:, :], isel[:, 2, 0, :], start=False, stop=True)
            pe.matmul(B[2][:, 2 * E:3 * E], ones[:, :], isel[:, 2, 0, :], start=True, stop=False)
            pe.matmul(B[2][:, 2 * E:3 * E], ones[:, :], isel[:, 2, 1, :], start=False, stop=True).then_inc(pos_psum, 1)
            pe.wait_ge(table_ready, 1)
            passes = pe.value_load(tabi[0:1, MAX_PASSES:MAX_PASSES + 1], min_val=1, max_val=MAX_PASSES)
            pe.wait_ge(x_low, NT)
            with pe.Fori(0, passes) as p:
                pe.wait_ge(pick_done, p + 1)
                pe.wait_ge(accumulated, p + NT)
                for t in range(NT):
                    last = pe.transpose(B[6][:, t * P:(t + 1) * P], pick[:, t, :].bitcast(F32), ident[:, :])
                last.then_inc(pick_psum, 1)
                for part, src in enumerate((xh, xl)):
                    for k in range(KD):
                        for t in range(NT):
                            last = pe.matmul(B[2 * part + k // 4][:, (k % 4) * P:(k % 4 + 1) * P],
                                             src[:, t, k * P:(k + 1) * P], pick[:, t, :], start=t == 0, stop=t == NT - 1)
                last.then_inc(gathered, 1)
                pe.wait_ge(gath_high, p + 1)
                pe.wait_ge(gath_low, p + 1)
                ffn_pe(pe.snap(p * MOE_CHUNKS + MOE_BASE), MOE_CHUNKS, False, 1, (7,), MOE_BASE - DENSE_FULL - 1)
                pe.wait_ge(pick_copied, p + 1)
                pe.wait_ge(y_low, p * 2 + 2)
                for t in range(NT):
                    for n in range(2):
                        cols = slice(n * WIDE, (n + 1) * WIDE)
                        pe.matmul(B[2 * t + n][:, :], pickt[:, t * P:(t + 1) * P], yh[:, cols], start=True, stop=False)
                        last = pe.matmul(B[2 * t + n][:, :], pickt[:, t * P:(t + 1) * P], yl[:, cols],
                                         start=False, stop=True)
                last.then_inc(scattered, 1)


_INS = ["x", "positions", "w_in", "gate_bias", "conv_w", "conv_b", "norm_attn", "norm_mlstm", "w_out",
        "ln1_g", "ln1_b", "dense_w_gate", "dense_w_up", "dense_w_down", "router_w", "router_b",
        "moe_w_gate", "moe_w_up", "moe_w_down", "ln2_g", "ln2_b"]


def kernel(**inputs):
    import numpy as _np
    import concourse.bacc as _bacc
    from concourse import mybir as _mybir
    from concourse.bass_utils import run_bass_kernel_spmd as _run

    nc = _bacc.Bacc("TRN2", target_bir_lowering=False, num_devices=1)
    arrays, args = {}, []
    for name in _INS:
        a = _np.ascontiguousarray(inputs[name])
        arrays[f"in_{name}_dram"] = a
        args.append(nc.dram_tensor(f"in_{name}_dram", a.shape, _mybir.dt.from_np(a.dtype), kind="ExternalInput").ap())
    shape = inputs["x"].shape
    args.append(nc.dram_tensor("out_0_dram", shape, _mybir.dt.float32, kind="ExternalOutput").ap())
    hybrid_moe_program(nc, *args)
    r = _run(nc, [arrays], core_ids=[0])
    return r.results[0]["out_0_dram"]
```

```python
from contextlib import ExitStack

import concourse.bass as bass
from concourse import mybir

F32 = mybir.dt.float32
F32R = mybir.dt.float32r
BF16 = mybir.dt.bfloat16
I32 = mybir.dt.int32
ALU = mybir.AluOpType
ACT = mybir.ActivationFunctionType
AX_X = mybir.AxisListType.X

P = 128
TWO_PI = 6.283185307179586
PI_SAFE = 3.1415925
NEG = -1.0e30
LN_EPS = 1e-5
RMS_EPS = 1e-6
ROPE_THETA = 500000.0

RAW_UNITS = 3
PIECES = 4
SPLIT_SLOTS = 6
ROUND = RAW_UNITS * PIECES
WIDE = 512


def hybrid_moe_program(nc, x, positions, w_in, gate_bias, conv_w, conv_b, norm_attn, norm_mlstm, w_out,
                       ln1_g, ln1_b, dense_w_gate, dense_w_up, dense_w_down, router_w, router_b,
                       moe_w_gate, moe_w_up, moe_w_down, ln2_g, ln2_b, out):
    _, SEQ, D = x.shape
    DEPTH = w_in.shape[0]
    N_IN = w_in.shape[2]
    D_FF = dense_w_gate.shape[2]
    E, D_EXPERT = moe_w_gate.shape[1], moe_w_gate.shape[3]
    NT = SEQ // P
    KD = D // P
    AH, AD = 8, 64
    AW = AH * AD
    MH, MV, MK = 4, 128, 64
    ALPHA = (2.0 * DEPTH) ** 0.25
    HALF_ROPE = AD // 4 // 2
    MAX_PASSES = E + 3
    assert NT == 2 and DEPTH == 2 and N_IN == 3 * AW + 3 * WIDE + 2 * MH and KD == 8

    MIX_ROUNDS = 3
    DENSE_FULL = D_FF // WIDE
    DENSE_ROUNDS = DENSE_FULL + 1
    MOE_CHUNKS = D_EXPERT // WIDE
    LAYER_ROUNDS = MIX_ROUNDS + DENSE_ROUNDS
    MOE_BASE = LAYER_ROUNDS + MIX_ROUNDS
    assert D_FF - DENSE_FULL * WIDE == WIDE // 2

    xd = x.rearrange("a (t p) d -> p (a t) d", p=P)
    outd = out.rearrange("a (t p) d -> p (a t) d", p=P)

    with ExitStack() as ctx:
        def sb(name, shape, dt=F32, where=ctx):
            return where.enter_context(nc.sbuf_tensor(name, shape, dt))

        def sem(name):
            return ctx.enter_context(nc.semaphore(name))

        raw = sb("raw", [P, RAW_UNITS, 8 * WIDE])
        wh = sb("wh", [P, SPLIT_SLOTS, 2 * WIDE], F32R)
        wl = sb("wl", [P, SPLIT_SLOTS, 2 * WIDE], F32R)
        xs = sb("xs", [P, NT, D])
        xth = sb("xth", [P, KD, SEQ], F32R)
        xtl = sb("xtl", [P, KD, SEQ], F32R)
        lng = sb("lng", [P, D])
        lnb = sb("lnb", [P, D])
        ident = sb("ident", [P, P])
        ones = sb("ones", [P, P])
        tri = sb("tri", [P, P])
        trs = sb("trs", [P, P])
        mask3 = sb("mask3", [P, 3 * P])
        maskt = sb("maskt", [P, P])
        slot_no = sb("slot_no", [P, P])
        zrow = sb("zrow", [P, WIDE], BF16)
        eps = sb("eps", [P, 2])
        rw = sb("rw", [P, KD, E])
        rwh = sb("rwh", [P, KD, E], F32R)
        rwl = sb("rwl", [P, KD, E], F32R)
        rb = sb("rb", [P, E])
        stats = sb("stats", [P, NT, 2, 6])
        moments = sb("moments", [P, NT, 2])
        lnc = sb("lnc", [P, NT, 2])

        mix_mem = ctx.enter_context(ExitStack())
        qk = sb("qk", [P, NT, 2 * AW], F32, mix_mem)
        mix = qk
        qkt = sb("qkt", [P, 8, SEQ], F32, mix_mem)
        posi = sb("posi", [P, NT], I32, mix_mem)
        posf = sb("posf", [P, NT], F32, mix_mem)
        invf = sb("invf", [P, HALF_ROPE], F32, mix_mem)
        ang = sb("ang", [P, 2, NT, HALF_ROPE], F32, mix_mem)
        turn = sb("turn", [P, 2, NT, HALF_ROPE], F32, mix_mem)
        turni = sb("turni", [P, 2, NT, HALF_ROPE], I32, mix_mem)
        sc8 = sb("sc8", [P, 2, NT, HALF_ROPE], F32, mix_mem)
        sincos = sb("sincos", [P, 2, NT, 2 * AH, HALF_ROPE], F32, mix_mem)
        gbias = sb("gbias", [P, 2 * MH], F32, mix_mem)
        cw = sb("cw", [P, 4, 4], F32, mix_mem)
        cb = sb("cb", [P, 4], F32, mix_mem)
        gna = sb("gna", [P, AW], F32, mix_mem)
        gnm = sb("gnm", [P, MH * MV], F32, mix_mem)
        vv = sb("vv", [P, NT, AW], F32, mix_mem)
        mpre = sb("mpre", [P, 4, 3 + SEQ], F32, mix_mem)
        cacc = sb("cacc", [P, 4, SEQ], F32, mix_mem)
        mqkt = sb("mqkt", [P, 4, SEQ], F32, mix_mem)
        ktok = sb("ktok", [P, MH * MK], F32, mix_mem)
        mv = sb("mv", [P, NT, MH, MV + 2], F32, mix_mem)
        mo = sb("mo", [P, NT, MH * MV], F32, mix_mem)
        sm = sb("sm", [P, 2, 3 * P], F32, mix_mem)
        pm = sb("pm", [P, 2, 3 * P], F32, mix_mem)
        ptm = sb("ptm", [P, 2, 3 * P], F32, mix_mem)
        smax = sb("smax", [P, AH, NT], F32, mix_mem)
        snb = sb("snb", [P, AH, NT], F32, mix_mem)
        norms = sb("norms", [P, 5, 24], F32, mix_mem)
        rsum = sb("rsum", [P, NT, AH], F32, mix_mem)
        araw = cacc[:, :, :].rearrange("p c n -> p (c n)").rearrange("p (t h d) -> p t h d", t=NT, h=AH)
        gates = sb("gates", [P, NT, 2 * MH], F32, mix_mem)
        gtmp = sb("gtmp", [P, 4, NT, MH], F32, mix_mem)
        bl = sb("bl", [P, NT, 2 * MH], F32, mix_mem)
        aa = sb("aa", [P, NT, MH], F32, mix_mem)
        diag = sb("diag", [P, NT, MH, P], F32, mix_mem)
        wtmp = sb("wtmp", [P, NT, MH, P], F32, mix_mem)
        st = diag
        wflat = wtmp[:, :, :, :].rearrange("p c h n -> p (c h n)")
        rt = wflat.rearrange("p (i t h j) -> p i t h j", i=4, t=NT, h=2 * AH)
        itmp = wflat[:, 0:MH * (MV + 2)].rearrange("p (h v) -> p h v", h=MH)
        mxs = sb("mxs", [P, 6, MH], F32, mix_mem)
        ein = sb("ein", [P, 4, MH], F32, mix_mem)
        eout = sb("eout", [P, 4, MH], F32, mix_mem)
        vw = sb("vw", [P, MH, MV + 2], F32, mix_mem)
        csb = sb("csb", [P, 2, MV + 2], F32, mix_mem)
        tot = sb("tot", [P, NT, MH, MV + 2], F32, mix_mem)
        mix_mem.close()
        hbuf = sb("hbuf", [P, NT, WIDE])
        hth = sb("hth", [P, 4, SEQ], F32R)
        htl = sb("htl", [P, 4, SEQ], F32R)
        xh = sb("xh", [P, NT, D], F32R)
        xl = sb("xl", [P, NT, D], F32R)
        yh = sb("yh", [P, D], F32R)
        yl = sb("yl", [P, D], F32R)
        pick = sb("pick", [P, NT, P], F32R)
        pickt = sb("pickt", [P, SEQ], F32R)
        lg = sb("lg", [P, NT, E])
        cmp4 = sb("cmp4", [P, 3, NT, E, E])
        rank = sb("rank", [P, NT, E])
        isel = sb("isel", [P, 3, NT, E])
        topv = sb("topv", [P, 6, NT])
        comb = sb("comb", [P, NT, E])
        posc = sb("posc", [P, 3, E])
        blk = sb("blk", [P, 5, E])
        pt11 = sb("pt11", [P, 5, MAX_PASSES, E])
        slotpos = sb("slotpos", [P, NT, MAX_PASSES + 1])
        cbp = sb("cbp", [P, NT, MAX_PASSES + 1])
        tabf = sb("tabf", [P, MAX_PASSES + 1])
        tabi = sb("tabi", [P, MAX_PASSES + 1], I32)
        low8 = sb("low8", [P, E, E])
        pass_no = sb("pass_no", [P, MAX_PASSES])
        expert_no = sb("expert_no", [P, E])

        B = [ctx.enter_context(nc.psum_tensor(f"B{i}", [P, WIDE], F32)) for i in range(8)]

        raw_full = [sem(f"raw_full{i}") for i in range(RAW_UNITS)]
        rounded = sem("rounded")
        split = sem("split")
        piece_used = sem("piece_used")
        x_loaded = [sem(f"x_loaded{t}") for t in range(NT)]
        const_ready, rope_in = sem("const_ready"), sem("rope_in")
        const_step = sem("const_step")
        mixp_loaded, ln_loaded, router_loaded = sem("mixp_loaded"), sem("ln_loaded"), sem("router_loaded")
        dve_init = sem("dve_init")
        rope_step, sin_in, sin_done, rope_table = sem("rope_step"), sem("sin_in"), sem("sin_done"), sem("rope_table")
        xt_psum, xt_high, xt_low = sem("xt_psum"), sem("xt_high"), sem("xt_low")
        q_copied, k_copied, v_copied = sem("q_copied"), sem("k_copied"), sem("v_copied")
        mqk_copied, roped, rot_step = sem("mqk_copied"), sem("roped"), sem("rot_step")
        conv_step, conv_done, conv_silu = sem("conv_step"), sem("conv_done"), sem("conv_silu")
        gates_in, absf, exp_f, ln_f, logf_done = sem("gates_in"), sem("absf"), sem("exp_f"), sem("ln_f"), sem("logf_done")
        cum_psum, cum_copied, a_done, ktok_psum, ktok_copied = (
            sem("cum_psum"), sem("cum_copied"), sem("a_done"), sem("ktok_psum"), sem("ktok_copied"))
        qkt_psum, qt_copied, kt_copied = sem("qkt_psum"), sem("qt_copied"), sem("kt_copied")
        score_psum, masked, row_max, score_ready = sem("score_psum"), sem("masked"), sem("row_max"), sem("score_ready")
        probs_done, probs_t_psum, probs_t, att_psum, att_copied = (
            sem("probs_done"), sem("probs_t_psum"), sem("probs_t"), sem("att_psum"), sem("att_copied"))
        diag_a, arow_psum, amask_step, m_step, diag_m, mrow_psum = (
            sem("diag_a"), sem("arow_psum"), sem("amask_step"), sem("m_step"), sem("diag_m"), sem("mrow_psum"))
        exp_small, wlog, wexp, kq_psum, st_done = (
            sem("exp_small"), sem("wlog"), sem("wexp"), sem("kq_psum"), sem("st_done"))
        mv_copied, mo_exp, vw_done, c_psum, c_copied = (
            sem("mv_copied"), sem("mo_exp"), sem("vw_done"), sem("c_psum"), sem("c_copied"))
        num_psum, num0_copied, inter_psum, inter_scaled, tot_done = (
            sem("num_psum"), sem("num0_copied"), sem("inter_psum"), sem("inter_scaled"), sem("tot_done"))
        mo_gate, squares, norm_step, mean_sq, std_done, mix_done = (
            sem("mo_gate"), sem("squares"), sem("norm_step"), sem("mean_sq"), sem("std_done"), sem("mix_done"))
        residual = sem("residual")
        ln_step, ln_var, ln_std, ln_out = sem("ln_step"), sem("ln_var"), sem("ln_std"), sem("ln_out")
        silu_done, h_done, ht_psum, ht_high, ht_low, ffn_added = (
            sem("silu_done"), sem("h_done"), sem("ht_psum"), sem("ht_high"), sem("ht_low"), sem("ffn_added"))
        rw_high, rw_low, logits_psum, route_step, picks_ready, pos_psum, table_ready = (
            sem("rw_high"), sem("rw_low"), sem("logits_psum"), sem("route_step"), sem("picks_ready"),
            sem("pos_psum"), sem("table_ready"))
        x_high, x_low = sem("x_high"), sem("x_low")
        pick_done, pick_psum, pick_copied, gathered, gath_high, gath_low = (
            sem("pick_done"), sem("pick_psum"), sem("pick_copied"), sem("gathered"), sem("gath_high"), sem("gath_low"))
        y_high, y_low, scattered, accumulated = (
            sem("y_high"), sem("y_low"), sem("scattered"), sem("accumulated"))
        stored = sem("stored")

        block = ctx.enter_context(nc.Block())

        class Rounds:

            def __init__(self, eng, r):
                fixed = isinstance(r, int)
                self.r = r if fixed else eng.snap(r)
                self.pieces = r * ROUND if fixed else eng.snap(self.r * ROUND)
                self.loads = r * 16 if fixed else eng.snap(self.r * 16)

        def piece_slot(g):
            return g % SPLIT_SLOTS

        def unit_of(g):
            return g // PIECES

        def ffn_stretch(eng, first, chunk, tail, r0, chunks, half):
            first(Rounds(eng, r0))
            with eng.Fori(0, chunks - 1) as c:
                chunk(Rounds(eng, c + r0), WIDE, WIDE)
            if half:
                chunk(Rounds(eng, r0 + chunks - 1), WIDE // 2, WIDE)
                tail(Rounds(eng, r0 + chunks), WIDE // 2)
            else:
                tail(Rounds(eng, r0 + chunks - 1), WIDE)

        @block.sync
        def _(sp):
            def load(R, j, dst, src):
                sp.wait_ge(split, R.pieces + PIECES * j + PIECES)
                sp.dma_start(dst, src).then_inc(raw_full[j % RAW_UNITS], 16)

            def slices(j, width, n=8):
                return raw[:, j % RAW_UNITS, 0:n * width].rearrange("p (k n) -> p k n", k=n)

            def columns(w2d, c0, width):
                return w2d.rearrange("(k p) n -> p k n", p=P)[:, :, c0:c0 + width]

            def load_columns(R, j, w2d, c0, width):
                load(R, j, slices(j, width), columns(w2d, c0, width))

            def load_rows(R, j, w2d, r0, n):
                load(R, j, raw[:, j % RAW_UNITS, 0:n * D].rearrange("p (k n) -> p k n", k=n), w2d(r0, n))

            for t in range(NT):
                sp.dma_start(xs[:, t, :], xd[:, t, :]).then_inc(x_loaded[t], 16)
            with sp.Fori(0, DEPTH) as l:
                R = Rounds(sp, l * LAYER_ROUNDS)
                wi = w_in[bass.ds(l, 1), :, :].rearrange("a (k p) n -> p (a k) n", p=P)
                wo = w_out[bass.ds(l, 1), :, :].rearrange("a (k p) n -> p (a k) n", p=P)
                order = [(0, WIDE), (AW, WIDE), (3 * AW, WIDE), (3 * AW + 3 * WIDE, 2 * MH),
                         (2 * AW, WIDE), (3 * AW + WIDE, WIDE), (3 * AW + 2 * WIDE, WIDE)]
                for j, (c0, width) in enumerate(order):
                    load(R, j, slices(j, width), wi[:, :, c0:c0 + width])
                for n in range(2):
                    load(R, 7 + n, slices(7 + n, WIDE), wo[:, :, n * WIDE:(n + 1) * WIDE])
                with sp.If(l < 1):
                    def down_rows(r0, n):
                        return dense_w_down[0, r0:r0 + n * P, :].rearrange("(k p) n -> p k n", p=P)

                    R = Rounds(sp, MIX_ROUNDS)
                    load_columns(R, 0, dense_w_gate[0], 0, WIDE)
                    load_columns(R, 1, dense_w_up[0], 0, WIDE)
                    with sp.Fori(0, DENSE_FULL - 1) as c:
                        R = Rounds(sp, c + MIX_ROUNDS)
                        cols = bass.ds(c * WIDE + WIDE, WIDE)
                        load(R, 2, slices(2, WIDE), dense_w_gate[0, :, cols].rearrange("(k p) n -> p k n", p=P))
                        load(R, 3, slices(3, WIDE), dense_w_up[0, :, cols].rearrange("(k p) n -> p k n", p=P))
                        load(R, 4, raw[:, 4 % RAW_UNITS, 0:4 * D].rearrange("p (k n) -> p k n", k=4),
                             dense_w_down[0, bass.ds(c * WIDE, WIDE), :].rearrange("(k p) n -> p k n", p=P))
                    R = Rounds(sp, MIX_ROUNDS + DENSE_FULL - 1)
                    load_columns(R, 2, dense_w_gate[0], DENSE_FULL * WIDE, WIDE // 2)
                    load_columns(R, 3, dense_w_up[0], DENSE_FULL * WIDE, WIDE // 2)
                    load_rows(R, 4, down_rows, (DENSE_FULL - 1) * WIDE, 4)
                    load_rows(Rounds(sp, MIX_ROUNDS + DENSE_FULL), 2, down_rows, DENSE_FULL * WIDE, 2)

            R = Rounds(sp, MOE_BASE)
            load_columns(R, 0, moe_w_gate[0, 0], 0, WIDE)
            load_columns(R, 1, moe_w_up[0, 0], 0, WIDE)
            sp.wait_ge(table_ready, 1)
            passes = sp.value_load(tabi[0:1, MAX_PASSES:MAX_PASSES + 1], min_val=1, max_val=MAX_PASSES)
            with sp.Fori(0, passes) as p:
                e = sp.value_load(tabi[0:1, bass.ds(p, 1)], min_val=0, max_val=E - 1)

                def expert_columns(w, which, cols):
                    return w[0, bass.ds(which, 1), :, cols].rearrange("a (k p) n -> p (a k) n", p=P)

                def expert_rows(rows):
                    return moe_w_down[0, bass.ds(e, 1), rows, :].rearrange("a (k p) n -> p (a k) n", p=P)

                r0 = sp.snap(p * MOE_CHUNKS + MOE_BASE)
                with sp.Fori(0, MOE_CHUNKS - 1) as c:
                    R = Rounds(sp, c + r0)
                    cols = bass.ds(c * WIDE + WIDE, WIDE)
                    load(R, 2, slices(2, WIDE), expert_columns(moe_w_gate, e, cols))
                    load(R, 3, slices(3, WIDE), expert_columns(moe_w_up, e, cols))
                    load(R, 4, raw[:, 4 % RAW_UNITS, 0:4 * D].rearrange("p (k n) -> p k n", k=4),
                         expert_rows(bass.ds(c * WIDE, WIDE)))
                R = Rounds(sp, r0 + (MOE_CHUNKS - 1))
                load(R, 2, raw[:, 2, 0:4 * D].rearrange("p (k n) -> p k n", k=4),
                     expert_rows(slice((MOE_CHUNKS - 1) * WIDE, MOE_CHUNKS * WIDE)))
                with sp.If(p + 1 < passes):
                    after = sp.value_load(tabi[0:1, bass.ds(p + 1, 1)], min_val=0, max_val=E - 1)
                    R = Rounds(sp, r0 + MOE_CHUNKS)
                    load(R, 0, slices(0, WIDE), expert_columns(moe_w_gate, after, slice(0, WIDE)))
                    load(R, 1, slices(1, WIDE), expert_columns(moe_w_up, after, slice(0, WIDE)))

            for t in range(NT):
                sp.wait_ge(ln_out, 2 * NT * (DEPTH - 1) + NT + t + 1)
                sp.dma_start(outd[:, t, :], xs[:, t, :]).then_inc(stored, 16)
            sp.wait_ge(stored, 16 * NT)

        @block.gpsimd
        def _(pool):

            pool.memset(zrow[:, :], 0.0)
            pool.memset(eps[:, 0:1], LN_EPS)
            pool.memset(eps[:, 1:2], RMS_EPS)
            pool.memset(ident[:, :], 0.0)
            pool.memset(tri[:, :], 1.0)
            pool.memset(trs[:, :], 1.0)
            pool.memset(mask3[:, :], 0.0)
            pool.memset(maskt[:, :], 0.0)
            pool.memset(ones[:, :], 1.0).then_inc(const_step, 1)
            pool.iota(slot_no[:, :], pattern=[[1, P]], base=0, channel_multiplier=0,
                      allow_small_or_imprecise_dtypes=True)
            pool.wait_ge(const_step, 1)
            pool.affine_select(out=ident[:, :], in_=ident[:, :], compare_op=ALU.not_equal, fill=1.0,
                               base=0, pattern=[[-1, P]], channel_multiplier=1)
            pool.affine_select(out=tri[:, :], in_=tri[:, :], compare_op=ALU.is_ge, fill=0.0,
                               base=0, pattern=[[1, P]], channel_multiplier=-1)
            pool.affine_select(out=trs[:, :], in_=trs[:, :], compare_op=ALU.is_ge, fill=0.0,
                               base=-1, pattern=[[1, P]], channel_multiplier=-1)
            pool.affine_select(out=maskt[:, :], in_=maskt[:, :], compare_op=ALU.is_ge, fill=NEG,
                               base=0, pattern=[[1, P]], channel_multiplier=-1)
            pool.affine_select(out=mask3[:, 0:P], in_=mask3[:, 0:P], compare_op=ALU.is_ge, fill=NEG,
                               base=0, pattern=[[-1, P]], channel_multiplier=1)
            pool.affine_select(out=mask3[:, 2 * P:3 * P], in_=mask3[:, 2 * P:3 * P], compare_op=ALU.is_ge,
                               fill=NEG, base=0, pattern=[[-1, P]], channel_multiplier=1).then_inc(const_ready, 1)
            with nc.allow_non_contiguous_dma(reason="small parameters"):
                pool.dma_start(rw[:, :, :], router_w[0].rearrange("(k p) e -> p k e", p=P)).then_inc(router_loaded, 16)
                pool.dma_start(rb[:, :], router_b.broadcast_to((P, E))).then_inc(router_loaded, 16)

            def load_ln(g, b, done):
                if done is not None:
                    pool.wait_ge(ln_out, done)
                pool.dma_start(lng[:, :], g.broadcast_to((P, D))).then_inc(ln_loaded, 16)
                pool.dma_start(lnb[:, :], b.broadcast_to((P, D))).then_inc(ln_loaded, 16)

            load_ln(ln1_g[0:1, :], ln1_b[0:1, :], None)
            with pool.Fori(0, DEPTH) as l:
                row = bass.ds(l, 1)
                pool.wait_ge(dve_init, 2 + l)
                with nc.allow_non_contiguous_dma(reason="small parameters"):
                    for j in range(4):
                        pool.dma_start(cw[:, :, j], conv_w[row, j, :].rearrange("a (c p) -> p (a c)", p=P))\
                            .then_inc(mixp_loaded, 16)
                    pool.dma_start(cb[:, :], conv_b[row, :].rearrange("a (c p) -> p (a c)", p=P)).then_inc(mixp_loaded, 16)
                    pool.dma_start(gbias[:, :], gate_bias[row, :].broadcast_to((P, 2 * MH))).then_inc(mixp_loaded, 16)
                    pool.dma_start(gna[:, :], norm_attn[row, :].broadcast_to((P, AW))).then_inc(mixp_loaded, 16)
                    pool.dma_start(gnm[:, :], norm_mlstm[row, :].broadcast_to((P, MH * MV))).then_inc(mixp_loaded, 16)

                pool.wait_ge(a_done, l + 1)
                for c in range(NT):
                    pool.tensor_tensor(diag[:, c], ident[:, :].unsqueeze(1).broadcast_to((P, MH, P)),
                                       aa[:, c, :].unsqueeze(2).broadcast_to((P, MH, P)), ALU.mult).then_inc(diag_a, 1)
                pool.wait_ge(m_step, l * 6 + 6)
                pool.wait_ge(arow_psum, l * 2 + 2)
                for c in range(NT):
                    pool.tensor_tensor(diag[:, c], ident[:, :].unsqueeze(1).broadcast_to((P, MH, P)),
                                       mxs[:, 4 + c, :].unsqueeze(2).broadcast_to((P, MH, P)), ALU.mult)\
                        .then_inc(diag_m, 1)
                pool.wait_ge(mixp_loaded, l * 128 + 128)
                pool.wait_ge(ln_loaded, l * 64 + 32)
                pool.wait_ge(exp_small, l + 1)
                pool.wait_ge(mv_copied, l * 2 + 1)
                pool.tensor_tensor(vw[:, :, 0:MV + 1], mv[:, 0, :, 0:MV + 1],
                                   eout[:, 0, :].unsqueeze(2).broadcast_to((P, MH, MV + 1)), ALU.mult)\
                    .then_inc(vw_done, 1)
                with pool.If(l < 1):
                    load_ln(ln2_g[0:1, :], ln2_b[0:1, :], NT)
                    pool.wait_ge(ln_loaded, 64)
                    load_ln(ln1_g[1:2, :], ln1_b[1:2, :], 2 * NT)
            load_ln(ln2_g[1:2, :], ln2_b[1:2, :], 3 * NT)
            pool.memset(low8[:, :, :], 1.0).then_inc(const_step, 1)
            pool.iota(pass_no[:, :], pattern=[[1, MAX_PASSES]], base=0, channel_multiplier=0,
                      allow_small_or_imprecise_dtypes=True)
            pool.iota(expert_no[:, :], pattern=[[1, E]], base=0, channel_multiplier=0,
                      allow_small_or_imprecise_dtypes=True)
            pool.wait_ge(const_step, 2)
            pool.affine_select(out=low8[:, :, :], in_=low8[:, :, :], compare_op=ALU.is_gt, fill=0.0,
                               base=0, pattern=[[1, E], [-1, E]], channel_multiplier=0).then_inc(const_ready, 1)
            pool.wait_ge(mixp_loaded, 16 * 8 * DEPTH)
            pool.wait_ge(ln_loaded, 16 * 2 * 2 * DEPTH)
            pool.wait_ge(router_loaded, 32)

        @block.scalar
        def _(act):
            def round_piece(R, g, n):
                if g % PIECES == 0:
                    act.wait_ge(raw_full[unit_of(g) % RAW_UNITS], R.loads + 16 * (unit_of(g) // RAW_UNITS) + 16)
                act.wait_ge(piece_used, R.pieces + g + 1)
                src = raw[:, unit_of(g) % RAW_UNITS, (g % PIECES) * n:(g % PIECES + 1) * n]
                act.activation(wh[:, piece_slot(g), 0:n], src, ACT.Copy).then_inc(rounded, 1)

            def pe_done(R, g):
                act.wait_ge(piece_used, R.pieces + SPLIT_SLOTS + g + 1)

            def transposed_high(base, t):
                for b in range(2):
                    act.wait_ge(xt_psum, base + 2 * t + b + 1)
                    act.activation(xth[:, 4 * b:4 * b + 4, t * P:(t + 1) * P],
                                   B[2 * t + b][:, :].rearrange("p (k n) -> p k n", k=4), ACT.Copy)\
                        .then_inc(xt_high, 1)

            def layer_norm_act(base):
                for t in range(NT):
                    act.wait_ge(ln_var, base + t + 1)
                    act.activation(lnc[:, t, 0:1], moments[:, t, 1:2], ACT.Sqrt, bias=eps[:, 0:1]).then_inc(ln_std, 1)

            def ffn_act(r0, chunks, half, tiles, tbank, chunk_off, ahead=0, before_down=None, during_down=None):
                def n_chunk(R):
                    return R.r - chunk_off

                def ht_high_parts(R, k, w):
                    act.wait_ge(ht_psum, k)
                    for t in range(tiles):
                        last = act.activation(hth[:, 0:w // P, t * P:(t + 1) * P],
                                              B[tbank[t]][:, 0:w].rearrange("p (f n) -> p f n", n=P), ACT.Copy)
                    last.then_inc(ht_high, 1)

                def silu(R, g, w):
                    pe_done(R, g)
                    for t in range(tiles):
                        last = act.activation(hbuf[:, t, 0:w], B[t][:, 0:w], ACT.Silu)
                    last.then_inc(silu_done, 1)

                def first(R):
                    for g in range(ahead, 8):
                        round_piece(R, g, 2 * WIDE)
                        if g == 7:
                            silu(R, 3, WIDE)

                def chunk(R, w, wprev):
                    for g in range(8, 20):
                        round_piece(R, g, (2 * w if g < 16 else 2 * WIDE))
                        if g == 11:
                            ht_high_parts(R, n_chunk(R) + 1, wprev)
                        if g == 17:
                            silu(R, 11, w)

                def tail(R, w):
                    if before_down:
                        before_down()
                    for g in range(8, 12):
                        round_piece(R, g, 2 * w)
                        if g == 9:
                            ht_high_parts(R, n_chunk(R) + 1, w)
                    if during_down:
                        during_down()

                ffn_stretch(act, first, chunk, tail, r0, chunks, half)

            with nc.allow_non_contiguous_dma(reason="one position per partition"):
                act.dma_start(posi[:, :], positions.rearrange("a (t p) -> p (a t)", p=P)).then_inc(rope_in, 16)
            act.wait_ge(sin_in, 1)
            act.activation(sc8[:, :, :, :], ang[:, :, :, :], ACT.Sin).then_inc(sin_done, 1)
            for t in range(NT):
                transposed_high(0, t)

            with act.Fori(0, DEPTH) as l:
                R = Rounds(act, l * LAYER_ROUNDS)
                one, two, eight = act.snap(l * 1), act.snap(l * 2), act.snap(l * 8)
                FULL = 2 * WIDE
                for g in range(8):
                    round_piece(R, g, FULL)
                pe_done(R, 3)
                for t in range(NT):
                    act.activation(qk[:, t, 0:AW], B[t][:, :], ACT.Copy).then_inc(q_copied, 1)
                for g in range(8, 12):
                    round_piece(R, g, FULL)
                pe_done(R, 7)
                for t in range(NT):
                    act.activation(qk[:, t, AW:2 * AW], B[2 + t][:, :], ACT.Copy).then_inc(k_copied, 1)
                for g in range(12, 16):
                    round_piece(R, g, 2 * 2 * MH)
                round_piece(R, 16, FULL)
                round_piece(R, 17, FULL)
                pe_done(R, 11)
                act.wait_ge(dve_init, 1)
                for ct in range(4):
                    act.activation(mpre[:, ct, 3:3 + SEQ], B[4 + ct][:, 0:SEQ], ACT.Copy).then_inc(mqk_copied, 1)
                round_piece(R, 18, FULL)
                round_piece(R, 19, FULL)
                act.wait_ge(conv_done, one + 1)
                act.activation(mqkt[:, :, :], cacc[:, :, :], ACT.Silu).then_inc(conv_silu, 1)
                act.wait_ge(absf, one + 1)
                act.activation(gtmp[:, 1], gtmp[:, 0], ACT.Exp).then_inc(exp_f, 1)
                act.wait_ge(exp_f, one + 1)
                act.activation(gtmp[:, 2], gtmp[:, 1], ACT.Ln, bias=ones[:, 0:1]).then_inc(ln_f, 1)
                round_piece(R, 20, FULL)
                round_piece(R, 21, FULL)
                pe_done(R, 19)
                for t in range(NT):
                    act.activation(vv[:, t, :], B[2 + t][:, :], ACT.Copy).then_inc(v_copied, 1)
                act.wait_ge(ktok_psum, one + 1)
                act.activation(ktok[:, :], B[1][:, 0:MH * MK], ACT.Copy).then_inc(ktok_copied, 1)
                act.wait_ge(qkt_psum, one + 1)
                for b in range(2):
                    act.activation(qkt[:, 2 * b:2 * b + 2, :], B[4 + b][:, :].rearrange("p (j n) -> p j n", j=2),
                                   ACT.Copy).then_inc(qt_copied, 1)

                def probs(h):
                    act.wait_ge(score_ready, eight + h + 1)
                    if h >= 2:
                        act.wait_ge(probs_t_psum, eight + h - 1)
                    else:
                        act.wait_ge(dve_init, 1)
                    act.activation(pm[:, h % 2, 0:P], sm[:, h % 2, 0:P], ACT.Exp, bias=snb[:, h, 0:1],
                                   scale=AD ** -0.5, accum_out=rsum[:, 0, h:h + 1])
                    act.activation(pm[:, h % 2, P:3 * P], sm[:, h % 2, P:3 * P], ACT.Exp, bias=snb[:, h, 1:2],
                                   scale=AD ** -0.5, accum_out=rsum[:, 1, h:h + 1]).then_inc(probs_done, 1)

                def probs_transposed(h):
                    act.wait_ge(probs_t_psum, eight + h + 1)
                    if h >= 2:
                        act.wait_ge(att_psum, eight + h - 1)
                    act.activation(ptm[:, h % 2, :], B[6][:, 0:3 * P], ACT.Copy).then_inc(probs_t, 1)

                def copy_attention(half):
                    act.wait_ge(att_psum, eight + 4 * half + 4)
                    act.activation(araw[:, :, 4 * half:4 * half + 4, :],
                                   B[7][:, :].rearrange("p (t h d) -> p t h d", t=NT, h=4), ACT.Copy)\
                        .then_inc(att_copied, 1)

                def state_weights(c):
                    act.wait_ge(wlog, two + c + 1)
                    for h in range(MH):
                        last = act.activation(wtmp[:, c, h, :], wtmp[:, c, h, :], ACT.Exp, bias=aa[:, c, h:h + 1])
                    last.then_inc(wexp, 1)

                for s in range(8):
                    round_piece(R, 22 + s, FULL)
                    if s == 4:
                        pe_done(R, 23)
                        act.wait_ge(dve_init, 1)
                        for t in range(NT):
                            act.activation(mv[:, t, :, 0:MV], B[t][:, :].rearrange("p (h v) -> p h v", h=MH),
                                           ACT.Copy).then_inc(mv_copied, 1)
                    probs(s)
                    if s >= 1:
                        probs_transposed(s - 1)
                    if s == 3:
                        act.wait_ge(m_step, l * 6 + 6)
                        act.activation(eout[:, :, :], ein[:, :, :], ACT.Exp).then_inc(exp_small, 1)
                    if s == 4:
                        state_weights(0)
                    if s == 5:
                        state_weights(1)
                        copy_attention(0)
                    if s == 7:
                        act.wait_ge(c_psum, one + 1)
                        act.activation(csb[:, :, 0:MV + 1],
                                       B[5][:, 0:2 * (MV + 2)].rearrange("p (j v) -> p j v", j=2)[:, :, 0:MV + 1],
                                       ACT.Copy).then_inc(c_copied, 1)
                round_piece(R, 30, FULL)
                pe_done(R, 27)
                for t in range(NT):
                    act.activation(mo[:, t, :], B[t][:, :], ACT.Exp, scale=-1.0).then_inc(mo_exp, 1)
                probs_transposed(7)
                act.wait_ge(num_psum, two + 1)
                for b in range(2):
                    last = act.activation(tot[:, 0, 2 * b:2 * b + 2, 0:MV + 1],
                                          B[2 + b][:, 0:2 * (MV + 2)].rearrange("p (j v) -> p j v", j=2)[:, :, 0:MV + 1],
                                          ACT.Copy)
                last.then_inc(num0_copied, 1)
                round_piece(R, 31, FULL)
                copy_attention(1)
                act.wait_ge(inter_psum, one + 1)
                act.wait_ge(norm_step, l * 9 + 1)
                for h in range(MH):
                    last = act.activation(itmp[:, h, 0:MV + 1],
                                          B[4 + h % 2][:, (h // 2) * (MV + 2):(h // 2) * (MV + 2) + MV + 1],
                                          ACT.Copy, scale=ein[:, 1, h:h + 1])
                last.then_inc(inter_scaled, 1)
                act.wait_ge(att_copied, two + 2)
                act.activation(mix[:, :, 0:AW], araw[:, :, :, :].rearrange("p t h d -> p t (h d)"),
                               ACT.Square).then_inc(squares, 1)
                act.wait_ge(tot_done, one + 1)
                act.wait_ge(num0_copied, one + 1)
                for c in range(NT):
                    last = act.activation(mix[:, c, AW:D].rearrange("p (h v) -> p h v", h=MH), tot[:, c, :, 0:MV],
                                          ACT.Square)
                last.then_inc(squares, 1)
                round_piece(R, 32, FULL)
                round_piece(R, 33, FULL)
                act.wait_ge(mean_sq, one + 1)
                act.activation(norms[:, 3, :], norms[:, 2, :], ACT.Sqrt, bias=eps[:, 1:2]).then_inc(std_done, 1)
                xt0 = act.snap(l * 12)
                for t in range(NT):
                    transposed_high(xt0 + 4, t)
                round_piece(R, 34, FULL)
                round_piece(R, 35, FULL)
                layer_norm_act(act.snap(l * 4))
                for t in range(NT):
                    transposed_high(xt0 + 8, t)
                with act.If(l < 1):
                    ffn_act(MIX_ROUNDS, DENSE_FULL, True, NT, (2, 3), 3)
                    layer_norm_act(2)
                    for t in range(NT):
                        transposed_high(12, t)

            act.wait_ge(router_loaded, 32)
            act.activation(rwh[:, :, :], rw[:, :, :], ACT.Copy).then_inc(rw_high, 1)
            act.wait_ge(ln_out, 3 * NT)
            for t in range(NT):
                act.activation(xh[:, t, :], xs[:, t, :], ACT.Copy).then_inc(x_high, 1)
            act.wait_ge(route_step, 8)
            act.activation(topv[:, 3, :], topv[:, 2, :], ACT.Exp).then_inc(exp_f, 1)
            for g in range(PIECES):
                round_piece(Rounds(act, MOE_BASE), g, 2 * WIDE)

            def gathered_high(p):
                act.wait_ge(gathered, p + 1)
                for b in range(2):
                    last = act.activation(xth[:, 4 * b:4 * b + 4, 0:P], B[b][:, :].rearrange("p (k n) -> p k n", k=4),
                                          ACT.Copy)
                last.then_inc(gath_high, 1)

            gathered_high(0)
            act.wait_ge(table_ready, 1)
            passes = act.value_load(tabi[0:1, MAX_PASSES:MAX_PASSES + 1], min_val=1, max_val=MAX_PASSES)
            with act.Fori(0, passes) as p:
                after = act.snap(p + 1)

                def copy_pick():
                    act.wait_ge(pick_psum, p + 1)
                    act.wait_ge(scattered, p * NT + 1)
                    act.activation(pickt[:, :], B[6][:, 0:SEQ], ACT.Copy).then_inc(pick_copied, 1)

                def next_pass():
                    with act.If(after < passes):
                        gathered_high(after)
                        R = Rounds(act, p * MOE_CHUNKS + (MOE_BASE + MOE_CHUNKS))
                        for g in range(PIECES):
                            round_piece(R, g, 2 * WIDE)

                ffn_act(act.snap(p * MOE_CHUNKS + MOE_BASE), MOE_CHUNKS, False, 1, (7,),
                        MOE_BASE - DENSE_FULL - 1, PIECES, copy_pick, next_pass)
                pe_done(Rounds(act, p * MOE_CHUNKS + (MOE_BASE + MOE_CHUNKS)), -1)
                for n in range(2):
                    act.activation(yh[:, n * WIDE:(n + 1) * WIDE], B[4 + n][:, :], ACT.Copy).then_inc(y_high, 1)
            layer_norm_act(3 * NT)

        @block.vector
        def _(dve):
            dve.sem_inc(split, ROUND)

            def low_piece(R, g, n):
                dve.wait_ge(rounded, R.pieces + g + 1)
                src = raw[:, unit_of(g) % RAW_UNITS, (g % PIECES) * n:(g % PIECES + 1) * n]
                dve.tensor_tensor(wl[:, piece_slot(g), 0:n], src, wh[:, piece_slot(g), 0:n].bitcast(F32),
                                  ALU.subtract).then_inc(split, 1)

            def pe_done(R, g):
                dve.wait_ge(piece_used, R.pieces + SPLIT_SLOTS + g + 1)

            def transposed_low(base, t):
                for b in range(2):
                    dve.wait_ge(xt_high, base + 2 * t + b + 1)
                    dve.tensor_tensor(xtl[:, 4 * b:4 * b + 4, t * P:(t + 1) * P],
                                      B[2 * t + b][:, :].rearrange("p (k n) -> p k n", k=4),
                                      xth[:, 4 * b:4 * b + 4, t * P:(t + 1) * P].bitcast(F32), ALU.subtract)\
                        .then_inc(xt_low, 1)

            def add_residual(t, n):
                cols = xs[:, t, n * WIDE:(n + 1) * WIDE]
                dve.scalar_tensor_tensor(out=cols, in0=cols, scalar=ALPHA, in1=B[4 + 2 * t + n][:, :],
                                         op0=ALU.mult, op1=ALU.add).then_inc(residual, 1)

            def statistics(t, n):
                return dve.bn_stats(stats[:, t, n, :], xs[:, t, n * WIDE:(n + 1) * WIDE])

            def layer_norm_tile(t, base, params, steps):
                dve.wait_ge(ln_step, steps + 3 * t + 1)
                dve.memset(lnc[:, t, 0:1], 1.0)
                dve.bn_aggr(moments[:, t, :], stats[:, t, :, :]).then_inc(ln_var, 1)
                if t == 0:
                    dve.wait_ge(ln_loaded, params)
                dve.wait_ge(ln_var, base + t + 1)
                dve.scalar_tensor_tensor(out=xs[:, t, :], in0=xs[:, t, :], scalar=moments[:, t, 0:1], in1=lng[:, :],
                                         op0=ALU.subtract, op1=ALU.mult).then_inc(ln_step, 1)
                dve.wait_ge(ln_std, base + t + 1)
                dve.reciprocal(lnc[:, t, 1:2], lnc[:, t, 0:1]).then_inc(ln_step, 1)
                dve.wait_ge(ln_step, steps + 3 * t + 3)
                dve.scalar_tensor_tensor(out=xs[:, t, :], in0=xs[:, t, :], scalar=lnc[:, t, 1:2], in1=lnb[:, :],
                                         op0=ALU.mult, op1=ALU.add).then_inc(ln_out, 1)

            def ffn_dve(r0, chunks, half, tiles, tbank, chunk_off, ahead=0, before_up=None, after_hidden=None,
                        during_down=None):
                def ht_low_parts(R, k, w):
                    dve.wait_ge(ht_high, k)
                    for t in range(tiles):
                        last = dve.tensor_tensor(htl[:, 0:w // P, t * P:(t + 1) * P],
                                                 B[tbank[t]][:, 0:w].rearrange("p (f n) -> p f n", n=P),
                                                 hth[:, 0:w // P, t * P:(t + 1) * P].bitcast(F32), ALU.subtract)
                    last.then_inc(ht_low, 1)

                def hidden(R, g, k, w):
                    dve.wait_ge(silu_done, k)
                    pe_done(R, g)
                    for t in range(tiles):
                        last = dve.tensor_tensor(hbuf[:, t, 0:w], hbuf[:, t, 0:w], B[2 + t][:, 0:w], ALU.mult)
                    last.then_inc(h_done, 1)

                def first(R):
                    for g in range(ahead, 8):
                        low_piece(R, g, 2 * WIDE)
                        if g == 5 and before_up:
                            before_up()
                    hidden(R, 7, R.r - chunk_off + 1, WIDE)
                    if after_hidden:
                        after_hidden()

                def chunk(R, w, wprev):
                    for g in range(8, 20):
                        low_piece(R, g, (2 * w if g < 16 else 2 * WIDE))
                        if g == 11:
                            ht_low_parts(R, R.r - chunk_off + 1, wprev)
                    hidden(R, 15, R.r - chunk_off + 2, w)

                def tail(R, w):
                    for g in range(8, 12):
                        low_piece(R, g, 2 * w)
                        if g == 9:
                            ht_low_parts(R, R.r - chunk_off + 1, w)
                    if during_down:
                        during_down()

                ffn_stretch(dve, first, chunk, tail, r0, chunks, half)

            dve.memset(mpre[:, :, 0:3], 0.0)
            dve.memset(mv[:, :, :, :], 1.0)
            dve.memset(smax[:, :, :], 0.0).then_inc(dve_init, 1)
            for j in range(HALF_ROPE):
                last = dve.memset(invf[:, j:j + 1], float(ROPE_THETA ** (-j / HALF_ROPE)))
            last.then_inc(rope_step, 1)
            dve.wait_ge(rope_in, 16)
            dve.tensor_copy(posf[:, :], posi[:, :]).then_inc(rope_step, 1)
            dve.wait_ge(rope_step, 2)
            for t in range(NT):
                last = dve.tensor_scalar(ang[:, 0, t, :], invf[:, :], posf[:, t:t + 1], None, ALU.mult)
            last.then_inc(rope_step, 1)
            dve.wait_ge(rope_step, 3)
            dve.tensor_scalar(turn[:, 0], ang[:, 0], 1.0 / TWO_PI, None, ALU.mult)
            dve.tensor_scalar(turn[:, 1], ang[:, 0], 1.0 / TWO_PI, 0.25, ALU.mult, ALU.add).then_inc(rope_step, 1)
            dve.tensor_copy(ang[:, 1], ang[:, 0])
            dve.wait_ge(rope_step, 4)
            dve.tensor_copy(turni[:, :, :, :], turn[:, :, :, :]).then_inc(rope_step, 1)
            dve.wait_ge(rope_step, 5)
            dve.tensor_copy(turn[:, :, :, :], turni[:, :, :, :]).then_inc(rope_step, 1)
            for i, part in enumerate((6.28125, 0.0019350051879882812, TWO_PI - 6.28125 - 0.0019350051879882812)):
                dve.wait_ge(rope_step, 6 + i)
                dve.scalar_tensor_tensor(out=ang[:, :, :, :], in0=turn[:, :, :, :], scalar=-part,
                                         in1=ang[:, :, :, :], op0=ALU.mult, op1=ALU.add).then_inc(rope_step, 1)
            dve.wait_ge(rope_step, 9)
            dve.tensor_scalar(ang[:, 1], ang[:, 1], TWO_PI / 4, None, ALU.add).then_inc(rope_step, 1)
            dve.wait_ge(rope_step, 10)
            dve.tensor_scalar(ang[:, :, :, :], ang[:, :, :, :], PI_SAFE, -PI_SAFE, ALU.min, ALU.max).then_inc(sin_in, 1)
            dve.wait_ge(sin_done, 1)
            for i in range(2):
                last = dve.tensor_copy(sincos[:, i],
                                       sc8[:, i].unsqueeze(2).broadcast_to((P, NT, 2 * AH, HALF_ROPE)))
            last.then_inc(rope_table, 1)
            dve.sem_inc(dve_init, 1)
            for t in range(NT):
                transposed_low(0, t)

            with dve.Fori(0, DEPTH) as l:
                R = Rounds(dve, l * LAYER_ROUNDS)
                one, two, four, eight = (dve.snap(l * k) for k in (1, 2, 4, 8))
                FULL = 2 * WIDE
                for g in range(12):
                    low_piece(R, g, FULL)
                heads = qk[:, :, :].rearrange("p t (h d) -> p t h d", d=AD)
                x1, x2 = heads[:, :, :, 0:HALF_ROPE], heads[:, :, :, HALF_ROPE:2 * HALF_ROPE]
                sin, cos = sincos[:, 0], sincos[:, 1]
                dve.wait_ge(q_copied, two + 2)
                dve.wait_ge(k_copied, two + 2)
                dve.wait_ge(rope_table, 1)
                dve.tensor_tensor(rt[:, 0], x1, cos, ALU.mult)
                dve.tensor_tensor(rt[:, 1], x2, sin, ALU.mult)
                dve.tensor_tensor(rt[:, 2], x2, cos, ALU.mult)
                dve.tensor_tensor(rt[:, 3], x1, sin, ALU.mult).then_inc(rot_step, 1)
                dve.wait_ge(rot_step, one + 1)
                dve.tensor_tensor(x1, rt[:, 0], rt[:, 1], ALU.subtract)
                dve.tensor_tensor(x2, rt[:, 2], rt[:, 3], ALU.add).then_inc(roped, 1)
                for g in range(12, 16):
                    low_piece(R, g, 2 * 2 * MH)
                low_piece(R, 16, FULL)
                low_piece(R, 17, FULL)
                dve.wait_ge(mixp_loaded, l * 128 + 128)
                dve.wait_ge(mqk_copied, four + 4)
                for ct in range(4):
                    last = dve.tensor_scalar(cacc[:, ct, :], mpre[:, ct, 0:SEQ], cw[:, ct, 0:1], cb[:, ct:ct + 1],
                                             ALU.mult, ALU.add)
                last.then_inc(conv_step, 1)
                for j in range(1, 4):
                    dve.wait_ge(conv_step, l * 3 + j)
                    for ct in range(4):
                        last = dve.scalar_tensor_tensor(out=cacc[:, ct, :], in0=mpre[:, ct, j:j + SEQ],
                                                        scalar=cw[:, ct, j:j + 1], in1=cacc[:, ct, :],
                                                        op0=ALU.mult, op1=ALU.add)
                    last.then_inc(conv_step if j < 3 else conv_done, 1)
                low_piece(R, 18, FULL)
                low_piece(R, 19, FULL)
                pe_done(R, 15)
                for t in range(NT):
                    last = dve.tensor_tensor(gates[:, t, :], B[t][:, 0:2 * MH], gbias[:, :], ALU.add)
                last.then_inc(gates_in, 1)
                dve.wait_ge(gates_in, one + 1)
                dve.scalar_tensor_tensor(out=gtmp[:, 0], in0=gates[:, :, MH:2 * MH], scalar=-1.0,
                                         in1=gates[:, :, MH:2 * MH], op0=ALU.mult, op1=ALU.min).then_inc(absf, 1)
                low_piece(R, 20, FULL)
                dve.wait_ge(ln_f, one + 1)
                dve.scalar_tensor_tensor(out=gtmp[:, 3], in0=gates[:, :, MH:2 * MH], scalar=0.0, in1=gtmp[:, 2],
                                         op0=ALU.min, op1=ALU.subtract).then_inc(logf_done, 1)
                low_piece(R, 21, FULL)
                dve.wait_ge(qkt_psum, one + 1)
                for b in range(2):
                    dve.tensor_copy(qkt[:, 4 + 2 * b:6 + 2 * b, :], B[6 + b][:, :].rearrange("p (j n) -> p j n", j=2))\
                        .then_inc(kt_copied, 1)
                dve.wait_ge(cum_psum, one + 1)
                dve.tensor_copy(bl[:, :, :], B[0][:, 0:4 * MH].rearrange("p (c n) -> p c n", c=NT)).then_inc(cum_copied, 1)
                dve.wait_ge(cum_copied, one + 1)
                dve.tensor_tensor(aa[:, :, :], gates[:, :, 0:MH], bl[:, :, 0:MH], ALU.subtract).then_inc(a_done, 1)

                def scores(h):
                    dve.wait_ge(score_psum, eight + h + 1)
                    if h >= 2:
                        dve.wait_ge(probs_done, eight + h - 1)
                    dve.tensor_tensor(sm[:, h % 2, :], B[4][:, 0:3 * P], mask3[:, :], ALU.add).then_inc(masked, 1)
                    dve.wait_ge(masked, eight + h + 1)
                    dve.reduce_max(smax[:, h, 0:1], sm[:, h % 2, 0:P], AX_X)
                    dve.reduce_max(smax[:, h, 1:2], sm[:, h % 2, P:3 * P], AX_X).then_inc(row_max, 1)
                    dve.wait_ge(row_max, eight + h + 1)
                    dve.tensor_scalar(snb[:, h, :], smax[:, h, :], -(AD ** -0.5), None, ALU.mult)\
                        .then_inc(score_ready, 1)

                def row_maxima():
                    causal = mask3[:, 0:P].unsqueeze(1).broadcast_to((P, MH, P))
                    for c in range(NT):
                        dve.wait_ge(arow_psum, two + c + 1)
                        dve.tensor_tensor(wtmp[:, c], B[2 + c][:, :].rearrange("p (h n) -> p h n", h=MH), causal,
                                          ALU.add).then_inc(amask_step, 1)
                    dve.reduce_max(mxs[:, 2, :], B[2][:, :].rearrange("p (h n) -> p h n", h=MH), AX_X)
                    for c in range(NT):
                        dve.wait_ge(amask_step, two + c + 1)
                        dve.reduce_max(mxs[:, c, :], wtmp[:, c], AX_X).then_inc(m_step, 1)
                    six = dve.snap(l * 6)
                    dve.wait_ge(m_step, six + 2)
                    dve.tensor_scalar(mxs[:, 2, :], mxs[:, 2, :], 0.0, None, ALU.max)
                    dve.tensor_scalar(mxs[:, 4, :], mxs[:, 0, :], 0.0, None, ALU.max).then_inc(m_step, 1)
                    dve.wait_ge(m_step, six + 3)
                    dve.tensor_tensor(mxs[:, 3, :], bl[:, 0, MH:2 * MH], mxs[:, 2, :], ALU.add).then_inc(m_step, 1)
                    dve.tensor_tensor(ein[:, 0, :], aa[:, 0, :], mxs[:, 2, :], ALU.subtract)
                    dve.wait_ge(m_step, six + 4)
                    dve.tensor_tensor(mxs[:, 5, :], mxs[:, 1, :], mxs[:, 3, :], ALU.max).then_inc(m_step, 1)
                    dve.wait_ge(m_step, six + 5)
                    dve.tensor_tensor(ein[:, 1, :], mxs[:, 3, :], mxs[:, 5, :], ALU.subtract)
                    dve.scalar_tensor_tensor(out=ein[:, 2:4, :], in0=bl[:, :, 0:MH], scalar=-1.0, in1=mxs[:, 4:6, :],
                                             op0=ALU.mult, op1=ALU.subtract).then_inc(m_step, 1)

                def weight_logs():
                    for c in range(NT):
                        dve.wait_ge(mrow_psum, two + c + 1)
                        dve.tensor_tensor(wtmp[:, c], maskt[:, :].unsqueeze(1).broadcast_to((P, MH, P)),
                                          B[2 + c][:, :].rearrange("p (h n) -> p h n", h=MH), ALU.subtract)\
                            .then_inc(wlog, 1)

                def weighted_scores(c):
                    dve.wait_ge(wexp, two + c + 1)
                    dve.wait_ge(kq_psum, one + 1)
                    for j in range(2):
                        last = dve.scalar_tensor_tensor(
                            out=st[:, c].rearrange("p (i j) n -> p i j n", j=2)[:, :, j, :],
                            in0=B[2 + j][:, 2 * c * P:(2 * c + 2) * P].rearrange("p (i n) -> p i n", i=2),
                            scalar=MK ** -0.5, in1=wtmp[:, c].rearrange("p (i j) n -> p i j n", j=2)[:, :, j, :],
                            op0=ALU.mult, op1=ALU.mult)
                    last.then_inc(st_done, 1)

                for s in range(8):
                    low_piece(R, 22 + s, FULL)
                    scores(s)
                    if s == 2:
                        row_maxima()
                    if s == 4:
                        weight_logs()
                    if s == 5:
                        weighted_scores(0)
                    if s == 6:
                        weighted_scores(1)
                low_piece(R, 30, FULL)
                nine = dve.snap(l * 9)
                dve.wait_ge(exp_small, one + 1)
                dve.tensor_scalar(ein[:, 1, :], eout[:, 1, :], MK ** -0.5, None, ALU.mult).then_inc(norm_step, 1)
                dve.wait_ge(mo_exp, two + 2)
                dve.tensor_scalar(mo[:, :, :], mo[:, :, :], 1.0, None, ALU.add).then_inc(norm_step, 1)
                dve.wait_ge(norm_step, nine + 2)
                dve.reciprocal(mo[:, :, :], mo[:, :, :]).then_inc(norm_step, 1)
                dve.wait_ge(norm_step, nine + 3)
                dve.tensor_tensor(mo[:, :, :], mo[:, :, :], gnm[:, :].unsqueeze(1).broadcast_to((P, NT, MH * MV)),
                                  ALU.mult).then_inc(mo_gate, 1)
                low_piece(R, 31, FULL)
                dve.wait_ge(num_psum, two + 2)
                dve.wait_ge(inter_scaled, one + 1)
                for b in range(2):
                    last = dve.tensor_tensor(tot[:, 1, 2 * b:2 * b + 2, 0:MV + 1],
                                             B[b][:, 0:2 * (MV + 2)].rearrange("p (j v) -> p j v", j=2)[:, :, 0:MV + 1],
                                             itmp[:, 2 * b:2 * b + 2, 0:MV + 1], ALU.add)
                last.then_inc(tot_done, 1)
                dve.wait_ge(probs_done, eight + 8)
                dve.wait_ge(num0_copied, one + 1)
                dve.wait_ge(tot_done, one + 1)
                dve.reciprocal(norms[:, 0, 0:16], rsum[:, :, :].rearrange("p t h -> p (t h)"))
                dve.scalar_tensor_tensor(out=norms[:, 3, 16:24].rearrange("p (c h) -> p c h", c=NT),
                                         in0=tot[:, :, :, MV], scalar=-1.0, in1=tot[:, :, :, MV],
                                         op0=ALU.mult, op1=ALU.max).then_inc(norm_step, 1)
                dve.wait_ge(norm_step, nine + 4)
                dve.tensor_tensor(norms[:, 3, 16:24], norms[:, 3, 16:24],
                                  eout[:, 2:4, :].rearrange("p c h -> p (c h)"), ALU.max).then_inc(norm_step, 1)
                dve.wait_ge(norm_step, nine + 5)
                dve.reciprocal(norms[:, 0, 16:24], norms[:, 3, 16:24]).then_inc(norm_step, 1)
                dve.wait_ge(squares, two + 2)
                for t in range(NT):
                    dve.reduce_sum(norms[:, 1, 8 * t:8 * t + 8],
                                   mix[:, t, 0:AW].rearrange("p (h d) -> p h d", h=AH), AX_X)
                for c in range(NT):
                    last = dve.reduce_sum(norms[:, 1, 16 + 4 * c:20 + 4 * c],
                                          mix[:, c, AW:D].rearrange("p (h v) -> p h v", h=MH), AX_X)
                last.then_inc(norm_step, 1)
                dve.wait_ge(norm_step, nine + 7)
                dve.scalar_tensor_tensor(out=norms[:, 2, 0:16], in0=norms[:, 1, 0:16], scalar=1.0 / AD,
                                         in1=norms[:, 0, 0:16], op0=ALU.mult, op1=ALU.mult)
                dve.scalar_tensor_tensor(out=norms[:, 2, 16:24], in0=norms[:, 1, 16:24], scalar=1.0 / MV,
                                         in1=norms[:, 0, 16:24], op0=ALU.mult, op1=ALU.mult).then_inc(norm_step, 1)
                dve.wait_ge(norm_step, nine + 8)
                dve.tensor_tensor(norms[:, 2, :], norms[:, 2, :], norms[:, 0, :], ALU.mult).then_inc(mean_sq, 1)
                low_piece(R, 32, FULL)
                low_piece(R, 33, FULL)
                dve.wait_ge(std_done, one + 1)
                dve.reciprocal(norms[:, 4, :], norms[:, 3, :]).then_inc(norm_step, 1)
                dve.wait_ge(norm_step, nine + 9)
                dve.tensor_tensor(norms[:, 4, :], norms[:, 4, :], norms[:, 0, :], ALU.mult).then_inc(mix_done, 1)
                dve.wait_ge(mo_gate, one + 1)
                five = dve.snap(l * 5)
                dve.wait_ge(mix_done, five + 1)
                for t in range(NT):
                    dve.tensor_tensor(mix[:, t, 0:AW].rearrange("p (h d) -> p h d", h=AH), araw[:, t],
                                      norms[:, 4, 8 * t:8 * t + 8].unsqueeze(2).broadcast_to((P, AH, AD)), ALU.mult)
                    dve.tensor_tensor(mix[:, t, AW:D].rearrange("p (h v) -> p h v", h=MH), tot[:, t, :, 0:MV],
                                      norms[:, 4, 16 + 4 * t:20 + 4 * t].unsqueeze(2).broadcast_to((P, MH, MV)),
                                      ALU.mult).then_inc(mix_done, 1)
                    dve.wait_ge(mix_done, five + 2 + 2 * t)
                    dve.tensor_tensor(mix[:, t, 0:AW], mix[:, t, 0:AW], gna[:, :], ALU.mult)
                    dve.tensor_tensor(mix[:, t, AW:D], mix[:, t, AW:D], mo[:, t, :], ALU.mult).then_inc(mix_done, 1)
                xt0 = dve.snap(l * 12)
                for t in range(NT):
                    transposed_low(xt0 + 4, t)
                low_piece(R, 34, FULL)
                low_piece(R, 35, FULL)
                pe_done(R, 31)
                for t in range(NT):
                    add_residual(t, 0)
                for t in range(NT):
                    dve.wait_ge(residual, eight + t + 1)
                    statistics(t, 0)
                pe_done(R, 35)
                for t in range(NT):
                    add_residual(t, 1)
                    dve.wait_ge(residual, eight + t + 3)
                    statistics(t, 1).then_inc(ln_step, 1)
                    layer_norm_tile(t, four, l * 64 + 32, xt0)
                dve.wait_ge(ln_out, four + 2)
                dve.sem_inc(dve_init, 1)
                for t in range(NT):
                    transposed_low(xt0 + 8, t)
                with dve.If(l < 1):
                    ffn_dve(MIX_ROUNDS, DENSE_FULL, True, NT, (2, 3), 3)
                    pe_done(Rounds(dve, LAYER_ROUNDS), -1)
                    for t in range(NT):
                        add_residual(t, 0)
                        add_residual(t, 1)
                        dve.wait_ge(residual, 4 + 2 * t + 1)
                        statistics(t, 0)
                        dve.wait_ge(residual, 4 + 2 * t + 2)
                        statistics(t, 1).then_inc(ln_step, 1)
                        layer_norm_tile(t, 2, 64, 6)
                    for t in range(NT):
                        transposed_low(12, t)

            dve.wait_ge(rw_high, 1)
            dve.tensor_tensor(rwl[:, :, :], rw[:, :, :], rwh[:, :, :].bitcast(F32), ALU.subtract).then_inc(rw_low, 1)
            for t in range(NT):
                dve.wait_ge(x_high, t + 1)
                dve.tensor_tensor(xl[:, t, :], xs[:, t, :], xh[:, t, :].bitcast(F32), ALU.subtract).then_inc(x_low, 1)
            for t in range(NT):
                dve.wait_ge(x_low, t + 1)
                dve.tensor_scalar(xs[:, t, :], xs[:, t, :], ALPHA, None, ALU.mult).then_inc(accumulated, 1)
            steps = [0]

            def then(ins):
                steps[0] += 1
                ins.then_inc(route_step, 1)
                dve.wait_ge(route_step, steps[0])

            dve.wait_ge(logits_psum, 1)
            dve.wait_ge(const_ready, 2)
            for t in range(NT):
                last = dve.tensor_tensor(lg[:, t, :], B[t][:, 0:E], rb[:, :], ALU.add)
            then(last)
            for t in range(NT):
                other = lg[:, t, :].unsqueeze(1).broadcast_to((P, E, E))
                own = lg[:, t, :].unsqueeze(2).broadcast_to((P, E, E))
                dve.tensor_tensor(cmp4[:, 0, t], other, own, ALU.is_gt)
                last = dve.tensor_tensor(cmp4[:, 1, t], other, own, ALU.is_equal)
            then(last)
            for t in range(NT):
                last = dve.tensor_tensor(cmp4[:, 1, t], cmp4[:, 1, t], low8[:, :, :], ALU.mult)
            then(last)
            for t in range(NT):
                last = dve.tensor_tensor(cmp4[:, 2, t], cmp4[:, 0, t], cmp4[:, 1, t], ALU.add)
            then(last)
            for t in range(NT):
                last = dve.reduce_sum(rank[:, t, :], cmp4[:, 2, t], AX_X)
            then(last)
            dve.tensor_scalar(isel[:, 0], rank[:, :, :], 0.0, None, ALU.is_equal)
            dve.tensor_scalar(isel[:, 1], rank[:, :, :], 1.0, None, ALU.is_equal)
            dve.tensor_scalar(isel[:, 2], rank[:, :, :], 1.0, None, ALU.is_le).then_inc(picks_ready, 1)
            dve.wait_ge(picks_ready, 1)
            for i in range(2):
                last = dve.tensor_tensor(cmp4[:, 0, :, i, :], isel[:, i], lg[:, :, :], ALU.mult)
            then(last)
            for i in range(2):
                last = dve.reduce_sum(topv[:, i, :], cmp4[:, 0, :, i, :], AX_X)
            then(last)
            then(dve.tensor_tensor(topv[:, 2, :], topv[:, 1, :], topv[:, 0, :], ALU.subtract))
            dve.wait_ge(exp_f, DEPTH + 1)
            then(dve.tensor_scalar(topv[:, 4, :], topv[:, 3, :], 1.0, None, ALU.add))
            then(dve.reciprocal(topv[:, 4, :], topv[:, 4, :]))
            then(dve.tensor_tensor(topv[:, 5, :], topv[:, 4, :], topv[:, 3, :], ALU.mult))
            for t in range(NT):
                last = dve.tensor_scalar(comb[:, t, :], isel[:, 0, t, :], topv[:, 4, t:t + 1], None, ALU.mult)
            then(last)
            for t in range(NT):
                last = dve.scalar_tensor_tensor(out=comb[:, t, :], in0=isel[:, 1, t, :], scalar=topv[:, 5, t:t + 1],
                                                in1=comb[:, t, :], op0=ALU.mult, op1=ALU.add)
            then(last)
            dve.wait_ge(pos_psum, 1)
            then(dve.tensor_copy(posc[:, :, :], B[2][:, 0:3 * E].rearrange("p (a e) -> p a e", a=3)))
            dve.tensor_scalar(blk[:, 0, 1:E], posc[:, 2, 1:E], 0.0, None, ALU.is_gt)
            dve.memset(blk[:, 0, 0:1], 1.0)
            then(dve.tensor_scalar(blk[:, 1, :], posc[:, 2, :], float(P), None, ALU.is_gt))
            then(dve.tensor_tensor(blk[:, 2, :], blk[:, 0, :], blk[:, 1, :], ALU.add))
            dve.tensor_copy(blk[:, 3, 0:1], blk[:, 2, 0:1])
            then(dve.memset(blk[:, 4, 0:1], 0.0))
            for i in range(1, E):
                then(dve.tensor_tensor(blk[:, 3, i:i + 1], blk[:, 3, i - 1:i], blk[:, 2, i:i + 1], ALU.add))
            then(dve.tensor_copy(blk[:, 4, 1:E], blk[:, 3, 0:E - 1]))
            shape = (P, MAX_PASSES, E)
            passn = pass_no[:, :].unsqueeze(2).broadcast_to(shape)
            dve.tensor_tensor(pt11[:, 0], passn, blk[:, 4, :].unsqueeze(1).broadcast_to(shape), ALU.is_ge)
            dve.tensor_tensor(pt11[:, 1], passn, blk[:, 3, :].unsqueeze(1).broadcast_to(shape), ALU.is_lt)
            then(dve.tensor_tensor(pt11[:, 2], passn, blk[:, 4, :].unsqueeze(1).broadcast_to(shape), ALU.subtract))
            then(dve.tensor_tensor(pt11[:, 0], pt11[:, 0], pt11[:, 1], ALU.mult))
            then(dve.scalar_tensor_tensor(out=pt11[:, 2], in0=pt11[:, 2], scalar=float(P), in1=pt11[:, 0],
                                          op0=ALU.mult, op1=ALU.mult))
            then(dve.tensor_tensor(pt11[:, 3], pt11[:, 0], expert_no[:, :].unsqueeze(1).broadcast_to(shape), ALU.mult))
            dve.reduce_sum(tabf[:, 0:MAX_PASSES], pt11[:, 3], AX_X)
            then(dve.tensor_copy(tabf[:, MAX_PASSES:MAX_PASSES + 1], blk[:, 3, E - 1:E]))
            dve.tensor_copy(tabi[:, :], tabf[:, :]).then_inc(table_ready, 1)
            dve.memset(slotpos[:, :, MAX_PASSES:MAX_PASSES + 1], -1.0)
            for t in range(NT):
                then(dve.tensor_scalar(posc[:, t, :], posc[:, t, :], 4096.0, None, ALU.add))
                then(dve.tensor_tensor(posc[:, t, :], posc[:, t, :], isel[:, 2, t, :], ALU.mult))
                then(dve.tensor_scalar(posc[:, t, :], posc[:, t, :], -4096.0, None, ALU.add))
                then(dve.tensor_tensor(pt11[:, 3], pt11[:, 0], posc[:, t, :].unsqueeze(1).broadcast_to(shape), ALU.mult))
                dve.tensor_tensor(pt11[:, 4], pt11[:, 0], comb[:, t, :].unsqueeze(1).broadcast_to(shape), ALU.mult)
                then(dve.tensor_tensor(pt11[:, 3], pt11[:, 3], pt11[:, 2], ALU.subtract))
                dve.reduce_sum(slotpos[:, t, 0:MAX_PASSES], pt11[:, 3], AX_X)
                then(dve.reduce_sum(cbp[:, t, 1:MAX_PASSES + 1], pt11[:, 4], AX_X))

            def make_pick(p):
                for t in range(NT):
                    last = dve.tensor_scalar(pick[:, t, :], slot_no[:, :], slotpos[:, t, bass.ds(p, 1)], None,
                                             ALU.is_equal)
                last.then_inc(pick_done, 1)

            def gathered_low(p):
                dve.wait_ge(gathered, p + 1)
                for b in range(2):
                    last = dve.tensor_copy(xtl[:, 4 * b:4 * b + 4, 0:P], B[2 + b][:, :].rearrange("p (k n) -> p k n", k=4))
                last.then_inc(gath_low, 1)

            make_pick(0)
            for g in range(PIECES):
                low_piece(Rounds(dve, MOE_BASE), g, 2 * WIDE)
            gathered_low(0)
            dve.wait_ge(table_ready, 1)
            passes = dve.value_load(tabi[0:1, MAX_PASSES:MAX_PASSES + 1], min_val=1, max_val=MAX_PASSES)

            def accumulate(banks, t, column, done):
                dve.wait_ge(scattered, done)
                for n in range(2):
                    cols = xs[:, t, n * WIDE:(n + 1) * WIDE]
                    last = dve.scalar_tensor_tensor(out=cols, in0=B[banks[n]][:, :],
                                                    scalar=cbp[:, t, bass.ds(column, 1)], in1=cols,
                                                    op0=ALU.mult, op1=ALU.add)
                last.then_inc(accumulated, 1)

            with dve.Fori(0, passes) as p:
                after, two = dve.snap(p + 1), dve.snap(p * 2)

                def last_pass_tile0():
                    with dve.If(p > 0):
                        dve.wait_ge(accumulated, two)
                        accumulate((1, 3), 0, p, two)

                def last_pass_tile1():
                    with dve.If(p > 0):
                        accumulate((1, 3), 1, p, two + 1)
                    dve.wait_ge(gathered, p + 1)
                    make_pick(after)

                def next_pass():
                    with dve.If(after < passes):
                        gathered_low(after)
                        R = Rounds(dve, p * MOE_CHUNKS + (MOE_BASE + MOE_CHUNKS))
                        for g in range(PIECES):
                            low_piece(R, g, 2 * WIDE)

                ffn_dve(dve.snap(p * MOE_CHUNKS + MOE_BASE), MOE_CHUNKS, False, 1, (7,), MOE_BASE - DENSE_FULL - 1,
                        PIECES, last_pass_tile0, last_pass_tile1, next_pass)
                for n in range(2):
                    dve.wait_ge(y_high, p * 2 + n + 1)
                    dve.tensor_tensor(yl[:, n * WIDE:(n + 1) * WIDE], B[4 + n][:, :],
                                      yh[:, n * WIDE:(n + 1) * WIDE].bitcast(F32), ALU.subtract).then_inc(y_low, 1)
            final = dve.snap(passes * 2)
            dve.wait_ge(accumulated, final)
            for t in range(NT):
                accumulate((2 * t, 2 * t + 1), t, passes, final + t)
                dve.wait_ge(accumulated, final + t + 1)
                statistics(t, 0)
                statistics(t, 1).then_inc(ln_step, 1)
                layer_norm_tile(t, 3 * NT, 128, 18)

        @block.tensor
        def _(pe):
            pe.sem_inc(piece_used, SPLIT_SLOTS)
            pe.wait_ge(const_ready, 1)

            def mm3(out_ap, high, low, w_high, w_low, start, stop):
                pe.matmul(out_ap, high, w_high, start=start, stop=False, skip_group_check=True)
                pe.matmul(out_ap, high, w_low, start=False, stop=False, skip_group_check=True)
                return pe.matmul(out_ap, low, w_high, start=False, stop=stop, skip_group_check=True)

            def use_piece(R, g, per_piece, width, body):
                pe.wait_ge(split, R.pieces + ROUND + g + 1)
                for i in range(per_piece):
                    s = (g % PIECES) * per_piece + i
                    cols = slice(i * width, (i + 1) * width)
                    last = body(s, wh[:, piece_slot(g), cols], wl[:, piece_slot(g), cols])
                last.then_inc(piece_used, 1)

            def project(banks, width=WIDE, tiles=NT):
                def body(s, w_high, w_low):
                    for t in range(tiles):
                        last = mm3(B[banks[t]][:, 0:width], xth[:, s, t * P:(t + 1) * P], xtl[:, s, t * P:(t + 1) * P],
                                   w_high, w_low, s == 0, s == KD - 1)
                    return last
                return body

            def project_transposed(s, w_high, w_low):
                for ct in range(4):
                    out_ap, cols = B[4 + ct][:, 0:SEQ], slice(ct * P, (ct + 1) * P)
                    pe.matmul(out_ap, w_high[:, cols], xth[:, s, :], start=s == 0, stop=False)
                    pe.matmul(out_ap, w_high[:, cols], xtl[:, s, :], start=False, stop=False)
                    last = pe.matmul(out_ap, w_low[:, cols], xth[:, s, :], start=False, stop=s == KD - 1)
                return last

            def transpose_tile(src, t):
                for k in range(KD):
                    last = pe.transpose(B[2 * t + k // 4][:, (k % 4) * P:(k % 4 + 1) * P],
                                        src[:, t, k * P:(k + 1) * P], ident[:, :])
                    if k % 4 == 3:
                        last.then_inc(xt_psum, 1)

            def down_body(tiles, stop_at):
                def body(s, w_high, w_low):
                    f, n = s // 2, s % 2
                    for t in range(tiles):
                        last = mm3(B[4 + 2 * t + n][:, :], hth[:, f, t * P:(t + 1) * P], htl[:, f, t * P:(t + 1) * P],
                                   w_high, w_low, False, f == stop_at)
                    return last
                return body

            def ffn_pe(r0, chunks, half, tiles, tbank, chunk_off, after_gate=None, after_up=None, before_down=None):
                def transpose_h(k, w):
                    pe.wait_ge(h_done, k)
                    for t in range(tiles):
                        for f in range(w // P):
                            last = pe.transpose(B[tbank[t]][:, f * P:(f + 1) * P], hbuf[:, t, f * P:(f + 1) * P],
                                                ident[:, :])
                    last.then_inc(ht_psum, 1)

                def open_down():
                    for i in range(2 * tiles):
                        pe.matmul(B[4 + i][:, :], zrow[:, 0:P], zrow[:, :], start=True, stop=False,
                                  skip_group_check=True)

                def gate_up(R, g0, w, k, after_gate=None):
                    for g in range(g0, g0 + 4):
                        use_piece(R, g, 2, w, project((0, 1), w, tiles))
                    if after_gate:
                        after_gate()
                    if k is not None and tiles > 1:
                        pe.wait_ge(ht_low, k)
                    for g in range(g0 + 4, g0 + 8):
                        use_piece(R, g, 2, w, project((2, 3), w, tiles))

                def first(R):
                    gate_up(R, 0, WIDE, None, after_gate)
                    if after_up:
                        after_up()
                    open_down()
                    transpose_h(R.r - chunk_off + 1, WIDE)

                def chunk(R, w, wprev):
                    gate_up(R, 8, w, R.r - chunk_off + 1)
                    pe.wait_ge(ht_low, R.r - chunk_off + 1)
                    for g in range(16, 20):
                        use_piece(R, g, 2, WIDE, down_body(tiles, None))
                    transpose_h(R.r - chunk_off + 2, w)

                def tail(R, w):
                    if before_down:
                        before_down()
                    pe.wait_ge(ht_low, R.r - chunk_off + 1)
                    for g in range(8, 12):
                        use_piece(R, g, w // 256, WIDE, down_body(tiles, w // P - 1))

                ffn_stretch(pe, first, chunk, tail, r0, chunks, half)

            for t in range(NT):
                pe.wait_ge(x_loaded[t], 16)
                transpose_tile(xs, t)

            with pe.Fori(0, DEPTH) as l:
                R = Rounds(pe, l * LAYER_ROUNDS)
                one, two, four, eight = (pe.snap(l * k) for k in (1, 2, 4, 8))
                pe.wait_ge(xt_low, l * 12 + 3)
                for g in range(0, 4):
                    if g == 2:
                        pe.wait_ge(xt_low, l * 12 + 4)
                    use_piece(R, g, 2, WIDE, project((0, 1)))
                for g in range(4, 8):
                    use_piece(R, g, 2, WIDE, project((2, 3)))
                for g in range(8, 12):
                    use_piece(R, g, 2, WIDE, project_transposed)
                pe.wait_ge(q_copied, two + 2)
                for g in range(12, 16):
                    use_piece(R, g, 2, 2 * MH, project((0, 1), 2 * MH))
                pe.wait_ge(k_copied, two + 2)
                for g in range(16, 20):
                    use_piece(R, g, 2, WIDE, project((2, 3)))
                pe.wait_ge(roped, one + 1)
                pe.wait_ge(mqk_copied, four + 4)
                for j in range(8):
                    for t in range(NT):
                        last = pe.transpose(B[4 + j // 2][:, (j % 2) * SEQ + t * P:(j % 2) * SEQ + (t + 1) * P],
                                            qk[:, t, j * P:(j + 1) * P], ident[:, :])
                last.then_inc(qkt_psum, 1)
                pe.wait_ge(conv_silu, one + 1)
                pe.wait_ge(gates_in, one + 1)
                for j in range(2):
                    last = pe.transpose(B[1][:, j * P:(j + 1) * P], mqkt[:, 2 + j, 0:P], ident[:, :])
                last.then_inc(ktok_psum, 1)
                pe.wait_ge(logf_done, one + 1)
                for c in range(NT):
                    pe.matmul(B[0][:, 8 * c:8 * c + MH], tri[:, :], gtmp[:, 3, c, :], start=True, stop=True)
                    last = pe.matmul(B[0][:, 8 * c + MH:8 * c + 2 * MH], ones[:, :], gtmp[:, 3, c, :],
                                     start=True, stop=True)
                last.then_inc(cum_psum, 1)
                pe.wait_ge(cum_copied, one + 1)
                pe.wait_ge(ktok_copied, one + 1)

                def scores(h):
                    r = slice(AD * (h % 2), AD * (h % 2) + AD)
                    if h == 0:
                        pe.wait_ge(qt_copied, two + 2)
                        pe.wait_ge(kt_copied, two + 2)
                    else:
                        pe.wait_ge(masked, eight + h)
                    q, k = qkt[r, h // 2, :], qkt[r, 4 + h // 2, :]
                    pe.matmul(B[4][:, 0:P], q[:, 0:P], k[:, 0:P], start=True, stop=True)
                    pe.matmul(B[4][:, P:3 * P], q[:, P:2 * P], k, start=True, stop=True).then_inc(score_psum, 1)

                def transpose_probs(h):
                    pe.wait_ge(probs_done, eight + h + 1)
                    if h >= 1:
                        pe.wait_ge(probs_t, eight + h)
                    else:
                        pe.wait_ge(kt_copied, two + 2)
                    for j in range(3):
                        last = pe.transpose(B[6][:, j * P:(j + 1) * P], pm[:, h % 2, j * P:(j + 1) * P], ident[:, :])
                    last.then_inc(probs_t_psum, 1)

                def attend(h):
                    pe.wait_ge(probs_t, eight + h + 1)
                    if h == 0:
                        pe.wait_ge(v_copied, two + 2)
                    if h == 4:
                        pe.wait_ge(att_copied, two + 1)
                    o, cols = (h % 4) * AD, slice(h * AD, (h + 1) * AD)
                    pt = ptm[:, h % 2, :]
                    pe.matmul(B[7][:, o:o + AD], pt[:, 0:P], vv[:, 0, cols], start=True, stop=True)
                    pe.matmul(B[7][:, 4 * AD + o:5 * AD + o], pt[:, P:2 * P], vv[:, 0, cols], start=True, stop=False)
                    pe.matmul(B[7][:, 4 * AD + o:5 * AD + o], pt[:, 2 * P:3 * P], vv[:, 1, cols],
                              start=False, stop=True).then_inc(att_psum, 1)

                def diag_rows(c, ready, done):
                    pe.wait_ge(ready, two + c + 1)
                    pe.matmul(B[2 + c][:, :], ones[:, :], diag[:, c].rearrange("p h n -> p (h n)"),
                              start=True, stop=True).then_inc(done, 1)

                def kq():
                    pe.wait_ge(wlog, two + 2)
                    for c in range(NT):
                        for h in range(MH):
                            r, o = slice(MK * (h % 2), MK * (h % 2) + MK), (2 * c + h // 2) * P
                            last = pe.matmul(B[2 + h % 2][:, o:o + P], mqkt[r, 2 + h // 2, c * P:(c + 1) * P],
                                             mqkt[r, h // 2, c * P:(c + 1) * P], start=True, stop=True)
                    last.then_inc(kq_psum, 1)

                def carried_state():
                    pe.wait_ge(vw_done, one + 1)
                    for h in range(MH):
                        o = (h // 2) * (MV + 2)
                        last = pe.matmul(B[5][MK * (h % 2):MK * (h % 2) + MK, o:o + MV + 1],
                                         ktok[:, h * MK:(h + 1) * MK], vw[:, h, 0:MV + 1], start=True, stop=True)
                    last.then_inc(c_psum, 1)

                def numerators(c, bank):
                    pe.wait_ge(st_done, two + 2)
                    pe.wait_ge(mv_copied, two + 2)
                    for h in range(MH):
                        o = (h % 2) * (MV + 2)
                        last = pe.matmul(B[bank + h // 2][:, o:o + MV + 1], st[:, c, h, :], mv[:, c, h, 0:MV + 1],
                                         start=True, stop=True)
                    last.then_inc(num_psum, 1)

                for s in range(8):
                    if s == 4:
                        pe.wait_ge(mv_copied, two + 2)
                    use_piece(R, 20 + s, 2, WIDE, project((0, 1)))
                    scores(s)
                    if s >= 1:
                        transpose_probs(s - 1)
                    if s >= 2:
                        attend(s - 2)
                    if s == 1:
                        pe.wait_ge(v_copied, two + 2)
                        diag_rows(0, diag_a, arow_psum)
                        diag_rows(1, diag_a, arow_psum)
                    if s == 3:
                        pe.wait_ge(m_step, l * 6 + 6)
                        diag_rows(0, diag_m, mrow_psum)
                        diag_rows(1, diag_m, mrow_psum)
                    if s == 4:
                        kq()
                    if s == 6:
                        carried_state()
                    if s == 7:
                        numerators(0, 2)
                transpose_probs(7)
                attend(6)
                attend(7)
                pe.wait_ge(mo_exp, two + 2)
                numerators(1, 0)
                pe.wait_ge(c_copied, one + 1)
                pe.wait_ge(masked, eight + 8)
                for h in range(MH):
                    r, o = slice(MK * (h % 2), MK * (h % 2) + MK), (h // 2) * (MV + 2)
                    last = pe.matmul(B[4 + h % 2][:, o:o + MV + 1], mqkt[r, h // 2, P:2 * P], csb[r, h // 2, 0:MV + 1],
                                     start=True, stop=True)
                last.then_inc(inter_psum, 1)
                pe.wait_ge(tot_done, one + 1)
                pe.wait_ge(num0_copied, one + 1)
                for t in range(NT):
                    pe.wait_ge(mix_done, l * 5 + 3 + 2 * t)
                    transpose_tile(mix, t)
                pe.wait_ge(xt_low, l * 12 + 7)
                pe.wait_ge(att_copied, two + 2)
                for g in range(28, 32):
                    if g == 30:
                        pe.wait_ge(xt_low, l * 12 + 8)
                    use_piece(R, g, 2, WIDE, project((4, 6)))
                for g in range(32, 36):
                    use_piece(R, g, 2, WIDE, project((5, 7)))
                for t in range(NT):
                    pe.wait_ge(ln_out, four + t + 1)
                    transpose_tile(xs, t)
                with pe.If(l < 1):
                    pe.wait_ge(xt_low, 12)
                    ffn_pe(MIX_ROUNDS, DENSE_FULL, True, NT, (2, 3), 3)
                    for t in range(NT):
                        pe.wait_ge(ln_out, NT + t + 1)
                        transpose_tile(xs, t)

            pe.wait_ge(xt_low, 24)
            pe.wait_ge(rw_low, 1)
            for t in range(NT):
                for k in range(KD):
                    last = mm3(B[t][:, 0:E], xth[:, k, t * P:(t + 1) * P], xtl[:, k, t * P:(t + 1) * P],
                               rwh[:, k, :], rwl[:, k, :], k == 0, k == KD - 1)
            last.then_inc(logits_psum, 1)
            pe.wait_ge(picks_ready, 1)
            pe.matmul(B[2][:, 0:E], trs[:, :], isel[:, 2, 0, :], start=True, stop=True)
            pe.matmul(B[2][:, E:2 * E], trs[:, :], isel[:, 2, 1, :], start=True, stop=False)
            pe.matmul(B[2][:, E:2 * E], ones[:, :], isel[:, 2, 0, :], start=False, stop=True)
            pe.matmul(B[2][:, 2 * E:3 * E], ones[:, :], isel[:, 2, 0, :], start=True, stop=False)
            pe.matmul(B[2][:, 2 * E:3 * E], ones[:, :], isel[:, 2, 1, :], start=False, stop=True).then_inc(pos_psum, 1)
            def gather(p):
                pe.wait_ge(pick_done, p + 1)
                for t in range(NT):
                    last = pe.transpose(B[6][:, t * P:(t + 1) * P], pick[:, t, :].bitcast(F32), ident[:, :])
                last.then_inc(pick_psum, 1)
                for part, src in enumerate((xh, xl)):
                    for k in range(KD):
                        for t in range(NT):
                            last = pe.matmul(B[2 * part + k // 4][:, (k % 4) * P:(k % 4 + 1) * P],
                                             src[:, t, k * P:(k + 1) * P], pick[:, t, :], start=t == 0, stop=t == NT - 1)
                last.then_inc(gathered, 1)

            def scatter(banks, t):
                for n in range(2):
                    cols = slice(n * WIDE, (n + 1) * WIDE)
                    pe.matmul(B[banks[n]][:, :], pickt[:, t * P:(t + 1) * P], yh[:, cols], start=True, stop=False)
                    last = pe.matmul(B[banks[n]][:, :], pickt[:, t * P:(t + 1) * P], yl[:, cols],
                                     start=False, stop=True)
                last.then_inc(scattered, 1)

            pe.wait_ge(x_low, NT)
            gather(0)
            pe.sem_inc(scattered, 1)
            pe.wait_ge(table_ready, 1)
            passes = pe.value_load(tabi[0:1, MAX_PASSES:MAX_PASSES + 1], min_val=1, max_val=MAX_PASSES)
            with pe.Fori(0, passes) as p:
                after, two = pe.snap(p + 1), pe.snap(p * 2)

                def last_pass_tile0():
                    with pe.If(p > 0):
                        pe.wait_ge(y_low, two)
                        scatter((1, 3), 0)

                def last_pass_tile1():
                    with pe.If(p > 0):
                        pe.wait_ge(accumulated, two + 1)
                        scatter((1, 3), 1)

                def next_pass():
                    with pe.If(after < passes):
                        pe.wait_ge(accumulated, two + 2)
                        pe.wait_ge(pick_copied, after)
                        gather(after)

                pe.wait_ge(gath_high, after)
                pe.wait_ge(gath_low, after)
                ffn_pe(pe.snap(p * MOE_CHUNKS + MOE_BASE), MOE_CHUNKS, False, 1, (7,), MOE_BASE - DENSE_FULL - 1,
                       last_pass_tile0, last_pass_tile1, next_pass)
            final = pe.snap(passes * 2)
            pe.wait_ge(pick_copied, passes)
            pe.wait_ge(y_low, final)
            for t in range(NT):
                scatter((2 * t, 2 * t + 1), t)


_INS = ["x", "positions", "w_in", "gate_bias", "conv_w", "conv_b", "norm_attn", "norm_mlstm", "w_out",
        "ln1_g", "ln1_b", "dense_w_gate", "dense_w_up", "dense_w_down", "router_w", "router_b",
        "moe_w_gate", "moe_w_up", "moe_w_down", "ln2_g", "ln2_b"]


def kernel(**inputs):
    import numpy as _np
    import concourse.bacc as _bacc
    from concourse import mybir as _mybir
    from concourse.bass_utils import run_bass_kernel_spmd as _run

    nc = _bacc.Bacc("TRN2", target_bir_lowering=False, num_devices=1)
    arrays, args = {}, []
    for name in _INS:
        a = _np.ascontiguousarray(inputs[name])
        arrays[f"in_{name}_dram"] = a
        args.append(nc.dram_tensor(f"in_{name}_dram", a.shape, _mybir.dt.from_np(a.dtype), kind="ExternalInput").ap())
    shape = inputs["x"].shape
    args.append(nc.dram_tensor("out_0_dram", shape, _mybir.dt.float32, kind="ExternalOutput").ap())
    hybrid_moe_program(nc, *args)
    r = _run(nc, [arrays], core_ids=[0])
    return r.results[0]["out_0_dram"]
```

```python
from contextlib import ExitStack

import concourse.bass as bass
from concourse import mybir

F32 = mybir.dt.float32
F32R = mybir.dt.float32r
BF16 = mybir.dt.bfloat16
I32 = mybir.dt.int32
ALU = mybir.AluOpType
ACT = mybir.ActivationFunctionType
AX_X = mybir.AxisListType.X

P = 128
TWO_PI = 6.283185307179586
PI_SAFE = 3.1415925
NEG = -1.0e30
LN_EPS = 1e-5
RMS_EPS = 1e-6
ROPE_THETA = 500000.0

RAW_UNITS = 3
PIECES = 4
SPLIT_SLOTS = 6
ROUND = RAW_UNITS * PIECES
WIDE = 512


def hybrid_moe_program(nc, x, positions, w_in, gate_bias, conv_w, conv_b, norm_attn, norm_mlstm, w_out,
                       ln1_g, ln1_b, dense_w_gate, dense_w_up, dense_w_down, router_w, router_b,
                       moe_w_gate, moe_w_up, moe_w_down, ln2_g, ln2_b, out):
    _, SEQ, D = x.shape
    DEPTH = w_in.shape[0]
    N_IN = w_in.shape[2]
    D_FF = dense_w_gate.shape[2]
    E, D_EXPERT = moe_w_gate.shape[1], moe_w_gate.shape[3]
    NT = SEQ // P
    KD = D // P
    AH, AD = 8, 64
    AW = AH * AD
    MH, MV, MK = 4, 128, 64
    ALPHA = (2.0 * DEPTH) ** 0.25
    HALF_ROPE = AD // 4 // 2
    MAX_PASSES = E + 3
    assert NT == 2 and DEPTH == 2 and N_IN == 3 * AW + 3 * WIDE + 2 * MH and KD == 8

    MIX_ROUNDS = 3
    DENSE_FULL = D_FF // WIDE
    DENSE_ROUNDS = DENSE_FULL + 1
    MOE_CHUNKS = D_EXPERT // WIDE
    LAYER_ROUNDS = MIX_ROUNDS + DENSE_ROUNDS
    MOE_BASE = LAYER_ROUNDS + MIX_ROUNDS
    assert D_FF - DENSE_FULL * WIDE == WIDE // 2

    xd = x.rearrange("a (t p) d -> p (a t) d", p=P)
    outd = out.rearrange("a (t p) d -> p (a t) d", p=P)

    with ExitStack() as ctx:
        def sb(name, shape, dt=F32, where=ctx):
            return where.enter_context(nc.sbuf_tensor(name, shape, dt))

        def sem(name):
            return ctx.enter_context(nc.semaphore(name))

        raw = sb("raw", [P, RAW_UNITS, 8 * WIDE])
        wh = sb("wh", [P, SPLIT_SLOTS, 2 * WIDE], F32R)
        wl = sb("wl", [P, SPLIT_SLOTS, 2 * WIDE], F32R)
        xs = sb("xs", [P, NT, D])
        xth = sb("xth", [P, KD, SEQ], F32R)
        xtl = sb("xtl", [P, KD, SEQ], F32R)
        lng = sb("lng", [P, D])
        lnb = sb("lnb", [P, D])
        ident = sb("ident", [P, P])
        ones = sb("ones", [P, P])
        tri = sb("tri", [P, P])
        trs = sb("trs", [P, P])
        mask3 = sb("mask3", [P, 3 * P])
        maskt = sb("maskt", [P, P])
        slot_no = sb("slot_no", [P, P])
        zrow = sb("zrow", [P, WIDE], BF16)
        eps = sb("eps", [P, 2])
        early = sb("early", [P, 1])
        rw = sb("rw", [P, KD, E])
        rwh = sb("rwh", [P, KD, E], F32R)
        rwl = sb("rwl", [P, KD, E], F32R)
        rb = sb("rb", [P, E])
        stats = sb("stats", [P, NT, 2, 6])
        moments = sb("moments", [P, NT, 2])
        lnc = sb("lnc", [P, NT, 2])

        mix_mem = ctx.enter_context(ExitStack())
        qk = sb("qk", [P, NT, 2 * AW], F32, mix_mem)
        mix = qk
        qkt = sb("qkt", [P, 8, SEQ], F32, mix_mem)
        posi = sb("posi", [P, NT], I32, mix_mem)
        posf = sb("posf", [P, NT], F32, mix_mem)
        invf = sb("invf", [P, HALF_ROPE], F32, mix_mem)
        ang = sb("ang", [P, 2, NT, HALF_ROPE], F32, mix_mem)
        turn = sb("turn", [P, 2, NT, HALF_ROPE], F32, mix_mem)
        turni = sb("turni", [P, 2, NT, HALF_ROPE], I32, mix_mem)
        sc8 = sb("sc8", [P, 2, NT, HALF_ROPE], F32, mix_mem)
        sincos = sb("sincos", [P, 2, NT, 2 * AH, HALF_ROPE], F32, mix_mem)
        gbias = sb("gbias", [P, 2 * MH], F32, mix_mem)
        cw = sb("cw", [P, 4, 4], F32, mix_mem)
        cb = sb("cb", [P, 4], F32, mix_mem)
        gna = sb("gna", [P, AW], F32, mix_mem)
        gnm = sb("gnm", [P, MH * MV], F32, mix_mem)
        vv = sb("vv", [P, NT, AW], F32, mix_mem)
        mpre = sb("mpre", [P, 4, 3 + SEQ], F32, mix_mem)
        cacc = sb("cacc", [P, 4, SEQ], F32, mix_mem)
        mqkt = sb("mqkt", [P, 4, SEQ], F32, mix_mem)
        ktok = sb("ktok", [P, MH * MK], F32, mix_mem)
        mv = sb("mv", [P, NT, MH, MV + 2], F32, mix_mem)
        mo = sb("mo", [P, NT, MH * MV], F32, mix_mem)
        sm = sb("sm", [P, 2, 3 * P], F32, mix_mem)
        pm = sb("pm", [P, 2, 3 * P], F32, mix_mem)
        ptm = sb("ptm", [P, 2, 3 * P], F32, mix_mem)
        smax = sb("smax", [P, AH, NT], F32, mix_mem)
        snb = sb("snb", [P, AH, NT], F32, mix_mem)
        norms = sb("norms", [P, 5, 24], F32, mix_mem)
        rsum = sb("rsum", [P, NT, AH], F32, mix_mem)
        araw = cacc[:, :, :].rearrange("p c n -> p (c n)").rearrange("p (t h d) -> p t h d", t=NT, h=AH)
        gates = sb("gates", [P, NT, 2 * MH], F32, mix_mem)
        gtmp = sb("gtmp", [P, 4, NT, MH], F32, mix_mem)
        bl = sb("bl", [P, NT, 2 * MH], F32, mix_mem)
        aa = sb("aa", [P, NT, MH], F32, mix_mem)
        diag = sb("diag", [P, NT, MH, P], F32, mix_mem)
        wtmp = sb("wtmp", [P, NT, MH, P], F32, mix_mem)
        st = diag
        wflat = wtmp[:, :, :, :].rearrange("p c h n -> p (c h n)")
        rt = wflat.rearrange("p (i t h j) -> p i t h j", i=4, t=NT, h=2 * AH)
        gatest = wflat[0:2 * MH, 0:SEQ]
        mxs = sb("mxs", [P, 6, MH], F32, mix_mem)
        ein = sb("ein", [P, 4, MH], F32, mix_mem)
        eout = sb("eout", [P, 4, MH], F32, mix_mem)
        vw = sb("vw", [P, MH, MV + 2], F32, mix_mem)
        csb = sb("csb", [P, 2, MV + 2], F32, mix_mem)
        tot = sb("tot", [P, NT, MH, MV + 2], F32, mix_mem)
        mix_mem.close()
        hbuf = sb("hbuf", [P, NT, WIDE])
        hth = sb("hth", [P, 4, SEQ], F32R)
        htl = sb("htl", [P, 4, SEQ], F32R)
        xb = sb("xb", [P, 3, NT, D], BF16)
        xrem = sb("xrem", [P, NT, D])
        yh = sb("yh", [P, D], F32R)
        yl = sb("yl", [P, D], F32R)
        pick = sb("pick", [P, NT, P], BF16)
        identb = sb("identb", [P, P], BF16)
        pickt = sb("pickt", [P, SEQ], F32R)
        lgt = sb("lgt", [E, SEQ])
        lg = sb("lg", [P, NT, E])
        cmp4 = sb("cmp4", [P, 3, NT, E, E])
        rank = sb("rank", [P, NT, E])
        isel = sb("isel", [P, 3, NT, E])
        topv = sb("topv", [P, 6, NT])
        comb = sb("comb", [P, NT, E])
        posc = sb("posc", [P, 3, E])
        blk = sb("blk", [P, 5, E])
        pt11 = sb("pt11", [P, 5, MAX_PASSES, E])
        slotpos = sb("slotpos", [P, NT, MAX_PASSES + 1])
        cbp = sb("cbp", [P, NT, MAX_PASSES + 1])
        tabf = sb("tabf", [P, MAX_PASSES + 1])
        tabi = sb("tabi", [P, MAX_PASSES + 1], I32)
        low8 = sb("low8", [P, E, E])
        pass_no = sb("pass_no", [P, MAX_PASSES])
        expert_no = sb("expert_no", [P, E])

        B = [ctx.enter_context(nc.psum_tensor(f"B{i}", [P, WIDE], F32)) for i in range(8)]

        raw_full = [sem(f"raw_full{i}") for i in range(RAW_UNITS)]
        rounded = sem("rounded")
        split = sem("split")
        piece_used = sem("piece_used")
        x_loaded = [sem(f"x_loaded{t}") for t in range(NT)]
        const_ready, rope_in = sem("const_ready"), sem("rope_in")
        const_step = sem("const_step")
        mixp_loaded, ln_loaded, router_loaded = sem("mixp_loaded"), sem("ln_loaded"), sem("router_loaded")
        dve_init = sem("dve_init")
        rope_step, sin_in, sin_done, rope_table = sem("rope_step"), sem("sin_in"), sem("sin_done"), sem("rope_table")
        xt_psum, xt_high, xt_low = sem("xt_psum"), sem("xt_high"), sem("xt_low")
        q_copied, k_copied, v_copied = sem("q_copied"), sem("k_copied"), sem("v_copied")
        mqk_copied, roped, rot_step = sem("mqk_copied"), sem("roped"), sem("rot_step")
        conv_step, conv_done, conv_silu = sem("conv_step"), sem("conv_done"), sem("conv_silu")
        gates_in, absf, exp_f, ln_f, logf_done = sem("gates_in"), sem("absf"), sem("exp_f"), sem("ln_f"), sem("logf_done")
        cum_psum, cum_copied, a_done, ktok_psum, ktok_copied = (
            sem("cum_psum"), sem("cum_copied"), sem("a_done"), sem("ktok_psum"), sem("ktok_copied"))
        qkt_psum, qt_copied, kt_copied = sem("qkt_psum"), sem("qt_copied"), sem("kt_copied")
        score_psum, masked, row_max, score_ready = sem("score_psum"), sem("masked"), sem("row_max"), sem("score_ready")
        probs_done, probs_t_psum, probs_t, att_psum, att_copied = (
            sem("probs_done"), sem("probs_t_psum"), sem("probs_t"), sem("att_psum"), sem("att_copied"))
        diag_a, arow_psum, amask_step, m_step, diag_m, mrow_psum = (
            sem("diag_a"), sem("arow_psum"), sem("amask_step"), sem("m_step"), sem("diag_m"), sem("mrow_psum"))
        exp_small, wlog, wexp, kq_psum, st_done = (
            sem("exp_small"), sem("wlog"), sem("wexp"), sem("kq_psum"), sem("st_done"))
        mv_copied, mo_sig, vw_done, c_psum, c_copied = (
            sem("mv_copied"), sem("mo_sig"), sem("vw_done"), sem("c_psum"), sem("c_copied"))
        num_psum, num_copied, inter_psum, tot_done = (
            sem("num_psum"), sem("num_copied"), sem("inter_psum"), sem("tot_done"))
        mo_gate, squares, norm_step, mean_sq, std_done, mix_done, inter_w = (
            sem("mo_gate"), sem("squares"), sem("norm_step"), sem("mean_sq"), sem("std_done"), sem("mix_done"),
            sem("inter_w"))
        residual = sem("residual")
        ln_step, ln_var, ln_std, ln_out = sem("ln_step"), sem("ln_var"), sem("ln_std"), sem("ln_out")
        silu_done, h_done, ht_psum, ht_high, ht_low, ffn_added = (
            sem("silu_done"), sem("h_done"), sem("ht_psum"), sem("ht_high"), sem("ht_low"), sem("ffn_added"))
        gates_t, gates_psum = sem("gates_t"), sem("gates_psum")
        logits_t_psum, logits_t, top_gap = sem("logits_t_psum"), sem("logits_t"), sem("top_gap")
        rw_high, rw_low, logits_psum, route_step, picks_ready, pos_psum, table_ready = (
            sem("rw_high"), sem("rw_low"), sem("logits_psum"), sem("route_step"), sem("picks_ready"),
            sem("pos_psum"), sem("table_ready"))
        x_high, x_rest, x_mid, x_low = sem("x_high"), sem("x_rest"), sem("x_mid"), sem("x_low")
        pick_done, pick_psum, pick_copied, gathered, gath_high, gath_low = (
            sem("pick_done"), sem("pick_psum"), sem("pick_copied"), sem("gathered"), sem("gath_high"), sem("gath_low"))
        y_high, y_low, scattered, accumulated = (
            sem("y_high"), sem("y_low"), sem("scattered"), sem("accumulated"))
        stored = sem("stored")

        block = ctx.enter_context(nc.Block())

        class Rounds:

            def __init__(self, eng, r):
                fixed = isinstance(r, int)
                self.r = r if fixed else eng.snap(r)
                self.pieces = r * ROUND if fixed else eng.snap(self.r * ROUND)
                self.loads = r * 16 if fixed else eng.snap(self.r * 16)

        def piece_slot(g):
            return g % SPLIT_SLOTS

        def unit_of(g):
            return g // PIECES

        def mixer_piece(g):
            return 2 * (2 * MH if unit_of(g) == 1 else WIDE)

        def ffn_stretch(eng, first, chunk, tail, r0, chunks, half):
            first(Rounds(eng, r0))
            with eng.Fori(0, chunks - 1) as c:
                chunk(Rounds(eng, c + r0), WIDE, WIDE)
            if half:
                chunk(Rounds(eng, r0 + chunks - 1), WIDE // 2, WIDE)
                tail(Rounds(eng, r0 + chunks), WIDE // 2)
            else:
                tail(Rounds(eng, r0 + chunks - 1), WIDE)

        @block.sync
        def _(sp):
            def load(R, j, dst, src):
                sp.wait_ge(split, R.pieces + PIECES * j + PIECES)
                sp.dma_start(dst, src).then_inc(raw_full[j % RAW_UNITS], 16)

            def slices(j, width, n=8):
                return raw[:, j % RAW_UNITS, 0:n * width].rearrange("p (k n) -> p k n", k=n)

            def columns(w2d, c0, width):
                return w2d.rearrange("(k p) n -> p k n", p=P)[:, :, c0:c0 + width]

            def load_columns(R, j, w2d, c0, width):
                load(R, j, slices(j, width), columns(w2d, c0, width))

            def load_rows(R, j, w2d, r0, n):
                load(R, j, raw[:, j % RAW_UNITS, 0:n * D].rearrange("p (k n) -> p k n", k=n), w2d(r0, n))

            for t in range(NT):
                sp.dma_start(xs[:, t, :], xd[:, t, :]).then_inc(x_loaded[t], 16)
            with sp.Fori(0, DEPTH) as l:
                R = Rounds(sp, l * LAYER_ROUNDS)
                wi = w_in[bass.ds(l, 1), :, :].rearrange("a (k p) n -> p (a k) n", p=P)
                wo = w_out[bass.ds(l, 1), :, :].rearrange("a (k p) n -> p (a k) n", p=P)
                order = [(0, WIDE), (3 * AW + 3 * WIDE, 2 * MH), (AW, WIDE), (3 * AW, WIDE),
                         (2 * AW, WIDE), (3 * AW + WIDE, WIDE), (3 * AW + 2 * WIDE, WIDE)]
                for j, (c0, width) in enumerate(order):
                    load(R, j, slices(j, width), wi[:, :, c0:c0 + width])
                for n in range(2):
                    load(R, 7 + n, slices(7 + n, WIDE), wo[:, :, n * WIDE:(n + 1) * WIDE])
                with sp.If(l < 1):
                    def down_rows(r0, n):
                        return dense_w_down[0, r0:r0 + n * P, :].rearrange("(k p) n -> p k n", p=P)

                    R = Rounds(sp, MIX_ROUNDS)
                    load_columns(R, 0, dense_w_gate[0], 0, WIDE)
                    load_columns(R, 1, dense_w_up[0], 0, WIDE)
                    with sp.Fori(0, DENSE_FULL - 1) as c:
                        R = Rounds(sp, c + MIX_ROUNDS)
                        cols = bass.ds(c * WIDE + WIDE, WIDE)
                        load(R, 2, slices(2, WIDE), dense_w_gate[0, :, cols].rearrange("(k p) n -> p k n", p=P))
                        load(R, 3, slices(3, WIDE), dense_w_up[0, :, cols].rearrange("(k p) n -> p k n", p=P))
                        load(R, 4, raw[:, 4 % RAW_UNITS, 0:4 * D].rearrange("p (k n) -> p k n", k=4),
                             dense_w_down[0, bass.ds(c * WIDE, WIDE), :].rearrange("(k p) n -> p k n", p=P))
                    R = Rounds(sp, MIX_ROUNDS + DENSE_FULL - 1)
                    load_columns(R, 2, dense_w_gate[0], DENSE_FULL * WIDE, WIDE // 2)
                    load_columns(R, 3, dense_w_up[0], DENSE_FULL * WIDE, WIDE // 2)
                    load_rows(R, 4, down_rows, (DENSE_FULL - 1) * WIDE, 4)
                    load_rows(Rounds(sp, MIX_ROUNDS + DENSE_FULL), 2, down_rows, DENSE_FULL * WIDE, 2)

            R = Rounds(sp, MOE_BASE)
            load_columns(R, 0, moe_w_gate[0, 0], 0, WIDE)
            load_columns(R, 1, moe_w_up[0, 0], 0, WIDE)
            sp.wait_ge(table_ready, 1)
            passes = sp.value_load(tabi[0:1, MAX_PASSES:MAX_PASSES + 1], min_val=1, max_val=MAX_PASSES)
            with sp.Fori(0, passes) as p:
                e = sp.value_load(tabi[0:1, bass.ds(p, 1)], min_val=0, max_val=E - 1)

                def expert_columns(w, which, cols):
                    return w[0, bass.ds(which, 1), :, cols].rearrange("a (k p) n -> p (a k) n", p=P)

                def expert_rows(rows):
                    return moe_w_down[0, bass.ds(e, 1), rows, :].rearrange("a (k p) n -> p (a k) n", p=P)

                r0 = sp.snap(p * MOE_CHUNKS + MOE_BASE)
                with sp.Fori(0, MOE_CHUNKS - 1) as c:
                    R = Rounds(sp, c + r0)
                    cols = bass.ds(c * WIDE + WIDE, WIDE)
                    load(R, 2, slices(2, WIDE), expert_columns(moe_w_gate, e, cols))
                    load(R, 3, slices(3, WIDE), expert_columns(moe_w_up, e, cols))
                    load(R, 4, raw[:, 4 % RAW_UNITS, 0:4 * D].rearrange("p (k n) -> p k n", k=4),
                         expert_rows(bass.ds(c * WIDE, WIDE)))
                R = Rounds(sp, r0 + (MOE_CHUNKS - 1))
                load(R, 2, raw[:, 2, 0:4 * D].rearrange("p (k n) -> p k n", k=4),
                     expert_rows(slice((MOE_CHUNKS - 1) * WIDE, MOE_CHUNKS * WIDE)))
                with sp.If(p + 1 < passes):
                    after = sp.value_load(tabi[0:1, bass.ds(p + 1, 1)], min_val=0, max_val=E - 1)
                    R = Rounds(sp, r0 + MOE_CHUNKS)
                    load(R, 0, slices(0, WIDE), expert_columns(moe_w_gate, after, slice(0, WIDE)))
                    load(R, 1, slices(1, WIDE), expert_columns(moe_w_up, after, slice(0, WIDE)))

            for t in range(NT):
                sp.wait_ge(ln_out, 2 * NT * (DEPTH - 1) + NT + t + 1)
                sp.dma_start(outd[:, t, :], xs[:, t, :]).then_inc(stored, 16)
            sp.wait_ge(stored, 16 * NT)

        @block.gpsimd
        def _(pool):

            pool.memset(zrow[:, :], 0.0)
            pool.memset(eps[:, 0:1], LN_EPS)
            pool.memset(eps[:, 1:2], RMS_EPS)
            pool.memset(ident[:, :], 0.0)
            pool.memset(tri[:, :], 1.0)
            pool.memset(trs[:, :], 1.0)
            pool.memset(mask3[:, :], 0.0)
            pool.memset(maskt[:, :], 0.0)
            pool.memset(ones[:, :], 1.0).then_inc(const_step, 1)
            pool.iota(slot_no[:, :], pattern=[[1, P]], base=0, channel_multiplier=0,
                      allow_small_or_imprecise_dtypes=True)
            pool.wait_ge(const_step, 1)
            pool.affine_select(out=ident[:, :], in_=ident[:, :], compare_op=ALU.not_equal, fill=1.0,
                               base=0, pattern=[[-1, P]], channel_multiplier=1)
            pool.affine_select(out=tri[:, :], in_=tri[:, :], compare_op=ALU.is_ge, fill=0.0,
                               base=0, pattern=[[1, P]], channel_multiplier=-1)
            pool.affine_select(out=trs[:, :], in_=trs[:, :], compare_op=ALU.is_ge, fill=0.0,
                               base=-1, pattern=[[1, P]], channel_multiplier=-1)
            pool.affine_select(out=maskt[:, :], in_=maskt[:, :], compare_op=ALU.is_ge, fill=NEG,
                               base=0, pattern=[[1, P]], channel_multiplier=-1)
            pool.affine_select(out=mask3[:, 0:P], in_=mask3[:, 0:P], compare_op=ALU.is_ge, fill=NEG,
                               base=0, pattern=[[-1, P]], channel_multiplier=1)
            pool.affine_select(out=mask3[:, 2 * P:3 * P], in_=mask3[:, 2 * P:3 * P], compare_op=ALU.is_ge,
                               fill=NEG, base=0, pattern=[[-1, P]], channel_multiplier=1).then_inc(const_ready, 1)
            with nc.allow_non_contiguous_dma(reason="small parameters"):
                pool.dma_start(rw[:, :, :], router_w[0].rearrange("(k p) e -> p k e", p=P)).then_inc(router_loaded, 16)
                pool.dma_start(rb[:, :], router_b.broadcast_to((P, E))).then_inc(router_loaded, 16)

            def load_ln(g, b, done):
                if done is not None:
                    pool.wait_ge(ln_out, done)
                pool.dma_start(lng[:, :], g.broadcast_to((P, D))).then_inc(ln_loaded, 16)
                pool.dma_start(lnb[:, :], b.broadcast_to((P, D))).then_inc(ln_loaded, 16)

            load_ln(ln1_g[0:1, :], ln1_b[0:1, :], None)
            with pool.Fori(0, DEPTH) as l:
                row = bass.ds(l, 1)
                pool.wait_ge(dve_init, 2 + l)
                with nc.allow_non_contiguous_dma(reason="small parameters"):
                    for j in range(4):
                        pool.dma_start(cw[:, :, j], conv_w[row, j, :].rearrange("a (c p) -> p (a c)", p=P))\
                            .then_inc(mixp_loaded, 16)
                    pool.dma_start(cb[:, :], conv_b[row, :].rearrange("a (c p) -> p (a c)", p=P)).then_inc(mixp_loaded, 16)
                    pool.dma_start(gbias[:, :], gate_bias[row, :].broadcast_to((P, 2 * MH))).then_inc(mixp_loaded, 16)
                    pool.dma_start(gna[:, :], norm_attn[row, :].broadcast_to((P, AW))).then_inc(mixp_loaded, 16)
                    pool.dma_start(gnm[:, :], norm_mlstm[row, :].broadcast_to((P, MH * MV))).then_inc(mixp_loaded, 16)

                pool.wait_ge(a_done, l + 1)
                for c in range(NT):
                    pool.tensor_tensor(diag[:, c], ident[:, :].unsqueeze(1).broadcast_to((P, MH, P)),
                                       aa[:, c, :].unsqueeze(2).broadcast_to((P, MH, P)), ALU.mult).then_inc(diag_a, 1)
                pool.wait_ge(m_step, l * 6 + 6)
                pool.wait_ge(arow_psum, l * 2 + 2)
                for c in range(NT):
                    pool.tensor_tensor(diag[:, c], ident[:, :].unsqueeze(1).broadcast_to((P, MH, P)),
                                       mxs[:, 4 + c, :].unsqueeze(2).broadcast_to((P, MH, P)), ALU.mult)\
                        .then_inc(diag_m, 1)
                pool.wait_ge(mixp_loaded, l * 128 + 128)
                pool.wait_ge(ln_loaded, l * 64 + 32)
                pool.wait_ge(exp_small, l + 1)
                pool.wait_ge(mv_copied, l * 2 + 1)
                pool.tensor_tensor(vw[:, :, 0:MV + 1], mv[:, 0, :, 0:MV + 1],
                                   eout[:, 0, :].unsqueeze(2).broadcast_to((P, MH, MV + 1)), ALU.mult)\
                    .then_inc(vw_done, 1)
                pool.wait_ge(mo_sig, l * 2 + 2)
                pool.tensor_tensor(mo[:, :, :], mo[:, :, :], gnm[:, :].unsqueeze(1).broadcast_to((P, NT, MH * MV)),
                                   ALU.mult).then_inc(mo_gate, 1)
                three = pool.snap(l * 3)
                for c in range(NT):
                    pool.wait_ge(squares, l * 4 + 2 + 2 * c)
                    if c == 0:
                        pool.wait_ge(mo_gate, three + 1)
                    pool.tensor_tensor(tot[:, c, :, 0:MV], tot[:, c, :, 0:MV],
                                       mo[:, c, :].rearrange("p (h v) -> p h v", h=MH), ALU.mult).then_inc(mo_gate, 1)
                with pool.If(l < 1):
                    load_ln(ln2_g[0:1, :], ln2_b[0:1, :], NT)
                    pool.wait_ge(ln_loaded, 64)
                    load_ln(ln1_g[1:2, :], ln1_b[1:2, :], 2 * NT)
            load_ln(ln2_g[1:2, :], ln2_b[1:2, :], 3 * NT)
            pool.memset(low8[:, :, :], 1.0).then_inc(const_step, 1)
            pool.tensor_copy(identb[:, :], ident[:, :])
            pool.iota(pass_no[:, :], pattern=[[1, MAX_PASSES]], base=0, channel_multiplier=0,
                      allow_small_or_imprecise_dtypes=True)
            pool.iota(expert_no[:, :], pattern=[[1, E]], base=0, channel_multiplier=0,
                      allow_small_or_imprecise_dtypes=True)
            pool.wait_ge(const_step, 2)
            pool.affine_select(out=low8[:, :, :], in_=low8[:, :, :], compare_op=ALU.is_gt, fill=0.0,
                               base=0, pattern=[[1, E], [-1, E]], channel_multiplier=0).then_inc(const_ready, 1)
            pool.wait_ge(x_low, NT)
            for t in range(NT):
                pool.tensor_scalar(xs[:, t, :], xs[:, t, :], ALPHA, None, ALU.mult).then_inc(accumulated, 1)
            pool.wait_ge(mixp_loaded, 16 * 8 * DEPTH)
            pool.wait_ge(ln_loaded, 16 * 2 * 2 * DEPTH)
            pool.wait_ge(router_loaded, 32)

        @block.scalar
        def _(act):
            def round_piece(R, g, n):
                if g % PIECES == 0:
                    act.wait_ge(raw_full[unit_of(g) % RAW_UNITS], R.loads + 16 * (unit_of(g) // RAW_UNITS) + 16)
                act.wait_ge(piece_used, R.pieces + g + 1)
                src = raw[:, unit_of(g) % RAW_UNITS, (g % PIECES) * n:(g % PIECES + 1) * n]
                act.activation(wh[:, piece_slot(g), 0:n], src, ACT.Copy).then_inc(rounded, 1)

            def pe_done(R, g):
                act.wait_ge(piece_used, R.pieces + SPLIT_SLOTS + g + 1)

            def transposed_high(base, t):
                for b in range(2):
                    act.wait_ge(xt_psum, base + 2 * t + b + 1)
                    act.activation(xth[:, 4 * b:4 * b + 4, t * P:(t + 1) * P],
                                   B[2 * t + b][:, :].rearrange("p (k n) -> p k n", k=4), ACT.Copy)\
                        .then_inc(xt_high, 1)

            def layer_norm_act(base):
                for t in range(NT):
                    act.wait_ge(ln_var, base + t + 1)
                    act.activation(lnc[:, t, 0:1], moments[:, t, 1:2], ACT.Sqrt, bias=eps[:, 0:1]).then_inc(ln_std, 1)

            def ffn_act(r0, chunks, half, tiles, tbank, chunk_off, ahead=0, before_down=None, during_down=None):
                def n_chunk(R):
                    return R.r - chunk_off

                def ht_high_parts(R, k, w):
                    act.wait_ge(ht_psum, k)
                    for t in range(tiles):
                        last = act.activation(hth[:, 0:w // P, t * P:(t + 1) * P],
                                              B[tbank[t]][:, 0:w].rearrange("p (f n) -> p f n", n=P), ACT.Copy)
                    last.then_inc(ht_high, 1)

                def silu(R, g, w):
                    pe_done(R, g)
                    for t in range(tiles):
                        last = act.activation(hbuf[:, t, 0:w], B[t][:, 0:w], ACT.Silu)
                    last.then_inc(silu_done, 1)

                def first(R):
                    for g in range(ahead, 8):
                        round_piece(R, g, 2 * WIDE)
                        if g == 7:
                            silu(R, 3, WIDE)

                def chunk(R, w, wprev):
                    for g in range(8, 20):
                        round_piece(R, g, (2 * w if g < 16 else 2 * WIDE))
                        if g == 11:
                            ht_high_parts(R, n_chunk(R) + 1, wprev)
                        if g == 17:
                            silu(R, 11, w)

                def tail(R, w):
                    if before_down:
                        before_down()
                    for g in range(8, 12):
                        round_piece(R, g, 2 * w)
                        if g == (11 if half else 9):
                            ht_high_parts(R, n_chunk(R) + 1, w)
                    if during_down:
                        during_down()

                ffn_stretch(act, first, chunk, tail, r0, chunks, half)

            with nc.allow_non_contiguous_dma(reason="one position per partition"):
                act.dma_start(posi[:, :], positions.rearrange("a (t p) -> p (a t)", p=P)).then_inc(rope_in, 16)
            act.wait_ge(sin_in, 1)
            act.activation(sc8[:, :, :, :], ang[:, :, :, :], ACT.Sin).then_inc(sin_done, 1)
            for t in range(NT):
                transposed_high(0, t)
            for g in range(PIECES):
                round_piece(Rounds(act, 0), g, mixer_piece(g))
            act.wait_ge(router_loaded, 32)
            act.activation(rwh[:, :, :], rw[:, :, :], ACT.Copy).then_inc(rw_high, 1)

            with act.Fori(0, DEPTH) as l:
                R = Rounds(act, l * LAYER_ROUNDS)
                one, two, four, eight = (act.snap(l * k) for k in (1, 2, 4, 8))
                FULL = 2 * WIDE
                for g in range(PIECES, 10):
                    round_piece(R, g, mixer_piece(g))
                pe_done(R, 3)
                for t in range(NT):
                    act.activation(qk[:, t, 0:AW], B[t][:, :], ACT.Copy).then_inc(q_copied, 1)
                for g in range(10, 16):
                    round_piece(R, g, FULL)
                act.wait_ge(absf, one + 1)
                act.activation(gtmp[:, 1], gtmp[:, 0], ACT.Exp).then_inc(exp_f, 1)
                act.wait_ge(exp_f, one + 1)
                act.activation(gtmp[:, 2], gtmp[:, 1], ACT.Ln, bias=ones[:, 0:1]).then_inc(ln_f, 1)
                pe_done(R, 11)
                for t in range(NT):
                    act.activation(qk[:, t, AW:2 * AW], B[2 + t][:, :], ACT.Copy).then_inc(k_copied, 1)
                for g in range(16, 20):
                    round_piece(R, g, FULL)
                pe_done(R, 15)
                act.wait_ge(dve_init, 1)
                for ct in range(4):
                    act.activation(mpre[:, ct, 3:3 + SEQ], B[4 + ct][:, 0:SEQ], ACT.Copy).then_inc(mqk_copied, 1)
                round_piece(R, 20, FULL)
                act.wait_ge(conv_done, one + 1)
                act.activation(mqkt[:, :, :], cacc[:, :, :], ACT.Silu).then_inc(conv_silu, 1)
                for g in range(21, 24):
                    round_piece(R, g, FULL)
                pe_done(R, 19)
                for t in range(NT):
                    act.activation(vv[:, t, :], B[2 + t][:, :], ACT.Copy).then_inc(v_copied, 1)
                act.wait_ge(ktok_psum, one + 1)
                act.activation(ktok[:, :], B[1][:, 0:MH * MK], ACT.Copy).then_inc(ktok_copied, 1)
                act.wait_ge(qkt_psum, one + 1)
                for b in range(2):
                    act.activation(qkt[:, 2 * b:2 * b + 2, :], B[4 + b][:, :].rearrange("p (j n) -> p j n", j=2),
                                   ACT.Copy).then_inc(qt_copied, 1)

                def probs(h):
                    act.wait_ge(score_ready, eight + h + 1)
                    if h >= 2:
                        act.wait_ge(probs_t_psum, eight + h - 1)
                    else:
                        act.wait_ge(dve_init, 1)
                    act.activation(pm[:, h % 2, 0:P], sm[:, h % 2, 0:P], ACT.Exp, bias=snb[:, h, 0:1],
                                   scale=AD ** -0.5, accum_out=rsum[:, 0, h:h + 1])
                    act.activation(pm[:, h % 2, P:3 * P], sm[:, h % 2, P:3 * P], ACT.Exp, bias=snb[:, h, 1:2],
                                   scale=AD ** -0.5, accum_out=rsum[:, 1, h:h + 1]).then_inc(probs_done, 1)

                def probs_transposed(h):
                    act.wait_ge(probs_t_psum, eight + h + 1)
                    if h >= 2:
                        act.wait_ge(att_psum, eight + h - 1)
                    act.activation(ptm[:, h % 2, :], B[6][:, 0:3 * P], ACT.Copy).then_inc(probs_t, 1)

                def copy_attention(half):
                    act.wait_ge(att_psum, eight + 4 * half + 4)
                    act.activation(araw[:, :, 4 * half:4 * half + 4, :],
                                   B[7][:, :].rearrange("p (t h d) -> p t h d", t=NT, h=4), ACT.Copy)\
                        .then_inc(att_copied, 1)

                def state_weights(c):
                    act.wait_ge(wlog, two + c + 1)
                    for h in range(MH):
                        last = act.activation(wtmp[:, c, h, :], wtmp[:, c, h, :], ACT.Exp, bias=aa[:, c, h:h + 1])
                    last.then_inc(wexp, 1)

                def square_attention(half):
                    act.wait_ge(att_copied, two + half + 1)
                    act.activation(mix[:, :, half * 4 * AD:(half + 1) * 4 * AD],
                                   araw[:, :, 4 * half:4 * half + 4, :].rearrange("p t h d -> p t (h d)"),
                                   ACT.Square).then_inc(squares, 1)

                def square_mlstm(c):
                    act.activation(mix[:, c, AW:D].rearrange("p (h v) -> p h v", h=MH), tot[:, c, :, 0:MV],
                                   ACT.Square).then_inc(squares, 1)

                for s in range(8):
                    if s == 4:
                        pe_done(R, 23)
                        act.wait_ge(dve_init, 1)
                        for t in range(NT):
                            act.activation(mv[:, t, :, 0:MV], B[t][:, :].rearrange("p (h v) -> p h v", h=MH),
                                           ACT.Copy).then_inc(mv_copied, 1)
                    if s >= 1:
                        probs_transposed(s - 1)
                    if s == 5:
                        copy_attention(0)
                    probs(s)
                    round_piece(R, 24 + s, FULL)
                    if s == 3:
                        act.wait_ge(m_step, l * 6 + 6)
                        act.activation(eout[:, :, :], ein[:, :, :], ACT.Exp).then_inc(exp_small, 1)
                    if s == 4:
                        state_weights(0)
                    if s == 5:
                        state_weights(1)
                    if s == 6:
                        square_attention(0)
                    if s == 7:
                        act.wait_ge(c_psum, one + 1)
                        act.activation(csb[:, :, 0:MV + 1],
                                       B[5][:, 0:2 * (MV + 2)].rearrange("p (j v) -> p j v", j=2)[:, :, 0:MV + 1],
                                       ACT.Copy).then_inc(c_copied, 1)
                probs_transposed(7)
                act.wait_ge(num_copied, two + 1)
                square_mlstm(0)
                pe_done(R, 27)
                for t in range(NT):
                    act.activation(mo[:, t, :], B[t][:, :], ACT.Sigmoid).then_inc(mo_sig, 1)
                copy_attention(1)
                square_attention(1)
                act.wait_ge(tot_done, one + 1)
                square_mlstm(1)
                act.activation(early[:, :], eps[:, 1:2], ACT.Sqrt)
                act.wait_ge(mean_sq, one + 1)
                act.activation(norms[:, 3, :], norms[:, 2, :], ACT.Sqrt, bias=eps[:, 1:2]).then_inc(std_done, 1)
                round_piece(R, 32, FULL)
                round_piece(R, 33, FULL)
                xt0 = act.snap(l * 12)
                for t in range(NT):
                    transposed_high(xt0 + 4, t)
                for g in range(34, 36 + PIECES):
                    round_piece(R, g, FULL)
                layer_norm_act(act.snap(l * 4))
                for t in range(NT):
                    transposed_high(xt0 + 8, t)
                with act.If(l < 1):
                    ffn_act(MIX_ROUNDS, DENSE_FULL, True, NT, (2, 3), 3, PIECES)
                    for g in range(PIECES):
                        round_piece(Rounds(act, LAYER_ROUNDS), g, mixer_piece(g))
                    layer_norm_act(2)
                    for t in range(NT):
                        transposed_high(12, t)

            act.wait_ge(ln_out, 3 * NT)
            for t in range(NT):
                act.activation(xb[:, 0, t, :], xs[:, t, :], ACT.Copy).then_inc(x_high, 1)
            for t in range(NT):
                act.wait_ge(x_rest, t + 1)
                act.activation(xb[:, 1, t, :], xrem[:, t, :], ACT.Copy).then_inc(x_mid, 1)
            act.wait_ge(logits_t_psum, 1)
            act.activation(lgt[:, :], B[0][0:E, 0:SEQ], ACT.Copy).then_inc(logits_t, 1)
            act.wait_ge(top_gap, 1)
            act.activation(topv[:, 3, :], topv[:, 2, :], ACT.Exp).then_inc(exp_f, 1)

            def gathered_high(p):
                act.wait_ge(gathered, p + 1)
                for b in range(2):
                    act.activation(xth[:, 4 * b:4 * b + 4, 0:P], B[b][:, :].rearrange("p (k n) -> p k n", k=4),
                                   ACT.Copy).then_inc(gath_high, 1)

            gathered_high(0)
            act.wait_ge(table_ready, 1)
            passes = act.value_load(tabi[0:1, MAX_PASSES:MAX_PASSES + 1], min_val=1, max_val=MAX_PASSES)
            with act.Fori(0, passes) as p:
                after = act.snap(p + 1)

                def copy_pick():
                    act.wait_ge(pick_psum, p + 1)
                    act.wait_ge(scattered, p * NT + 1)
                    act.activation(pickt[:, :], B[6][:, 0:SEQ], ACT.Copy).then_inc(pick_copied, 1)

                def next_pass():
                    with act.If(after < passes):
                        gathered_high(after)
                        R = Rounds(act, p * MOE_CHUNKS + (MOE_BASE + MOE_CHUNKS))
                        for g in range(PIECES):
                            round_piece(R, g, 2 * WIDE)

                ffn_act(act.snap(p * MOE_CHUNKS + MOE_BASE), MOE_CHUNKS, False, 1, (7,),
                        MOE_BASE - DENSE_FULL - 1, PIECES, copy_pick, next_pass)
                pe_done(Rounds(act, p * MOE_CHUNKS + (MOE_BASE + MOE_CHUNKS)), -1)
                for n in range(2):
                    act.activation(yh[:, n * WIDE:(n + 1) * WIDE], B[4 + n][:, :], ACT.Copy).then_inc(y_high, 1)
            layer_norm_act(3 * NT)

        @block.vector
        def _(dve):
            dve.sem_inc(split, ROUND)

            def low_piece(R, g, n):
                dve.wait_ge(rounded, R.pieces + g + 1)
                src = raw[:, unit_of(g) % RAW_UNITS, (g % PIECES) * n:(g % PIECES + 1) * n]
                dve.tensor_tensor(wl[:, piece_slot(g), 0:n], src, wh[:, piece_slot(g), 0:n].bitcast(F32),
                                  ALU.subtract).then_inc(split, 1)

            def pe_done(R, g):
                dve.wait_ge(piece_used, R.pieces + SPLIT_SLOTS + g + 1)

            def transposed_low(base, t):
                for b in range(2):
                    dve.wait_ge(xt_high, base + 2 * t + b + 1)
                    dve.tensor_tensor(xtl[:, 4 * b:4 * b + 4, t * P:(t + 1) * P],
                                      B[2 * t + b][:, :].rearrange("p (k n) -> p k n", k=4),
                                      xth[:, 4 * b:4 * b + 4, t * P:(t + 1) * P].bitcast(F32), ALU.subtract)\
                        .then_inc(xt_low, 1)

            def add_residual(t, n):
                cols = xs[:, t, n * WIDE:(n + 1) * WIDE]
                dve.scalar_tensor_tensor(out=cols, in0=cols, scalar=ALPHA, in1=B[4 + 2 * t + n][:, :],
                                         op0=ALU.mult, op1=ALU.add).then_inc(residual, 1)

            def statistics(t, n):
                return dve.bn_stats(stats[:, t, n, :], xs[:, t, n * WIDE:(n + 1) * WIDE])

            def layer_norm_tile(t, base, params, steps):
                dve.wait_ge(ln_step, steps + 3 * t + 1)
                dve.memset(lnc[:, t, 0:1], 1.0)
                dve.bn_aggr(moments[:, t, :], stats[:, t, :, :]).then_inc(ln_var, 1)
                if t == 0:
                    dve.wait_ge(ln_loaded, params)
                dve.wait_ge(ln_var, base + t + 1)
                dve.scalar_tensor_tensor(out=xs[:, t, :], in0=xs[:, t, :], scalar=moments[:, t, 0:1], in1=lng[:, :],
                                         op0=ALU.subtract, op1=ALU.mult).then_inc(ln_step, 1)
                dve.wait_ge(ln_std, base + t + 1)
                dve.reciprocal(lnc[:, t, 1:2], lnc[:, t, 0:1]).then_inc(ln_step, 1)
                dve.wait_ge(ln_step, steps + 3 * t + 3)
                dve.scalar_tensor_tensor(out=xs[:, t, :], in0=xs[:, t, :], scalar=lnc[:, t, 1:2], in1=lnb[:, :],
                                         op0=ALU.mult, op1=ALU.add).then_inc(ln_out, 1)

            def ffn_dve(r0, chunks, half, tiles, tbank, chunk_off, ahead=0, before_up=None, after_hidden=None,
                        during_down=None):
                def ht_low_parts(R, k, w):
                    dve.wait_ge(ht_high, k)
                    for t in range(tiles):
                        last = dve.tensor_tensor(htl[:, 0:w // P, t * P:(t + 1) * P],
                                                 B[tbank[t]][:, 0:w].rearrange("p (f n) -> p f n", n=P),
                                                 hth[:, 0:w // P, t * P:(t + 1) * P].bitcast(F32), ALU.subtract)
                    last.then_inc(ht_low, 1)

                def hidden(R, g, k, w):
                    dve.wait_ge(silu_done, k)
                    pe_done(R, g)
                    for t in range(tiles):
                        last = dve.tensor_tensor(hbuf[:, t, 0:w], hbuf[:, t, 0:w], B[2 + t][:, 0:w], ALU.mult)
                    last.then_inc(h_done, 1)

                def first(R):
                    for g in range(ahead, 8):
                        low_piece(R, g, 2 * WIDE)
                        if g == 5 and before_up:
                            before_up()
                    hidden(R, 7, R.r - chunk_off + 1, WIDE)
                    if after_hidden:
                        after_hidden()

                def chunk(R, w, wprev):
                    for g in range(8, 20):
                        low_piece(R, g, (2 * w if g < 16 else 2 * WIDE))
                        if g == 11:
                            ht_low_parts(R, R.r - chunk_off + 1, wprev)
                    hidden(R, 15, R.r - chunk_off + 2, w)

                def tail(R, w):
                    for g in range(8, 12):
                        low_piece(R, g, 2 * w)
                        if g == (11 if half else 9):
                            ht_low_parts(R, R.r - chunk_off + 1, w)
                    if during_down:
                        during_down()

                ffn_stretch(dve, first, chunk, tail, r0, chunks, half)

            dve.memset(mpre[:, :, 0:3], 0.0)
            dve.memset(mv[:, :, :, :], 1.0)
            dve.memset(smax[:, :, :], 0.0).then_inc(dve_init, 1)
            for j in range(HALF_ROPE):
                last = dve.memset(invf[:, j:j + 1], float(ROPE_THETA ** (-j / HALF_ROPE)))
            last.then_inc(rope_step, 1)
            dve.wait_ge(rope_in, 16)
            dve.tensor_copy(posf[:, :], posi[:, :]).then_inc(rope_step, 1)
            dve.wait_ge(rope_step, 2)
            for t in range(NT):
                last = dve.tensor_scalar(ang[:, 0, t, :], invf[:, :], posf[:, t:t + 1], None, ALU.mult)
            last.then_inc(rope_step, 1)
            dve.wait_ge(rope_step, 3)
            dve.tensor_scalar(turn[:, 0], ang[:, 0], 1.0 / TWO_PI, None, ALU.mult)
            dve.tensor_scalar(turn[:, 1], ang[:, 0], 1.0 / TWO_PI, 0.25, ALU.mult, ALU.add).then_inc(rope_step, 1)
            dve.tensor_copy(ang[:, 1], ang[:, 0])
            dve.wait_ge(rope_step, 4)
            dve.tensor_copy(turni[:, :, :, :], turn[:, :, :, :]).then_inc(rope_step, 1)
            dve.wait_ge(rope_step, 5)
            dve.tensor_copy(turn[:, :, :, :], turni[:, :, :, :]).then_inc(rope_step, 1)
            for i, part in enumerate((6.28125, 0.0019350051879882812, TWO_PI - 6.28125 - 0.0019350051879882812)):
                dve.wait_ge(rope_step, 6 + i)
                dve.scalar_tensor_tensor(out=ang[:, :, :, :], in0=turn[:, :, :, :], scalar=-part,
                                         in1=ang[:, :, :, :], op0=ALU.mult, op1=ALU.add).then_inc(rope_step, 1)
            dve.wait_ge(rope_step, 9)
            dve.tensor_scalar(ang[:, 1], ang[:, 1], TWO_PI / 4, None, ALU.add).then_inc(rope_step, 1)
            dve.wait_ge(rope_step, 10)
            dve.tensor_scalar(ang[:, :, :, :], ang[:, :, :, :], PI_SAFE, -PI_SAFE, ALU.min, ALU.max).then_inc(sin_in, 1)
            dve.wait_ge(sin_done, 1)
            for i in range(2):
                last = dve.tensor_copy(sincos[:, i],
                                       sc8[:, i].unsqueeze(2).broadcast_to((P, NT, 2 * AH, HALF_ROPE)))
            last.then_inc(rope_table, 1)
            dve.sem_inc(dve_init, 1)
            for t in range(NT):
                transposed_low(0, t)
            for g in range(PIECES):
                low_piece(Rounds(dve, 0), g, mixer_piece(g))
            dve.wait_ge(rw_high, 1)
            dve.tensor_tensor(rwl[:, :, :], rw[:, :, :], rwh[:, :, :].bitcast(F32), ALU.subtract).then_inc(rw_low, 1)

            with dve.Fori(0, DEPTH) as l:
                R = Rounds(dve, l * LAYER_ROUNDS)
                one, two, three, four, eight = (dve.snap(l * k) for k in (1, 2, 3, 4, 8))
                FULL = 2 * WIDE
                for g in range(PIECES, 8):
                    low_piece(R, g, mixer_piece(g))
                for g in range(8, 10):
                    low_piece(R, g, FULL)
                pe_done(R, 7)
                dve.tensor_copy(gatest, B[4][0:2 * MH, 0:SEQ]).then_inc(gates_t, 1)
                for g in range(10, 14):
                    low_piece(R, g, FULL)
                dve.wait_ge(mixp_loaded, l * 128 + 128)
                dve.wait_ge(gates_psum, one + 1)
                for t in range(NT):
                    last = dve.tensor_tensor(gates[:, t, :], B[5][:, t * 2 * MH:(t + 1) * 2 * MH], gbias[:, :], ALU.add)
                last.then_inc(gates_in, 1)
                dve.wait_ge(gates_in, one + 1)
                dve.scalar_tensor_tensor(out=gtmp[:, 0], in0=gates[:, :, MH:2 * MH], scalar=-1.0,
                                         in1=gates[:, :, MH:2 * MH], op0=ALU.mult, op1=ALU.min).then_inc(absf, 1)
                low_piece(R, 14, FULL)
                low_piece(R, 15, FULL)
                dve.wait_ge(ln_f, one + 1)
                dve.scalar_tensor_tensor(out=gtmp[:, 3], in0=gates[:, :, MH:2 * MH], scalar=0.0, in1=gtmp[:, 2],
                                         op0=ALU.min, op1=ALU.subtract).then_inc(logf_done, 1)
                heads = qk[:, :, :].rearrange("p t (h d) -> p t h d", d=AD)
                x1, x2 = heads[:, :, :, 0:HALF_ROPE], heads[:, :, :, HALF_ROPE:2 * HALF_ROPE]
                sin, cos = sincos[:, 0], sincos[:, 1]
                dve.wait_ge(q_copied, two + 2)
                dve.wait_ge(k_copied, two + 2)
                dve.wait_ge(rope_table, 1)
                dve.tensor_tensor(rt[:, 0], x1, cos, ALU.mult)
                dve.tensor_tensor(rt[:, 1], x2, sin, ALU.mult)
                dve.tensor_tensor(rt[:, 2], x2, cos, ALU.mult)
                dve.tensor_tensor(rt[:, 3], x1, sin, ALU.mult).then_inc(rot_step, 1)
                dve.wait_ge(rot_step, one + 1)
                dve.tensor_tensor(x1, rt[:, 0], rt[:, 1], ALU.subtract)
                dve.tensor_tensor(x2, rt[:, 2], rt[:, 3], ALU.add).then_inc(roped, 1)
                for g in range(16, 20):
                    low_piece(R, g, FULL)
                dve.wait_ge(cum_psum, one + 1)
                dve.tensor_copy(bl[:, :, :], B[0][:, 0:4 * MH].rearrange("p (c n) -> p c n", c=NT)).then_inc(cum_copied, 1)
                dve.wait_ge(cum_copied, one + 1)
                dve.tensor_tensor(aa[:, :, :], gates[:, :, 0:MH], bl[:, :, 0:MH], ALU.subtract).then_inc(a_done, 1)

                def scores(h):
                    dve.wait_ge(score_psum, eight + h + 1)
                    if h >= 2:
                        dve.wait_ge(probs_done, eight + h - 1)
                    dve.tensor_tensor(sm[:, h % 2, :], B[4][:, 0:3 * P], mask3[:, :], ALU.add).then_inc(masked, 1)
                    dve.wait_ge(masked, eight + h + 1)
                    dve.reduce_max(smax[:, h, 0:1], sm[:, h % 2, 0:P], AX_X)
                    dve.reduce_max(smax[:, h, 1:2], sm[:, h % 2, P:3 * P], AX_X).then_inc(row_max, 1)
                    dve.wait_ge(row_max, eight + h + 1)
                    dve.tensor_scalar(snb[:, h, :], smax[:, h, :], -(AD ** -0.5), None, ALU.mult)\
                        .then_inc(score_ready, 1)

                dve.wait_ge(mqk_copied, four + 4)
                for ct in range(4):
                    last = dve.tensor_scalar(cacc[:, ct, :], mpre[:, ct, 0:SEQ], cw[:, ct, 0:1], cb[:, ct:ct + 1],
                                             ALU.mult, ALU.add)
                last.then_inc(conv_step, 1)
                for j in range(1, 4):
                    dve.wait_ge(conv_step, l * 3 + j)
                    for ct in range(4):
                        last = dve.scalar_tensor_tensor(out=cacc[:, ct, :], in0=mpre[:, ct, j:j + SEQ],
                                                        scalar=cw[:, ct, j:j + 1], in1=cacc[:, ct, :],
                                                        op0=ALU.mult, op1=ALU.add)
                    last.then_inc(conv_step if j < 3 else conv_done, 1)
                for g in range(20, 24):
                    low_piece(R, g, FULL)
                dve.wait_ge(qkt_psum, one + 1)
                for b in range(2):
                    dve.tensor_copy(qkt[:, 4 + 2 * b:6 + 2 * b, :], B[6 + b][:, :].rearrange("p (j n) -> p j n", j=2))\
                        .then_inc(kt_copied, 1)
                six = dve.snap(l * 6)

                def row_maxima(c):
                    causal = mask3[:, 0:P].unsqueeze(1).broadcast_to((P, MH, P))
                    dve.wait_ge(arow_psum, two + c + 1)
                    dve.tensor_tensor(wtmp[:, c], B[2 + c][:, :].rearrange("p (h n) -> p h n", h=MH), causal,
                                      ALU.add).then_inc(amask_step, 1)
                    if c == 0:
                        dve.reduce_max(mxs[:, 2, :], B[2][:, :].rearrange("p (h n) -> p h n", h=MH), AX_X)
                    dve.wait_ge(amask_step, two + c + 1)
                    dve.reduce_max(mxs[:, c, :], wtmp[:, c], AX_X).then_inc(m_step, 1)

                def stabilisers():
                    dve.wait_ge(m_step, six + 2)
                    dve.tensor_scalar(mxs[:, 2, :], mxs[:, 2, :], 0.0, None, ALU.max)
                    dve.tensor_scalar(mxs[:, 4, :], mxs[:, 0, :], 0.0, None, ALU.max).then_inc(m_step, 1)
                    dve.wait_ge(m_step, six + 3)
                    dve.tensor_tensor(mxs[:, 3, :], bl[:, 0, MH:2 * MH], mxs[:, 2, :], ALU.add).then_inc(m_step, 1)
                    dve.tensor_tensor(ein[:, 0, :], aa[:, 0, :], mxs[:, 2, :], ALU.subtract)
                    dve.wait_ge(m_step, six + 4)
                    dve.tensor_tensor(mxs[:, 5, :], mxs[:, 1, :], mxs[:, 3, :], ALU.max).then_inc(m_step, 1)
                    dve.wait_ge(m_step, six + 5)
                    dve.tensor_tensor(ein[:, 1, :], mxs[:, 3, :], mxs[:, 5, :], ALU.subtract)
                    dve.scalar_tensor_tensor(out=ein[:, 2:4, :], in0=bl[:, :, 0:MH], scalar=-1.0, in1=mxs[:, 4:6, :],
                                             op0=ALU.mult, op1=ALU.subtract).then_inc(m_step, 1)

                def weight_logs():
                    for c in range(NT):
                        dve.wait_ge(mrow_psum, two + c + 1)
                        dve.tensor_tensor(wtmp[:, c], maskt[:, :].unsqueeze(1).broadcast_to((P, MH, P)),
                                          B[2 + c][:, :].rearrange("p (h n) -> p h n", h=MH), ALU.subtract)\
                            .then_inc(wlog, 1)

                def weighted_scores(c):
                    dve.wait_ge(wexp, two + c + 1)
                    dve.wait_ge(kq_psum, one + 1)
                    for j in range(2):
                        last = dve.scalar_tensor_tensor(
                            out=st[:, c].rearrange("p (i j) n -> p i j n", j=2)[:, :, j, :],
                            in0=B[2 + j][:, 2 * c * P:(2 * c + 2) * P].rearrange("p (i n) -> p i n", i=2),
                            scalar=MK ** -0.5, in1=wtmp[:, c].rearrange("p (i j) n -> p i j n", j=2)[:, :, j, :],
                            op0=ALU.mult, op1=ALU.mult)
                    last.then_inc(st_done, 1)

                for s in range(8):
                    scores(s)
                    if s == 1:
                        row_maxima(0)
                    if s == 2:
                        row_maxima(1)
                        stabilisers()
                    if s == 4:
                        weight_logs()
                    if s == 5:
                        weighted_scores(0)
                        dve.wait_ge(exp_small, one + 1)
                        dve.tensor_scalar(ein[:, 1, :], eout[:, 1, :], MK ** -0.5, None, ALU.mult).then_inc(inter_w, 1)
                    if s == 6:
                        weighted_scores(1)
                    low_piece(R, 24 + s, FULL)
                nine = dve.snap(l * 9)

                def sum_attention(half):
                    dve.wait_ge(squares, four + 1 + 2 * half)
                    for t in range(NT):
                        last = dve.reduce_sum(norms[:, 1, 8 * t + 4 * half:8 * t + 4 * half + 4],
                                              mix[:, t, 4 * AD * half:4 * AD * (half + 1)]
                                              .rearrange("p (h d) -> p h d", h=4), AX_X)
                    return last

                def sum_mlstm(c):
                    dve.wait_ge(squares, four + 2 + 2 * c)
                    return dve.reduce_sum(norms[:, 1, 16 + 4 * c:20 + 4 * c],
                                          mix[:, c, AW:D].rearrange("p (h v) -> p h v", h=MH), AX_X)

                dve.wait_ge(probs_done, eight + 8)
                dve.reciprocal(norms[:, 0, 0:16], rsum[:, :, :].rearrange("p t h -> p (t h)"))

                def copy_numerators(c):
                    dve.wait_ge(num_psum, two + c + 1)
                    for b in range(2):
                        last = dve.tensor_copy(tot[:, c, 2 * b:2 * b + 2, 0:MV + 1],
                                               B[2 + b][:, 0:2 * (MV + 2)].rearrange("p (j v) -> p j v", j=2)
                                               [:, :, 0:MV + 1])
                    last.then_inc(num_copied, 1)

                copy_numerators(0)
                sum_attention(0)
                sum_mlstm(0)
                copy_numerators(1)
                dve.wait_ge(inter_psum, one + 1)
                dve.wait_ge(num_copied, two + 2)
                dve.wait_ge(inter_w, one + 1)
                for h in range(MH):
                    io = (h // 2) * (MV + 2)
                    last = dve.scalar_tensor_tensor(out=tot[:, 1, h, 0:MV + 1], in0=B[4 + h % 2][:, io:io + MV + 1],
                                                    scalar=ein[:, 1, h:h + 1], in1=tot[:, 1, h, 0:MV + 1],
                                                    op0=ALU.mult, op1=ALU.add)
                last.then_inc(tot_done, 1)
                dve.wait_ge(num_copied, two + 1)
                dve.wait_ge(tot_done, one + 1)
                dve.scalar_tensor_tensor(out=norms[:, 3, 16:24].rearrange("p (c h) -> p c h", c=NT),
                                         in0=tot[:, :, :, MV], scalar=-1.0, in1=tot[:, :, :, MV],
                                         op0=ALU.mult, op1=ALU.max).then_inc(norm_step, 1)
                sum_attention(1)
                dve.wait_ge(norm_step, nine + 1)
                dve.tensor_tensor(norms[:, 3, 16:24], norms[:, 3, 16:24],
                                  eout[:, 2:4, :].rearrange("p c h -> p (c h)"), ALU.max).then_inc(norm_step, 1)
                dve.wait_ge(norm_step, nine + 2)
                dve.reciprocal(norms[:, 0, 16:24], norms[:, 3, 16:24]).then_inc(norm_step, 1)
                sum_mlstm(1).then_inc(norm_step, 1)
                dve.wait_ge(norm_step, nine + 4)
                dve.scalar_tensor_tensor(out=norms[:, 2, 0:16], in0=norms[:, 1, 0:16], scalar=1.0 / AD,
                                         in1=norms[:, 0, 0:16], op0=ALU.mult, op1=ALU.mult)
                dve.scalar_tensor_tensor(out=norms[:, 2, 16:24], in0=norms[:, 1, 16:24], scalar=1.0 / MV,
                                         in1=norms[:, 0, 16:24], op0=ALU.mult, op1=ALU.mult).then_inc(norm_step, 1)
                dve.wait_ge(norm_step, nine + 5)
                dve.tensor_tensor(norms[:, 2, :], norms[:, 2, :], norms[:, 0, :], ALU.mult).then_inc(mean_sq, 1)
                dve.wait_ge(std_done, one + 1)
                dve.reciprocal(norms[:, 4, :], norms[:, 3, :]).then_inc(norm_step, 1)
                dve.wait_ge(norm_step, nine + 6)
                dve.tensor_tensor(norms[:, 4, :], norms[:, 4, :], norms[:, 0, :], ALU.mult).then_inc(norm_step, 1)
                dve.wait_ge(norm_step, nine + 7)
                for t in range(NT):
                    dve.tensor_tensor(mix[:, t, 0:AW].rearrange("p (h d) -> p h d", h=AH), araw[:, t],
                                      norms[:, 4, 8 * t:8 * t + 8].unsqueeze(2).broadcast_to((P, AH, AD)),
                                      ALU.mult).then_inc(norm_step, 1)
                    dve.wait_ge(mo_gate, three + t + 2)
                    dve.tensor_tensor(mix[:, t, AW:D].rearrange("p (h v) -> p h v", h=MH), tot[:, t, :, 0:MV],
                                      norms[:, 4, 16 + 4 * t:20 + 4 * t].unsqueeze(2).broadcast_to((P, MH, MV)),
                                      ALU.mult)
                    dve.wait_ge(norm_step, nine + 8 + t)
                    dve.tensor_tensor(mix[:, t, 0:AW], mix[:, t, 0:AW], gna[:, :], ALU.mult).then_inc(mix_done, 1)
                low_piece(R, 32, FULL)
                xt0 = dve.snap(l * 12)
                for t in range(NT):
                    transposed_low(xt0 + 4, t)
                for g in range(33, 38):
                    low_piece(R, g, FULL)
                pe_done(R, 31)
                for t in range(NT):
                    add_residual(t, 0)
                for t in range(NT):
                    dve.wait_ge(residual, eight + t + 1)
                    statistics(t, 0)
                low_piece(R, 38, FULL)
                low_piece(R, 39, FULL)
                pe_done(R, 35)
                for t in range(NT):
                    add_residual(t, 1)
                    dve.wait_ge(residual, eight + t + 3)
                    statistics(t, 1).then_inc(ln_step, 1)
                    layer_norm_tile(t, four, l * 64 + 32, xt0)
                dve.wait_ge(ln_out, four + 2)
                dve.sem_inc(dve_init, 1)
                for t in range(NT):
                    transposed_low(xt0 + 8, t)
                with dve.If(l < 1):
                    ffn_dve(MIX_ROUNDS, DENSE_FULL, True, NT, (2, 3), 3, PIECES)
                    for g in range(PIECES):
                        low_piece(Rounds(dve, LAYER_ROUNDS), g, mixer_piece(g))
                    pe_done(Rounds(dve, LAYER_ROUNDS), -1)
                    for t in range(NT):
                        add_residual(t, 0)
                        add_residual(t, 1)
                        dve.wait_ge(residual, 4 + 2 * t + 1)
                        statistics(t, 0)
                        dve.wait_ge(residual, 4 + 2 * t + 2)
                        statistics(t, 1).then_inc(ln_step, 1)
                        layer_norm_tile(t, 2, 64, 6)
                    for t in range(NT):
                        transposed_low(12, t)

            for t in range(NT):
                dve.wait_ge(x_high, t + 1)
                dve.tensor_tensor(xrem[:, t, :], xs[:, t, :], xb[:, 0, t, :], ALU.subtract).then_inc(x_rest, 1)
            for t in range(NT):
                dve.wait_ge(x_mid, t + 1)
                dve.tensor_tensor(xb[:, 2, t, :], xrem[:, t, :], xb[:, 1, t, :], ALU.subtract).then_inc(x_low, 1)
            steps = [0]

            def then(ins):
                steps[0] += 1
                ins.then_inc(route_step, 1)
                dve.wait_ge(route_step, steps[0])

            dve.wait_ge(logits_psum, 1)
            dve.wait_ge(const_ready, 2)
            for t in range(NT):
                last = dve.tensor_tensor(lg[:, t, :], B[1][:, t * E:(t + 1) * E], rb[:, :], ALU.add)
            then(last)
            for t in range(NT):
                other = lg[:, t, :].unsqueeze(1).broadcast_to((P, E, E))
                own = lg[:, t, :].unsqueeze(2).broadcast_to((P, E, E))
                dve.tensor_tensor(cmp4[:, 0, t], other, own, ALU.is_gt)
                last = dve.tensor_tensor(cmp4[:, 1, t], other, own, ALU.is_equal)
            then(last)
            for t in range(NT):
                last = dve.tensor_tensor(cmp4[:, 1, t], cmp4[:, 1, t], low8[:, :, :], ALU.mult)
            then(last)
            for t in range(NT):
                last = dve.tensor_tensor(cmp4[:, 2, t], cmp4[:, 0, t], cmp4[:, 1, t], ALU.add)
            then(last)
            for t in range(NT):
                last = dve.reduce_sum(rank[:, t, :], cmp4[:, 2, t], AX_X)
            then(last)
            dve.tensor_scalar(isel[:, 0], rank[:, :, :], 0.0, None, ALU.is_equal)
            dve.tensor_scalar(isel[:, 1], rank[:, :, :], 1.0, None, ALU.is_equal)
            dve.tensor_scalar(isel[:, 2], rank[:, :, :], 1.0, None, ALU.is_le).then_inc(picks_ready, 1)
            dve.wait_ge(picks_ready, 1)
            dve.wait_ge(pos_psum, 1)
            then(dve.tensor_copy(posc[:, :, :], B[2][:, 0:3 * E].rearrange("p (a e) -> p a e", a=3)))
            then(dve.scalar_tensor_tensor(out=posc[:, 0:NT, :], in0=posc[:, 0:NT, :], scalar=4096.0, in1=isel[:, 2],
                                          op0=ALU.add, op1=ALU.mult))
            then(dve.tensor_scalar(posc[:, 0:NT, :], posc[:, 0:NT, :], -4096.0, None, ALU.add))
            for t in range(NT):
                last = dve.tensor_scalar(pick[:, t, :], slot_no[:, :], posc[:, t, 0:1], None, ALU.is_equal)
            last.then_inc(pick_done, 1)
            for i in range(2):
                last = dve.tensor_tensor(cmp4[:, 0, :, i, :], isel[:, i], lg[:, :, :], ALU.mult)
            then(last)
            for i in range(2):
                last = dve.reduce_sum(topv[:, i, :], cmp4[:, 0, :, i, :], AX_X)
            then(last)
            dve.tensor_tensor(topv[:, 2, :], topv[:, 1, :], topv[:, 0, :], ALU.subtract).then_inc(top_gap, 1)
            dve.tensor_scalar(blk[:, 0, 1:E], posc[:, 2, 1:E], 0.0, None, ALU.is_gt)
            dve.memset(blk[:, 0, 0:1], 1.0)
            then(dve.tensor_scalar(blk[:, 1, :], posc[:, 2, :], float(P), None, ALU.is_gt))
            then(dve.tensor_tensor(blk[:, 2, :], blk[:, 0, :], blk[:, 1, :], ALU.add))
            dve.tensor_copy(blk[:, 3, 0:1], blk[:, 2, 0:1])
            then(dve.memset(blk[:, 4, 0:1], 0.0))
            for i in range(1, E):
                then(dve.tensor_tensor(blk[:, 3, i:i + 1], blk[:, 3, i - 1:i], blk[:, 2, i:i + 1], ALU.add))
            then(dve.tensor_copy(blk[:, 4, 1:E], blk[:, 3, 0:E - 1]))
            shape = (P, MAX_PASSES, E)
            passn = pass_no[:, :].unsqueeze(2).broadcast_to(shape)
            dve.tensor_tensor(pt11[:, 0], passn, blk[:, 4, :].unsqueeze(1).broadcast_to(shape), ALU.is_ge)
            dve.tensor_tensor(pt11[:, 1], passn, blk[:, 3, :].unsqueeze(1).broadcast_to(shape), ALU.is_lt)
            then(dve.tensor_tensor(pt11[:, 2], passn, blk[:, 4, :].unsqueeze(1).broadcast_to(shape), ALU.subtract))
            then(dve.tensor_tensor(pt11[:, 0], pt11[:, 0], pt11[:, 1], ALU.mult))
            then(dve.scalar_tensor_tensor(out=pt11[:, 2], in0=pt11[:, 2], scalar=float(P), in1=pt11[:, 0],
                                          op0=ALU.mult, op1=ALU.mult))
            then(dve.tensor_tensor(pt11[:, 3], pt11[:, 0], expert_no[:, :].unsqueeze(1).broadcast_to(shape), ALU.mult))
            dve.reduce_sum(tabf[:, 0:MAX_PASSES], pt11[:, 3], AX_X)
            then(dve.tensor_copy(tabf[:, MAX_PASSES:MAX_PASSES + 1], blk[:, 3, E - 1:E]))
            dve.tensor_copy(tabi[:, :], tabf[:, :]).then_inc(table_ready, 1)
            def make_pick(p):
                for t in range(NT):
                    last = dve.tensor_scalar(pick[:, t, :], slot_no[:, :], slotpos[:, t, bass.ds(p, 1)], None,
                                             ALU.is_equal)
                last.then_inc(pick_done, 1)

            def gathered_low(p):
                for b in range(2):
                    dve.wait_ge(gath_high, p * 2 + b + 1)
                    last = dve.tensor_tensor(xtl[:, 4 * b:4 * b + 4, 0:P], B[b][:, :].rearrange("p (k n) -> p k n", k=4),
                                             xth[:, 4 * b:4 * b + 4, 0:P].bitcast(F32), ALU.subtract)
                last.then_inc(gath_low, 1)

            gathered_low(0)
            dve.wait_ge(exp_f, DEPTH + 1)
            then(dve.tensor_scalar(topv[:, 4, :], topv[:, 3, :], 1.0, None, ALU.add))
            then(dve.reciprocal(topv[:, 4, :], topv[:, 4, :]))
            then(dve.tensor_tensor(topv[:, 5, :], topv[:, 4, :], topv[:, 3, :], ALU.mult))
            for t in range(NT):
                last = dve.tensor_scalar(comb[:, t, :], isel[:, 0, t, :], topv[:, 4, t:t + 1], None, ALU.mult)
            then(last)
            for t in range(NT):
                last = dve.scalar_tensor_tensor(out=comb[:, t, :], in0=isel[:, 1, t, :], scalar=topv[:, 5, t:t + 1],
                                                in1=comb[:, t, :], op0=ALU.mult, op1=ALU.add)
            then(last)
            dve.memset(slotpos[:, :, MAX_PASSES:MAX_PASSES + 1], -1.0)
            for t in range(NT):
                then(dve.tensor_tensor(pt11[:, 3], pt11[:, 0], posc[:, t, :].unsqueeze(1).broadcast_to(shape), ALU.mult))
                dve.tensor_tensor(pt11[:, 4], pt11[:, 0], comb[:, t, :].unsqueeze(1).broadcast_to(shape), ALU.mult)
                then(dve.tensor_tensor(pt11[:, 3], pt11[:, 3], pt11[:, 2], ALU.subtract))
                dve.reduce_sum(slotpos[:, t, 0:MAX_PASSES], pt11[:, 3], AX_X)
                then(dve.reduce_sum(cbp[:, t, 1:MAX_PASSES + 1], pt11[:, 4], AX_X))

            dve.wait_ge(table_ready, 1)
            passes = dve.value_load(tabi[0:1, MAX_PASSES:MAX_PASSES + 1], min_val=1, max_val=MAX_PASSES)

            def accumulate(banks, t, column, done):
                dve.wait_ge(scattered, done)
                for n in range(2):
                    cols = xs[:, t, n * WIDE:(n + 1) * WIDE]
                    last = dve.scalar_tensor_tensor(out=cols, in0=B[banks[n]][:, :],
                                                    scalar=cbp[:, t, bass.ds(column, 1)], in1=cols,
                                                    op0=ALU.mult, op1=ALU.add)
                last.then_inc(accumulated, 1)

            with dve.Fori(0, passes) as p:
                after, two = dve.snap(p + 1), dve.snap(p * 2)

                def last_pass_tile0():
                    with dve.If(p > 0):
                        dve.wait_ge(accumulated, two)
                        accumulate((1, 3), 0, p, two)

                def last_pass_tile1():
                    with dve.If(p > 0):
                        accumulate((1, 3), 1, p, two + 1)
                    dve.wait_ge(gathered, p + 1)
                    make_pick(after)

                def next_pass():
                    with dve.If(after < passes):
                        gathered_low(after)
                        R = Rounds(dve, p * MOE_CHUNKS + (MOE_BASE + MOE_CHUNKS))
                        for g in range(PIECES):
                            low_piece(R, g, 2 * WIDE)

                ffn_dve(dve.snap(p * MOE_CHUNKS + MOE_BASE), MOE_CHUNKS, False, 1, (7,), MOE_BASE - DENSE_FULL - 1,
                        PIECES, last_pass_tile0, last_pass_tile1, next_pass)
                for n in range(2):
                    dve.wait_ge(y_high, p * 2 + n + 1)
                    dve.tensor_tensor(yl[:, n * WIDE:(n + 1) * WIDE], B[4 + n][:, :],
                                      yh[:, n * WIDE:(n + 1) * WIDE].bitcast(F32), ALU.subtract).then_inc(y_low, 1)
            final = dve.snap(passes * 2)
            dve.wait_ge(accumulated, final)
            for t in range(NT):
                accumulate((2 * t, 2 * t + 1), t, passes, final + t)
                dve.wait_ge(accumulated, final + t + 1)
                statistics(t, 0)
                statistics(t, 1).then_inc(ln_step, 1)
                layer_norm_tile(t, 3 * NT, 128, 18)

        @block.tensor
        def _(pe):
            pe.sem_inc(piece_used, SPLIT_SLOTS)
            pe.wait_ge(const_ready, 1)

            def mm3(out_ap, high, low, w_high, w_low, start, stop):
                pe.matmul(out_ap, high, w_high, start=start, stop=False, skip_group_check=True)
                pe.matmul(out_ap, high, w_low, start=False, stop=False, skip_group_check=True)
                return pe.matmul(out_ap, low, w_high, start=False, stop=stop, skip_group_check=True)

            def use_piece(R, g, per_piece, width, body):
                pe.wait_ge(split, R.pieces + ROUND + g + 1)
                for i in range(per_piece):
                    s = (g % PIECES) * per_piece + i
                    cols = slice(i * width, (i + 1) * width)
                    last = body(s, wh[:, piece_slot(g), cols], wl[:, piece_slot(g), cols])
                last.then_inc(piece_used, 1)

            def project(banks, width=WIDE, tiles=NT):
                def body(s, w_high, w_low):
                    for t in range(tiles):
                        last = mm3(B[banks[t]][:, 0:width], xth[:, s, t * P:(t + 1) * P], xtl[:, s, t * P:(t + 1) * P],
                                   w_high, w_low, s == 0, s == KD - 1)
                    return last
                return body

            def project_transposed(s, w_high, w_low):
                for ct in range(4):
                    out_ap, cols = B[4 + ct][:, 0:SEQ], slice(ct * P, (ct + 1) * P)
                    pe.matmul(out_ap, w_high[:, cols], xth[:, s, :], start=s == 0, stop=False)
                    pe.matmul(out_ap, w_high[:, cols], xtl[:, s, :], start=False, stop=False)
                    last = pe.matmul(out_ap, w_low[:, cols], xth[:, s, :], start=False, stop=s == KD - 1)
                return last

            def project_gates(s, w_high, w_low):
                out_ap = B[4][0:2 * MH, 0:SEQ]
                pe.matmul(out_ap, w_high, xth[:, s, :], start=s == 0, stop=False)
                pe.matmul(out_ap, w_high, xtl[:, s, :], start=False, stop=False)
                return pe.matmul(out_ap, w_low, xth[:, s, :], start=False, stop=s == KD - 1)

            def transpose_tile(src, t):
                for k in range(KD):
                    last = pe.transpose(B[2 * t + k // 4][:, (k % 4) * P:(k % 4 + 1) * P],
                                        src[:, t, k * P:(k + 1) * P], ident[:, :])
                    if k % 4 == 3:
                        last.then_inc(xt_psum, 1)

            def down_body(tiles, stop_at):
                def body(s, w_high, w_low):
                    f, n = s // 2, s % 2
                    for t in range(tiles):
                        last = mm3(B[4 + 2 * t + n][:, :], hth[:, f, t * P:(t + 1) * P], htl[:, f, t * P:(t + 1) * P],
                                   w_high, w_low, False, f == stop_at)
                    return last
                return body

            def ffn_pe(r0, chunks, half, tiles, tbank, chunk_off, rest_of_input=None, after_gate=None,
                       after_up=None, before_down=None):
                def transpose_h(k, w):
                    pe.wait_ge(h_done, k)
                    for t in range(tiles):
                        for f in range(w // P):
                            last = pe.transpose(B[tbank[t]][:, f * P:(f + 1) * P], hbuf[:, t, f * P:(f + 1) * P],
                                                ident[:, :])
                    last.then_inc(ht_psum, 1)

                def open_down():
                    for i in range(2 * tiles):
                        pe.matmul(B[4 + i][:, :], zrow[:, 0:P], zrow[:, :], start=True, stop=False,
                                  skip_group_check=True)

                def gate_up(R, g0, w, k, after_gate=None):
                    for g in range(g0, g0 + 4):
                        if g == 2 and rest_of_input:
                            pe.wait_ge(xt_low, rest_of_input)
                        use_piece(R, g, 2, w, project((0, 1), w, tiles))
                    if after_gate:
                        after_gate()
                    if k is not None and tiles > 1:
                        pe.wait_ge(ht_low, k)
                    for g in range(g0 + 4, g0 + 8):
                        use_piece(R, g, 2, w, project((2, 3), w, tiles))

                def first(R):
                    gate_up(R, 0, WIDE, None, after_gate)
                    if after_up:
                        after_up()
                    open_down()
                    transpose_h(R.r - chunk_off + 1, WIDE)

                def chunk(R, w, wprev):
                    gate_up(R, 8, w, R.r - chunk_off + 1)
                    pe.wait_ge(ht_low, R.r - chunk_off + 1)
                    for g in range(16, 20):
                        use_piece(R, g, 2, WIDE, down_body(tiles, None))
                    transpose_h(R.r - chunk_off + 2, w)

                def tail(R, w):
                    if before_down:
                        before_down()
                    pe.wait_ge(ht_low, R.r - chunk_off + 1)
                    for g in range(8, 12):
                        use_piece(R, g, w // 256, WIDE, down_body(tiles, w // P - 1))

                ffn_stretch(pe, first, chunk, tail, r0, chunks, half)

            for t in range(NT):
                pe.wait_ge(x_loaded[t], 16)
                transpose_tile(xs, t)

            with pe.Fori(0, DEPTH) as l:
                R = Rounds(pe, l * LAYER_ROUNDS)
                one, two, four, eight = (pe.snap(l * k) for k in (1, 2, 4, 8))
                pe.wait_ge(xt_low, l * 12 + 3)
                for g in range(0, 4):
                    if g == 2:
                        pe.wait_ge(xt_low, l * 12 + 4)
                    use_piece(R, g, 2, WIDE, project((0, 1)))
                for g in range(4, 8):
                    use_piece(R, g, 2, 2 * MH, project_gates)
                for g in range(8, 12):
                    if g == 10:
                        pe.wait_ge(gates_t, one + 1)
                    if g == 11:
                        for t in range(NT):
                            last = pe.transpose(B[5][:, t * 2 * MH:(t + 1) * 2 * MH], gatest[:, t * P:(t + 1) * P],
                                                ident[0:2 * MH, 0:2 * MH])
                        last.then_inc(gates_psum, 1)
                    use_piece(R, g, 2, WIDE, project((2, 3)))
                pe.wait_ge(gates_in, one + 1)
                for g in range(12, 16):
                    use_piece(R, g, 2, WIDE, project_transposed)
                pe.wait_ge(q_copied, two + 2)
                pe.wait_ge(logf_done, one + 1)
                for c in range(NT):
                    pe.matmul(B[0][:, 8 * c:8 * c + MH], tri[:, :], gtmp[:, 3, c, :], start=True, stop=True)
                    last = pe.matmul(B[0][:, 8 * c + MH:8 * c + 2 * MH], ones[:, :], gtmp[:, 3, c, :],
                                     start=True, stop=True)
                last.then_inc(cum_psum, 1)
                pe.wait_ge(k_copied, two + 2)
                for g in range(16, 20):
                    use_piece(R, g, 2, WIDE, project((2, 3)))
                pe.wait_ge(roped, one + 1)
                pe.wait_ge(mqk_copied, four + 4)
                for j in range(8):
                    for t in range(NT):
                        last = pe.transpose(B[4 + j // 2][:, (j % 2) * SEQ + t * P:(j % 2) * SEQ + (t + 1) * P],
                                            qk[:, t, j * P:(j + 1) * P], ident[:, :])
                last.then_inc(qkt_psum, 1)
                pe.wait_ge(conv_silu, one + 1)
                for j in range(2):
                    last = pe.transpose(B[1][:, j * P:(j + 1) * P], mqkt[:, 2 + j, 0:P], ident[:, :])
                last.then_inc(ktok_psum, 1)
                pe.wait_ge(cum_copied, one + 1)
                pe.wait_ge(ktok_copied, one + 1)

                def scores(h):
                    r = slice(AD * (h % 2), AD * (h % 2) + AD)
                    if h == 0:
                        pe.wait_ge(qt_copied, two + 2)
                        pe.wait_ge(kt_copied, two + 2)
                    else:
                        pe.wait_ge(masked, eight + h)
                    q, k = qkt[r, h // 2, :], qkt[r, 4 + h // 2, :]
                    pe.matmul(B[4][:, 0:P], q[:, 0:P], k[:, 0:P], start=True, stop=True)
                    pe.matmul(B[4][:, P:3 * P], q[:, P:2 * P], k, start=True, stop=True).then_inc(score_psum, 1)

                def transpose_probs(h):
                    pe.wait_ge(probs_done, eight + h + 1)
                    if h >= 1:
                        pe.wait_ge(probs_t, eight + h)
                    else:
                        pe.wait_ge(kt_copied, two + 2)
                    for j in range(3):
                        last = pe.transpose(B[6][:, j * P:(j + 1) * P], pm[:, h % 2, j * P:(j + 1) * P], ident[:, :])
                    last.then_inc(probs_t_psum, 1)

                def attend(h):
                    pe.wait_ge(probs_t, eight + h + 1)
                    if h == 0:
                        pe.wait_ge(v_copied, two + 2)
                    if h == 4:
                        pe.wait_ge(att_copied, two + 1)
                    o, cols = (h % 4) * AD, slice(h * AD, (h + 1) * AD)
                    pt = ptm[:, h % 2, :]
                    pe.matmul(B[7][:, o:o + AD], pt[:, 0:P], vv[:, 0, cols], start=True, stop=True)
                    pe.matmul(B[7][:, 4 * AD + o:5 * AD + o], pt[:, P:2 * P], vv[:, 0, cols], start=True, stop=False)
                    pe.matmul(B[7][:, 4 * AD + o:5 * AD + o], pt[:, 2 * P:3 * P], vv[:, 1, cols],
                              start=False, stop=True).then_inc(att_psum, 1)

                def diag_rows(c, ready, done):
                    pe.wait_ge(ready, two + c + 1)
                    pe.matmul(B[2 + c][:, :], ones[:, :], diag[:, c].rearrange("p h n -> p (h n)"),
                              start=True, stop=True).then_inc(done, 1)

                def kq():
                    pe.wait_ge(wlog, two + 2)
                    for c in range(NT):
                        for h in range(MH):
                            r, o = slice(MK * (h % 2), MK * (h % 2) + MK), (2 * c + h // 2) * P
                            last = pe.matmul(B[2 + h % 2][:, o:o + P], mqkt[r, 2 + h // 2, c * P:(c + 1) * P],
                                             mqkt[r, h // 2, c * P:(c + 1) * P], start=True, stop=True)
                    last.then_inc(kq_psum, 1)

                def carried_state():
                    pe.wait_ge(vw_done, one + 1)
                    for h in range(MH):
                        o = (h // 2) * (MV + 2)
                        last = pe.matmul(B[5][MK * (h % 2):MK * (h % 2) + MK, o:o + MV + 1],
                                         ktok[:, h * MK:(h + 1) * MK], vw[:, h, 0:MV + 1], start=True, stop=True)
                    last.then_inc(c_psum, 1)

                def numerators(c, bank):
                    pe.wait_ge(st_done, two + 2)
                    pe.wait_ge(mv_copied, two + 2)
                    for h in range(MH):
                        o = (h % 2) * (MV + 2)
                        last = pe.matmul(B[bank + h // 2][:, o:o + MV + 1], st[:, c, h, :], mv[:, c, h, 0:MV + 1],
                                         start=True, stop=True)
                    last.then_inc(num_psum, 1)

                for s in range(8):
                    scores(s)
                    if s == 1:
                        pe.wait_ge(v_copied, two + 2)
                        diag_rows(0, diag_a, arow_psum)
                        diag_rows(1, diag_a, arow_psum)
                    if s == 5:
                        kq()
                    if s == 4:
                        pe.wait_ge(mv_copied, two + 2)
                    use_piece(R, 20 + s, 2, WIDE, project((0, 1)))
                    transpose_probs(s)
                    if s >= 1:
                        attend(s - 1)
                    if s == 3:
                        pe.wait_ge(m_step, l * 6 + 6)
                        diag_rows(0, diag_m, mrow_psum)
                        diag_rows(1, diag_m, mrow_psum)
                    if s == 6:
                        carried_state()
                    if s == 7:
                        numerators(0, 2)
                attend(7)
                pe.wait_ge(num_copied, two + 1)
                numerators(1, 2)
                pe.wait_ge(c_copied, one + 1)
                pe.wait_ge(masked, eight + 8)
                for h in range(MH):
                    r, o = slice(MK * (h % 2), MK * (h % 2) + MK), (h // 2) * (MV + 2)
                    last = pe.matmul(B[4 + h % 2][:, o:o + MV + 1], mqkt[r, h // 2, P:2 * P], csb[r, h // 2, 0:MV + 1],
                                     start=True, stop=True)
                last.then_inc(inter_psum, 1)
                pe.wait_ge(tot_done, one + 1)
                pe.wait_ge(mo_sig, two + 2)
                for t in range(NT):
                    pe.wait_ge(mix_done, two + t + 1)
                    transpose_tile(mix, t)
                pe.wait_ge(xt_low, l * 12 + 7)
                pe.wait_ge(att_copied, two + 2)
                for g in range(28, 32):
                    if g == 30:
                        pe.wait_ge(xt_low, l * 12 + 8)
                    use_piece(R, g, 2, WIDE, project((4, 6)))
                for g in range(32, 36):
                    use_piece(R, g, 2, WIDE, project((5, 7)))
                for t in range(NT):
                    pe.wait_ge(ln_out, four + t + 1)
                    transpose_tile(xs, t)
                with pe.If(l < 1):
                    pe.wait_ge(xt_low, 11)
                    ffn_pe(MIX_ROUNDS, DENSE_FULL, True, NT, (2, 3), 3, 12)
                    for t in range(NT):
                        pe.wait_ge(ln_out, NT + t + 1)
                        transpose_tile(xs, t)

            pe.wait_ge(xt_low, 23)
            pe.wait_ge(rw_low, 1)
            for k in range(KD):
                if k == KD // 2:
                    pe.wait_ge(xt_low, 24)
                pe.matmul(B[0][0:E, 0:SEQ], rwh[:, k, :], xth[:, k, :], start=k == 0, stop=False)
                pe.matmul(B[0][0:E, 0:SEQ], rwl[:, k, :], xth[:, k, :], start=False, stop=False)
                last = pe.matmul(B[0][0:E, 0:SEQ], rwh[:, k, :], xtl[:, k, :], start=False, stop=k == KD - 1)
            last.then_inc(logits_t_psum, 1)
            pe.wait_ge(logits_t, 1)
            for t in range(NT):
                last = pe.transpose(B[1][:, t * E:(t + 1) * E], lgt[:, t * P:(t + 1) * P], ident[0:E, 0:E])
            last.then_inc(logits_psum, 1)
            pe.wait_ge(picks_ready, 1)
            pe.matmul(B[2][:, 0:E], trs[:, :], isel[:, 2, 0, :], start=True, stop=True)
            pe.matmul(B[2][:, E:2 * E], trs[:, :], isel[:, 2, 1, :], start=True, stop=False)
            pe.matmul(B[2][:, E:2 * E], ones[:, :], isel[:, 2, 0, :], start=False, stop=True)
            pe.matmul(B[2][:, 2 * E:3 * E], ones[:, :], isel[:, 2, 0, :], start=True, stop=False)
            pe.matmul(B[2][:, 2 * E:3 * E], ones[:, :], isel[:, 2, 1, :], start=False, stop=True).then_inc(pos_psum, 1)
            def gather(p):
                pe.wait_ge(pick_done, p + 1)
                for t in range(NT):
                    last = pe.matmul(B[6][:, t * P:(t + 1) * P], pick[:, t, :], identb[:, :], start=True, stop=True)
                last.then_inc(pick_psum, 1)
                for k in range(KD):
                    for t in range(NT):
                        for part in range(3):
                            last = pe.matmul(B[k // 4][:, (k % 4) * P:(k % 4 + 1) * P],
                                             xb[:, part, t, k * P:(k + 1) * P], pick[:, t, :],
                                             start=t + part == 0, stop=t + part == NT + 1)
                last.then_inc(gathered, 1)

            def scatter(banks, t):
                for n in range(2):
                    cols = slice(n * WIDE, (n + 1) * WIDE)
                    pe.matmul(B[banks[n]][:, :], pickt[:, t * P:(t + 1) * P], yh[:, cols], start=True, stop=False)
                    last = pe.matmul(B[banks[n]][:, :], pickt[:, t * P:(t + 1) * P], yl[:, cols],
                                     start=False, stop=True)
                last.then_inc(scattered, 1)

            pe.wait_ge(x_low, NT)
            gather(0)
            pe.sem_inc(scattered, 1)
            pe.wait_ge(table_ready, 1)
            passes = pe.value_load(tabi[0:1, MAX_PASSES:MAX_PASSES + 1], min_val=1, max_val=MAX_PASSES)
            with pe.Fori(0, passes) as p:
                after, two = pe.snap(p + 1), pe.snap(p * 2)

                def last_pass_tile0():
                    with pe.If(p > 0):
                        pe.wait_ge(y_low, two)
                        scatter((1, 3), 0)

                def last_pass_tile1():
                    with pe.If(p > 0):
                        pe.wait_ge(accumulated, two + 1)
                        scatter((1, 3), 1)

                def next_pass():
                    with pe.If(after < passes):
                        pe.wait_ge(accumulated, two + 2)
                        pe.wait_ge(pick_copied, after)
                        gather(after)

                pe.wait_ge(gath_low, after)
                ffn_pe(pe.snap(p * MOE_CHUNKS + MOE_BASE), MOE_CHUNKS, False, 1, (7,), MOE_BASE - DENSE_FULL - 1,
                       None, last_pass_tile0, last_pass_tile1, next_pass)
            final = pe.snap(passes * 2)
            pe.wait_ge(pick_copied, passes)
            pe.wait_ge(y_low, final)
            for t in range(NT):
                scatter((2 * t, 2 * t + 1), t)


_INS = ["x", "positions", "w_in", "gate_bias", "conv_w", "conv_b", "norm_attn", "norm_mlstm", "w_out",
        "ln1_g", "ln1_b", "dense_w_gate", "dense_w_up", "dense_w_down", "router_w", "router_b",
        "moe_w_gate", "moe_w_up", "moe_w_down", "ln2_g", "ln2_b"]


def kernel(**inputs):
    import numpy as _np
    import concourse.bacc as _bacc
    from concourse import mybir as _mybir
    from concourse.bass_utils import run_bass_kernel_spmd as _run

    nc = _bacc.Bacc("TRN2", target_bir_lowering=False, num_devices=1)
    arrays, args = {}, []
    for name in _INS:
        a = _np.ascontiguousarray(inputs[name])
        arrays[f"in_{name}_dram"] = a
        args.append(nc.dram_tensor(f"in_{name}_dram", a.shape, _mybir.dt.from_np(a.dtype), kind="ExternalInput").ap())
    shape = inputs["x"].shape
    args.append(nc.dram_tensor("out_0_dram", shape, _mybir.dt.float32, kind="ExternalOutput").ap())
    hybrid_moe_program(nc, *args)
    r = _run(nc, [arrays], core_ids=[0])
    return r.results[0]["out_0_dram"]
```
